# Optimizing a Trainium2 kernel written in Bass

```python
import math
import jax, jax.numpy as jnp
from jax import lax
import numpy as np

D_MODEL = 1024
BATCH = 1
SEQ = 256
DEPTH = 1

RMS_EPS = 1e-6
NEG_INF = -1e30

POOL_WIDTH = D_MODEL // 2
POOL_WINDOWS = (2, 4, 8, 16)
POOL_GROUPS = len(POOL_WINDOWS)
POOL_GW = POOL_WIDTH // POOL_GROUPS
RWKV_HEAD_DIM = 64
RWKV_WIDTH = D_MODEL // 2
RWKV_HEADS = RWKV_WIDTH // RWKV_HEAD_DIM
DECAY_LORA = 32
AAA_LORA = 32
GATE_LORA = 96
RWKV_GN_EPS = 64e-5
NSA_HEAD_DIM = 64
NSA_WIDTH = D_MODEL
NSA_HEADS = NSA_WIDTH // NSA_HEAD_DIM
NSA_KV_HEADS = 4
NSA_GROUP = NSA_HEADS // NSA_KV_HEADS
NSA_KV_WIDTH = NSA_KV_HEADS * NSA_HEAD_DIM
N_NSA_BRANCHES = 3
CMP_BLOCK = 32
CMP_STRIDE = 16
CMP_HIDDEN = 256
SLC_BLOCK = 64
N_SELECT = 8
WINDOW = 512
NSA_Q_BLOCK = 64
FORCE_BONUS = 1e3
N_BUCKETS = 32
MAX_EXACT = 16
MAX_DISTANCE = 128
N_BRANCHES = 3
POOL_COLS = POOL_WIDTH
RWKV_COLS = 3 * RWKV_WIDTH + DECAY_LORA + AAA_LORA + GATE_LORA
NSA_COLS = NSA_WIDTH + 2 * N_NSA_BRANCHES * NSA_KV_WIDTH + N_NSA_BRANCHES * NSA_HEADS
IN_COLS = POOL_COLS + RWKV_COLS + NSA_COLS
BRANCH_ROWS = POOL_WIDTH + RWKV_WIDTH + NSA_WIDTH
N_GROUPS = 4
EXPERTS_PER_GROUP = 8
N_EXPERTS = N_GROUPS * EXPERTS_PER_GROUP
TOP_K_EXPERTS = 2
D_EXPERT = 256

kernel_name = 'hybrid_pool_rwkv7_nsa_hmoe_block'

def rms_norm(x, g):
    xf = x.astype(jnp.float32)
    y = xf * lax.rsqrt(jnp.mean(xf * xf, axis=-1, keepdims=True) + RMS_EPS)
    return (y * g).astype(x.dtype)

def split_cols(t, sizes):
    return jnp.split(t, [int(o) for o in np.cumsum(sizes)[:-1]], axis=-1)

def masked_softmax(logits, mask):
    lf = jnp.where(mask, logits.astype(jnp.float32), NEG_INF)
    return jax.nn.softmax(lf, axis=-1) * mask

def t5_bucket(dist):
    n = jnp.maximum(dist, 0)
    nf = jnp.maximum(n, 1).astype(jnp.float32)
    large = MAX_EXACT + (jnp.log(nf / MAX_EXACT) / math.log(MAX_DISTANCE / MAX_EXACT)
                         * (N_BUCKETS - MAX_EXACT)).astype(jnp.int32)
    large = jnp.minimum(large, N_BUCKETS - 1)
    return jnp.where(n < MAX_EXACT, n, large)

def pool_mixer(u, w_grp, scale):
    B, S, _ = u.shape
    uf = u.astype(jnp.float32)
    cs = jnp.concatenate([jnp.zeros((B, 1, POOL_WIDTH), jnp.float32), jnp.cumsum(uf, axis=1)], axis=1)
    t = jnp.arange(S)
    means = []
    for gi, win in enumerate(POOL_WINDOWS):
        c = cs[..., gi * POOL_GW:(gi + 1) * POOL_GW]
        lo = jnp.maximum(t + 1 - win, 0)
        cnt = (t + 1 - lo).astype(jnp.float32)
        means.append((c[:, t + 1] - c[:, lo]) / cnt[None, :, None])
    pooled = (jnp.stack(means, axis=2) - uf.reshape(B, S, POOL_GROUPS, POOL_GW)).astype(u.dtype)
    mixed = jnp.einsum('bsgc,gcd->bsgd', pooled, w_grp)
    return mixed.reshape(B, S, POOL_WIDTH) * scale

def rwkv7_mixer(u, mu, w0, w_up, a0, a_up, g_up, k_k, k_a, r_k, gn_w, gn_b):
    B, S, _ = u.shape
    H, N = RWKV_HEADS, RWKV_HEAD_DIM
    u_prev = jnp.pad(u, ((0, 0), (1, 0), (0, 0)))[:, :-1]
    u = u + (u_prev - u) * mu
    r, k, v, wd, ad, gd = split_cols(u, [RWKV_WIDTH] * 3 + [DECAY_LORA, AAA_LORA, GATE_LORA])
    w_log = -jax.nn.softplus(-(w0 + jnp.tanh(wd) @ w_up)) - 0.5
    decay = jnp.exp(-jnp.exp(w_log.astype(jnp.float32)))
    a = jax.nn.sigmoid(a0 + ad @ a_up)
    g = jax.nn.sigmoid(gd) @ g_up
    heads = lambda t: t.reshape(B, S, H, N).astype(jnp.float32)
    kk = heads(k * k_k)
    kk = kk / jnp.maximum(jnp.sqrt(jnp.sum(kk * kk, axis=-1, keepdims=True)), 1e-12)
    k = k * (1.0 + (a - 1.0) * k_a)
    r_h, k_h, v_h, w_h, a_h = heads(r), heads(k), heads(v), heads(decay), heads(a)

    def step(state, inp):
        r_t, w_t, k_t, v_t, kk_t, a_t = inp
        sa = jnp.einsum('bhvk,bhk->bhv', state, -kk_t)
        state = (state * w_t[:, :, None, :] + sa[..., None] * (kk_t * a_t)[:, :, None, :]
                 + v_t[..., None] * k_t[:, :, None, :])
        return state, jnp.einsum('bhvk,bhk->bhv', state, r_t)

    xs = tuple(jnp.moveaxis(t, 1, 0) for t in (r_h, w_h, k_h, v_h, kk, a_h))
    _, y = lax.scan(step, jnp.zeros((B, H, N, N), jnp.float32), xs)
    y = jnp.moveaxis(y, 0, 1)
    mean = jnp.mean(y, axis=-1, keepdims=True)
    var = jnp.mean(jnp.square(y - mean), axis=-1, keepdims=True)
    yn = (y - mean) * lax.rsqrt(var + RWKV_GN_EPS) * gn_w.reshape(H, N) + gn_b.reshape(H, N)
    bonus = jnp.sum(r_h * k_h * r_k, axis=-1, keepdims=True) * v_h
    return ((yn + bonus).reshape(B, S, RWKV_WIDTH) * g).astype(u.dtype)

def nsa_mixer(q, k_c, v_c, k_s, v_s, k_w, v_w, gate_logits, rel_bias,
              pos_k, w1_k, w2_k, pos_v, w1_v, w2_v):
    B, S, _ = q.shape
    G, Hg, dh = NSA_KV_HEADS, NSA_GROUP, NSA_HEAD_DIM
    qh = q.reshape(B, S, G, Hg, dh).transpose(0, 2, 3, 1, 4) * (dh ** -0.5)
    kv = lambda t: t.reshape(B, S, G, dh).transpose(0, 2, 1, 3)
    k_c, v_c, k_s, v_s, k_w, v_w = (kv(t) for t in (k_c, v_c, k_s, v_s, k_w, v_w))
    gates = jax.nn.sigmoid(gate_logits.reshape(B, S, G, Hg, N_NSA_BRANCHES)).transpose(0, 2, 3, 1, 4)

    n_cmp = (S - CMP_BLOCK) // CMP_STRIDE + 1
    cmp_start = np.arange(n_cmp) * CMP_STRIDE
    cmp_idx = cmp_start[:, None] + np.arange(CMP_BLOCK)[None, :]
    cmp_end = jnp.asarray(cmp_start + CMP_BLOCK - 1, jnp.int32)

    def compress(t, pos, w1, w2):
        blocks = (t[:, :, cmp_idx] + pos).reshape(B, G, n_cmp, CMP_BLOCK * dh)
        return jax.nn.gelu(blocks @ w1) @ w2

    kc_blk = compress(k_c, pos_k, w1_k, w2_k)
    vc_blk = compress(v_c, pos_v, w1_v, w2_v)

    n_slc = S // SLC_BLOCK
    n_sel = min(N_SELECT, n_slc)
    slc_start = np.arange(n_slc) * SLC_BLOCK
    overlap = jnp.asarray(((cmp_start[:, None] <= slc_start[None, :] + SLC_BLOCK - 1)
                           & (cmp_start[:, None] + CMP_BLOCK - 1 >= slc_start[None, :])).astype(np.float32))
    ks_blk = k_s.reshape(B, G, n_slc, SLC_BLOCK, dh)
    vs_blk = v_s.reshape(B, G, n_slc, SLC_BLOCK, dh)

    kw_pad = jnp.pad(k_w, ((0, 0), (0, 0), (WINDOW, 0), (0, 0)))
    vw_pad = jnp.pad(v_w, ((0, 0), (0, 0), (WINDOW, 0), (0, 0)))

    tbl_g = rel_bias.reshape(N_BUCKETS, G, Hg).transpose(1, 0, 2)
    b_idx = jnp.arange(B)[:, None, None, None]
    g_idx = jnp.arange(G)[None, :, None, None]

    def shared_bias(dist):
        return rel_bias[t5_bucket(dist)].reshape(dist.shape + (G, Hg)).transpose(2, 3, 0, 1)

    def block(i):
        q0 = i * NSA_Q_BLOCK
        t = q0 + jnp.arange(NSA_Q_BLOCK, dtype=jnp.int32)
        qb = lax.dynamic_slice_in_dim(qh, q0, NSA_Q_BLOCK, axis=3)
        gb = lax.dynamic_slice_in_dim(gates, q0, NSA_Q_BLOCK, axis=3)
        dist_c = t[:, None] - cmp_end[None, :]
        lc = jnp.einsum('bghqd,bgcd->bghqc', qb, kc_blk) + shared_bias(dist_c)
        pc = masked_softmax(lc, dist_c >= 0).astype(vc_blk.dtype)
        o_c = jnp.einsum('bghqc,bgcd->bghqd', pc, vc_blk)
        imp = jnp.einsum('bghqc,cn->bgqn', pc, overlap)
        blk = jnp.arange(n_slc)[None, :]
        cur = (t // SLC_BLOCK)[:, None]
        valid = blk <= cur
        forced = (blk == 0) | (blk == cur) | (blk == cur - 1)
        score = jnp.where(valid, imp + jnp.where(forced, FORCE_BONUS, 0.0), -1.0)
        top_val, top_idx = lax.top_k(score, n_sel)
        k_sel = ks_blk[b_idx, g_idx, top_idx].reshape(B, G, NSA_Q_BLOCK, n_sel * SLC_BLOCK, dh)
        v_sel = vs_blk[b_idx, g_idx, top_idx].reshape(B, G, NSA_Q_BLOCK, n_sel * SLC_BLOCK, dh)
        pos_s = (top_idx[..., None] * SLC_BLOCK + jnp.arange(SLC_BLOCK)).reshape(B, G, NSA_Q_BLOCK, n_sel * SLC_BLOCK)
        dist_s = t[None, None, :, None] - pos_s
        mask_s = jnp.repeat(top_val >= 0, SLC_BLOCK, axis=-1) & (dist_s >= 0)
        bias_s = tbl_g[g_idx, t5_bucket(dist_s)].transpose(0, 1, 4, 2, 3)
        ls = jnp.einsum('bghqd,bgqkd->bghqk', qb, k_sel) + bias_s
        ps = masked_softmax(ls, mask_s[:, :, None]).astype(v_sel.dtype)
        o_s = jnp.einsum('bghqk,bgqkd->bghqd', ps, v_sel)
        kwb = lax.dynamic_slice_in_dim(kw_pad, q0, NSA_Q_BLOCK + WINDOW, axis=2)
        vwb = lax.dynamic_slice_in_dim(vw_pad, q0, NSA_Q_BLOCK + WINDOW, axis=2)
        pos_w = q0 - WINDOW + jnp.arange(NSA_Q_BLOCK + WINDOW, dtype=jnp.int32)
        dist_w = t[:, None] - pos_w[None, :]
        mask_w = (dist_w >= 0) & (dist_w < WINDOW) & (pos_w[None, :] >= 0)
        lw = jnp.einsum('bghqd,bgkd->bghqk', qb, kwb) + shared_bias(dist_w)
        pw = masked_softmax(lw, mask_w).astype(vwb.dtype)
        o_w = jnp.einsum('bghqk,bgkd->bghqd', pw, vwb)
        return gb[..., 0:1] * o_c + gb[..., 1:2] * o_s + gb[..., 2:3] * o_w

    out = lax.map(block, jnp.arange(S // NSA_Q_BLOCK, dtype=jnp.int32))
    return out.transpose(1, 0, 4, 2, 3, 5).reshape(B, S, NSA_WIDTH)

def hier_moe(h, w_rg, b_rg, w_re, b_re, w_gate, w_up, w_down):
    B, S, _ = h.shape
    p_grp = jax.nn.softmax((h @ w_rg + b_rg).astype(jnp.float32), axis=-1)
    p_top, grp = lax.top_k(p_grp, 1)
    le = (h @ w_re + b_re).astype(jnp.float32).reshape(B, S, N_GROUPS, EXPERTS_PER_GROUP)
    le_g = jnp.sum(le * jax.nn.one_hot(grp[..., 0], N_GROUPS)[..., None], axis=2)
    e_val, e_idx = lax.top_k(le_g, TOP_K_EXPERTS)
    w_e = jax.nn.softmax(e_val, axis=-1) * p_top
    expert_id = grp * EXPERTS_PER_GROUP + e_idx
    combine = jnp.sum(jax.nn.one_hot(expert_id, N_EXPERTS) * w_e[..., None], axis=2).astype(h.dtype)
    y = jnp.zeros_like(h)
    for e in range(N_EXPERTS):
        hid = jax.nn.silu(h @ w_gate[e]) * (h @ w_up[e])
        y = y + combine[..., e:e + 1] * (hid @ w_down[e])
    return y

def setup_inputs(seed: int = 0) -> dict:
    key = jax.random.key(seed)
    keys = iter(jax.random.split(key, 48))
    L, D = DEPTH, D_MODEL

    def nrm(shape, scale):
        return jax.random.normal(next(keys), shape, jnp.float32) * scale

    def gain(shape):
        return 1.0 + nrm(shape, 0.1)

    branch_scale = jnp.concatenate([jnp.full((POOL_WIDTH,), POOL_WIDTH ** -0.5, jnp.float32),
                                    jnp.full((RWKV_WIDTH,), RWKV_WIDTH ** -0.5, jnp.float32),
                                    jnp.full((NSA_WIDTH,), NSA_WIDTH ** -0.5, jnp.float32)])
    return {
        'x': nrm((BATCH, SEQ, D), 1.0),
        'rel_bias': nrm((N_BUCKETS, NSA_HEADS), 0.5),
        'norm_mix': gain((L, D)),
        'w_in': nrm((L, D, IN_COLS), D ** -0.5),
        'pool_w': nrm((L, POOL_GROUPS, POOL_GW, POOL_GW), POOL_GW ** -0.5),
        'pool_scale': gain((L, POOL_WIDTH)),
        'rw_mu': jax.random.uniform(next(keys), (L, RWKV_COLS), jnp.float32),
        'rw_w0': nrm((L, RWKV_WIDTH), 0.5) + 0.5,
        'rw_w_up': nrm((L, DECAY_LORA, RWKV_WIDTH), DECAY_LORA ** -0.5),
        'rw_a0': nrm((L, RWKV_WIDTH), 0.5),
        'rw_a_up': nrm((L, AAA_LORA, RWKV_WIDTH), AAA_LORA ** -0.5),
        'rw_g_up': nrm((L, GATE_LORA, RWKV_WIDTH), GATE_LORA ** -0.5),
        'rw_k_k': gain((L, RWKV_WIDTH)),
        'rw_k_a': gain((L, RWKV_WIDTH)),
        'rw_r_k': nrm((L, RWKV_HEADS, RWKV_HEAD_DIM), 0.1),
        'rw_gn_w': gain((L, RWKV_WIDTH)),
        'rw_gn_b': nrm((L, RWKV_WIDTH), 0.02),
        'cmp_pos_k': nrm((L, CMP_BLOCK, NSA_HEAD_DIM), 0.5),
        'cmp_w1_k': nrm((L, CMP_BLOCK * NSA_HEAD_DIM, CMP_HIDDEN), (CMP_BLOCK * NSA_HEAD_DIM) ** -0.5),
        'cmp_w2_k': nrm((L, CMP_HIDDEN, NSA_HEAD_DIM), CMP_HIDDEN ** -0.5),
        'cmp_pos_v': nrm((L, CMP_BLOCK, NSA_HEAD_DIM), 0.5),
        'cmp_w1_v': nrm((L, CMP_BLOCK * NSA_HEAD_DIM, CMP_HIDDEN), (CMP_BLOCK * NSA_HEAD_DIM) ** -0.5),
        'cmp_w2_v': nrm((L, CMP_HIDDEN, NSA_HEAD_DIM), CMP_HIDDEN ** -0.5),
        'w_branch': nrm((L, BRANCH_ROWS, D), 1.0) * branch_scale[None, :, None],
        'w_merge': nrm((L, D, N_BRANCHES * D), D ** -0.5),
        'b_merge': nrm((L, N_BRANCHES * D), 0.1),
        'w_out': nrm((L, D, D), D ** -0.5),
        'norm_ffn': gain((L, D)),
        'w_router_grp': nrm((L, D, N_GROUPS), D ** -0.5),
        'b_router_grp': nrm((L, N_GROUPS), 0.01),
        'w_router_exp': nrm((L, D, N_EXPERTS), D ** -0.5),
        'b_router_exp': nrm((L, N_EXPERTS), 0.01),
        'w_exp_gate': nrm((L, N_EXPERTS, D, D_EXPERT), D ** -0.5),
        'w_exp_up': nrm((L, N_EXPERTS, D, D_EXPERT), D ** -0.5),
        'w_exp_down': nrm((L, N_EXPERTS, D_EXPERT, D), D_EXPERT ** -0.5),
        'norm_final': gain((D,)),
    }

def reference(x, rel_bias, norm_mix, w_in, pool_w, pool_scale, rw_mu, rw_w0, rw_w_up, rw_a0,
              rw_a_up, rw_g_up, rw_k_k, rw_k_a, rw_r_k, rw_gn_w, rw_gn_b, cmp_pos_k, cmp_w1_k,
              cmp_w2_k, cmp_pos_v, cmp_w1_v, cmp_w2_v, w_branch, w_merge, b_merge, w_out, norm_ffn,
              w_router_grp, b_router_grp, w_router_exp, b_router_exp, w_exp_gate, w_exp_up,
              w_exp_down, norm_final):
    B, S, D = x.shape
    for l in range(DEPTH):
        h = rms_norm(x, norm_mix[l])
        proj = h @ w_in[l]
        u_pool, u_rwkv, u_nsa = split_cols(proj, [POOL_COLS, RWKV_COLS, NSA_COLS])
        y_pool = pool_mixer(u_pool, pool_w[l], pool_scale[l])
        y_rwkv = rwkv7_mixer(u_rwkv, rw_mu[l], rw_w0[l], rw_w_up[l], rw_a0[l], rw_a_up[l], rw_g_up[l],
                             rw_k_k[l], rw_k_a[l], rw_r_k[l], rw_gn_w[l], rw_gn_b[l])
        q, k_c, v_c, k_s, v_s, k_w, v_w, g_nsa = split_cols(
            u_nsa, [NSA_WIDTH] + [NSA_KV_WIDTH] * (2 * N_NSA_BRANCHES) + [N_NSA_BRANCHES * NSA_HEADS])
        y_nsa = nsa_mixer(q, k_c, v_c, k_s, v_s, k_w, v_w, g_nsa, rel_bias,
                          cmp_pos_k[l], cmp_w1_k[l], cmp_w2_k[l], cmp_pos_v[l], cmp_w1_v[l], cmp_w2_v[l])
        wb = w_branch[l]
        br_pool = y_pool @ wb[:POOL_WIDTH]
        br_rwkv = y_rwkv @ wb[POOL_WIDTH:POOL_WIDTH + RWKV_WIDTH]
        br_nsa = y_nsa @ wb[POOL_WIDTH + RWKV_WIDTH:]
        gates = jax.nn.sigmoid(h @ w_merge[l] + b_merge[l]).reshape(B, S, N_BRANCHES, D)
        merged = gates[:, :, 0] * br_pool + gates[:, :, 1] * br_rwkv + gates[:, :, 2] * br_nsa
        x = x + merged @ w_out[l]
        h = rms_norm(x, norm_ffn[l])
        x = x + hier_moe(h, w_router_grp[l], b_router_grp[l], w_router_exp[l], b_router_exp[l],
                         w_exp_gate[l], w_exp_up[l], w_exp_down[l])
    return rms_norm(x, norm_final)


_drawn_inputs = setup_inputs


def setup_inputs(seed=0):
    import zlib

    import numpy as np

    out = dict(_drawn_inputs(seed))
    spreads = {}
    factors = {'rw_k_k': 4.234,
     'rw_gn_b': 6.504,
     'cmp_pos_k': 3.165,
     'b_router_grp': 5.847,
     'b_router_exp': 4.443}
    for name, (base, spread) in spreads.items():
        noise = np.random.default_rng([zlib.crc32(name.encode()), seed]).standard_normal(out[name].shape)
        drawn = base * np.exp(spread * noise) if base else spread * noise
        out[name] = __import__('jax').numpy.asarray(drawn.astype(out[name].dtype))
    for name, factor in factors.items():
        out[name] = (out[name] * factor).astype(out[name].dtype)
    return out
```

```python
import math
from contextlib import ExitStack

import numpy as np

import concourse.bass as bass
from concourse import mybir

F32 = mybir.dt.float32
ALU = mybir.AluOpType
ACT = mybir.ActivationFunctionType
AXX = mybir.AxisListType.X

P = 128
D = 1024
S = 256
NT = S // P
KD = D // P
PW = 512
RW = 512
RH = 8
NH, NG = 16, 4
DH = 64
NCMP, CSTRIDE, CBLOCK = 15, 16, 32
NB = 32
E, EPG, NGRP = 32, 8, 4
DE = 256
CH = 64
NCH = S // CH
NEG = -1.0e30
DECAY = math.exp(-0.5)
GELU_C = math.sqrt(2.0 / math.pi)

SLOT = 2048
RING = 12
FRING = 6
C_LORA = 0
C_K, C_R, C_V = 1, 3, 5
C_KC, C_VC, C_Q = 7, 8, 9
C_KS, C_KW, C_VS, C_VW = 13, 14, 15, 16
C_POOL = 17
C_W1K, C_W1V = 19, 21
C_MERGE = 23
C_OUT = 43
C_ROUTER = 47
NFRONT = 48
GANG = 4
NGANG = E // GANG
CAP = 32
GCH = 12


def columns(parts):
    at, out = 0, {}
    for name, n in parts:
        out[name] = (at, at + n)
        at += n
    return out, at


PARAMS, NPARAMS = columns([
    ("g_mix", 8), ("g_ffn", 8), ("mu", 14), ("w0", 4), ("a0", 4), ("k_k", 4), ("k_a", 4), ("r_k", 4),
    ("gn_w", 4), ("gn_b", 4), ("pool_scale", 4), ("b_merge", 24),
    ("lora_up", RW), ("g_up", RW), ("pool_w", PW), ("w2_k", 2 * DH), ("w2_v", 2 * DH),
    ("pos_k", 16), ("pos_v", 16), ("rel", NH), ("b_router", NGRP + E)])
CONSTS, NCONSTS = columns([
    ("ident", P), ("flip", P), ("headsum", P), ("intra", 4 * P), ("level", 6 * P),
    ("onehot", 384), ("eye64", DH), ("count", 4 * 16), ("ones", P), ("earlier", P),
    ("neghalf", 8), ("falling", E)])


def t5_bucket(dist):
    n = np.maximum(dist, 0)
    nf = np.maximum(n, 1).astype(np.float32)
    large = 16 + (np.log(nf / np.float32(16)) / np.float32(math.log(8)) * np.float32(16)).astype(np.int32)
    return np.where(n < 16, n, np.minimum(large, NB - 1))


def constants():
    c = np.zeros((P, NCONSTS), np.float32)

    def put(name, a):
        lo, hi = CONSTS[name]
        c[:a.shape[0], lo:hi] = a.reshape(a.shape[0], hi - lo)

    r = np.arange(P)
    put("ident", np.eye(P))
    put("flip", np.eye(P)[::-1])
    put("headsum", (r[:, None] // DH == r[None, :] // DH) * 1.0)
    same = r[:, None] // CH == r[None, :] // CH
    before, upto = same & (r[:, None] < r[None, :]), same & (r[:, None] <= r[None, :])
    put("intra", np.concatenate([before, upto, before, upto], 1) * 1.0)
    level = []
    for n in (1, 2, 4, 8, 16, 32):
        level.append((r[:, None] // (2 * n) == r[None, :] // (2 * n))
                     & (r[:, None] % (2 * n) < n) & (r[None, :] % (2 * n) >= n))
    put("level", np.concatenate(level, 1) * 1.0)
    dist = 255 - np.arange(384)
    put("onehot", np.concatenate([(np.arange(NB)[:, None] == t5_bucket(dist)[None, :]) * 1.0,
                                  np.where(dist < 0, NEG, 0.0)[None]]))
    put("eye64", np.eye(P)[:, :DH] + np.eye(P)[:, DH:])
    w = np.array([2, 4, 8, 16])
    put("count", np.broadcast_to(1.0 / np.minimum(np.arange(16)[None] + 1, w[:, None]), (P, 4, 16)))
    put("ones", np.ones((P, P)))
    put("earlier", (r[:, None] < r[None, :]) * 1.0)
    put("neghalf", np.full((P, 8), -0.5))
    put("falling", np.broadcast_to(E - np.arange(E), (P, E)) * 1.0)
    return c


def build_layer(nc, x, params, consts, front, experts, g_final, out, bias_rows):
    ctx = ExitStack()
    with ctx:
        def sb(name, shape):
            return ctx.enter_context(nc.sbuf_tensor(name, shape, F32))

        def sem(name):
            return ctx.enter_context(nc.semaphore(name))

        def like(ap, shape):
            return ap.to_broadcast(shape)

        ring = sb("ring", [P, RING * SLOT])
        par = sb("par", [P, NPARAMS])
        con = sb("con", [P, NCONSTS])
        tok = sb("tok", [P, NT, D])
        hT = sb("hT", [P, KD, S])
        yT = sb("yT", [P, 16, S])
        rawf = sb("raw", [P, 4 * (S + 1)])
        raw = rawf[:, :].rearrange("p (b m t) -> p b m t", b=2, m=2)
        mix = sb("mix", [P, 14, S])
        t1 = sb("t1", [P, 4, S])
        t2 = sb("t2", [P, 4, S])
        t3 = sb("t3", [P, 4, S])
        arbk = sb("arbk", [P, 16, S])
        xcmp = sb("xcmp", [P, 2, 16, NG * NCMP])
        vtok = sb("vtok", [P, 2, NT, 256])
        small = sb("small", [P, 256])
        state = sb("state", [P, 2, 4, DH])
        gate_t = sb("gate_t", [P, NT, 3 * NH])

        def pr(name, rows=P):
            lo, hi = PARAMS[name]
            return par[0:rows, lo:hi]

        def cn(name, rows=P):
            lo, hi = CONSTS[name]
            return con[0:rows, lo:hi]

        ident = cn("ident")
        late = ring[:, FRING * SLOT:RING * SLOT]
        bias = late[:, 0:4096].rearrange("p (h m) -> p h m", h=NH)
        amat = late[:, 4096:8192].rearrange("p (h j t) -> p h j t", h=RH, j=4)
        qT = late[:, 8192:10240].rearrange("p (m t) -> p m t", m=8)
        kT = late[:, 10240:12288].rearrange("p (b g t) -> p b g t", b=2, g=NG)
        window = arbk[:, :, :]
        ar = arbk[:, 0:8, :].rearrange("p c t -> p (c t)").rearrange("p (m i j t) -> p m i j t", m=4, i=2, j=2)
        bf = arbk[:, 8:12, :]
        kf = arbk[:, 12:16, :]
        kshift = yT[:, 8:16, :].rearrange("p (b g) t -> p b g t", b=2)
        btok = t1[:, 0:2, :].rearrange("p c t -> p (c t)")
        ktok = t1[:, 2:4, :].rearrange("p c t -> p (c t)")
        vrow = t2[:, 0:2, :].rearrange("p c t -> p (c t)")
        lmask = t2[:, 2:4, :].rearrange("p c t -> p (c t)").rearrange("p (h t) -> p h t", h=4)
        xinv = t3[:, 0:2, :].rearrange("p c t -> p (c t)").rearrange("p (h t) -> p h t", h=4)
        zinv = [rawf[:, g * 512:(g + 1) * 512].rearrange("p (h t) -> p h t", h=4) for g in range(2)]
        winv = t3[:, 2:4, :].rearrange("p c t -> p (c t)").rearrange("p (h t) -> p h t", h=4)
        rhs = mix[:, 0:4, :].rearrange("p c t -> p (c t)").rearrange("p (h j v) -> p h j v", h=RH, j=2)
        bonus = mix[:, 4:8, :]
        fc = t3[:, :, :].rearrange("p c t -> p (c t)").rearrange("p (c m j v) -> p c m j v", c=2, m=4, j=2)
        ynorm = t2[:, 2:4, :].rearrange("p c t -> p (c t)")
        ysq = t3[:, 0:2, :].rearrange("p c t -> p (c t)")
        pend = small[:, 0:16].rearrange("p (m c) -> p m c", m=4)
        stat = small[:, 16:64]
        tokf = tok[:, :, :].rearrange("p i d -> p (i d)")
        prob = tokf[:, 0:1024].rearrange("p (b n) -> p b n", b=2)
        probT = tokf[:, 1024:2048].rearrange("p (b n) -> p b n", b=2)
        xf = xcmp[:, :, :, :].rearrange("p b j n -> p (b j n)")
        gx = xf[0:60, 0:512]
        gy = xf[0:60, 512:1024]
        hidT = xf[:, 1024:1264].rearrange("p (f n) -> p f n", f=4)
        kcb = xf[:, 1264:1324]
        vcb = xf[0:NCMP, 1324:1580].rearrange("p (g v) -> p g v", g=NG)
        cprob = t2[:, :, :].rearrange("p c t -> p (c t)")[:, 0:480].rearrange("p (u m n) -> p u m n", u=4, m=8)
        cprobT = t1[0:NCMP, :, :].rearrange("p c t -> p (c t)").rearrange("p (i h t) -> p i h t", i=2, h=4)
        astat = small[:, 64:128]
        gsig = [t1[:, 0:2, :], t1[:, 2:4, :], t3[:, 0:2, :]]
        merged = arbk[:, 0:8, :]
        macc = t2[:, 0:2, :]
        mtmp = t2[:, 2:4, :]
        xn = mix[:, 0:8, :].rearrange("p c t -> p (c t)").rearrange("p (i d) -> p i d", i=2)
        arf = arbk[:, :, :].rearrange("p c t -> p (c t)")
        gath = arf[:, 0:1024].rearrange("p (k s) -> p k s", k=KD)
        ydown = arf[:, 1024:2048]
        gtanh = arf[:, 2048:2304]
        ghid = arf[:, 2304:2560]
        ghidT = arf[:, 2560:2816].rearrange("p (f s) -> p f s", f=2)
        sel = arf[:, 2816:3072].rearrange("p (i s) -> p i s", i=2)
        wsel = arf[:, 3072:3328].rearrange("p (i s) -> p i s", i=2)
        wselT = arf[:, 3328:3584].rearrange("p (i t) -> p i t", i=2)
        place = arf[:, 3584:3584 + 2 * (E + GANG)].rearrange("p (i e) -> p i e", i=2)
        gsi = arbk[:, 8:12, :].rearrange("p c t -> p (c t)").rearrange("p (e n) -> p e n", e=GANG)
        hid = arbk[:, 12:16, :].rearrange("p c t -> p (c t)").rearrange("p (e n) -> p e n", e=GANG)
        hidm = t1[:, :, :].rearrange("p c t -> p (c t)").rearrange("p (e f t) -> p e f t", e=GANG, f=2)
        combine = small[:, 112:112 + 2 * (E + GANG)].rearrange("p (i e) -> p i e", i=2)
        member = mix[:, 8, 0:2 * E].rearrange("p (i e) -> p i e", i=2)
        crowd = ctx.enter_context(nc.sbuf_tensor("crowd", [P, 1], mybir.dt.int32))
        halves = small[:, 192:224]
        rtf = t3[:, :, :].rearrange("p c t -> p (c t)")
        rt_at, _ = columns([("lg", 72), ("gh", 8), ("ge", 8), ("h1", 64), ("h2", 64), ("gm", 2), ("m1", 2), ("m2", 2),
                            ("tmp", 2), ("w1", 2), ("w2", 2)])

        def rt(name):
            lo, hi = rt_at[name]
            return rtf[:, lo:hi] if hi - lo == 2 else rtf[:, lo:hi].rearrange("p (i n) -> p i n", i=2)

        gfin = yT[:, 0:4, :].rearrange("p c t -> p (c t)")

        bank = [ctx.enter_context(nc.psum_tensor(f"bank{b}", [P, 512], F32)) for b in range(8)]

        loaded = [sem(f"slot_loaded{s}") for s in range(RING)]
        taken = sem("chunks_taken")
        bank_full = [sem(f"bank_full{b}") for b in range(8)]
        bank_free = [sem(f"bank_free{b}") for b in range(8)]
        names = [
            "small_loaded", "x_loaded", "x_again", "stored", "gfin_loaded", "win_stored", "win_ready",
            "raw_zeroed", "root_ready", "lmask_ready", "state_zeroed",
            "raw_ready", "gate_tanh", "lora_w_ready", "lora_g_tanh", "kshift_ready", "bias_ready", "q_ready",
            "k_ready", "v_ready", "u_ready", "gx_ready", "gelu_tanh", "decay_tanh", "rate_tanh", "kk_root",
            "hidT_ready", "cmp_kv_ready", "decay_exp", "cexp_ready", "cprobT_ready", "exp_ready", "probT_ready",
            "tok_ready", "w_ready", "rhs_ready", "xu_ready", "gn_ready", "gsig_ready", "router_exp",
            "silu_tanh", "hidT2_ready", "act_chain", "gtanh_ready", "wselT_ready", "ghidT_ready",
            "ydown_ready",
            "gathered", "wsel_turned", "gate_up", "hid_turned", "downed", "scattered",
            "halves_ready", "rms_in", "xn_ready", "hT_ready", "raw_used", "mix_ready", "win_row", "gates_ready",
            "xcmp_ready", "pool_ready", "kk_sq_ready", "kk_max", "gelu_in", "gelu_ready", "log_ready",
            "lora_g_ready", "pool_out", "bonus_ready", "rwkv_ready", "cexp_in", "cprob_ready", "exp_in",
            "prob_ready", "nsa_ready", "amat_ready", "z_ready", "x_ready", "rx_ready", "fc_ready",
            "state_ready", "ynorm_ready", "yrw_ready", "gated", "merged_ready", "sum_ready", "router_in",
            "combine_ready", "hid_ready", "moe_ready", "member_ready", "crowd_ready", "sel_ready", "gath_ready",
            "ghid_ready", "summed", "final_ready", "dve_chain"]
        q = {n: sem(n) for n in names}

        def ordinal():
            seen = {}

            def nth(b):
                seen[b] = seen.get(b, -1) + 1
                return seen[b]
            return nth

        plan = {}
        nth = ordinal()

        def hand(name, b):
            assert name not in plan
            plan[name] = (b, nth(b))

        for n in range(4):
            hand(f"xT{n}", n)
        hand("brow", 4)
        hand("lora_in", 0)
        hand("gates", 1)
        for c in range(1, 7):
            hand(f"rkv{c}", 2 + c % 2)
        for n in range(8):
            hand(f"bias{n}", 5 + n % 2)
        hand("kc", 0), hand("vc", 1)
        for n in range(4):
            hand(f"q{n}", 2 + n % 2)
        hand("ks", 0), hand("kw", 1), hand("vs", 2), hand("vw", 3)
        hand("pool0", 4), hand("pool1", 5)
        hand("mlp_k", 6), hand("mlp_v", 7)
        for n in range(2):
            hand(f"wup{n}", n)
        for n in range(2):
            hand(f"aup{n}", 2 + n)
        for n in range(2):
            hand(f"kk{n}", n)
        hand("poolmix0", 2), hand("poolmix1", 3)
        hand("hidT", 6), hand("kcb", 7), hand("vcb", 6)
        for n in range(2):
            hand(f"bonus{n}", n)
        for u in range(4):
            hand(f"cs{u}", 2 + u % 2)
        for g in range(NG):
            for i in range(NT):
                hand(f"cT{g}{i}", 4 + i)
            for u in range(6):
                hand(f"s{g}{u}", 2 + u % 2)
                hand(f"pT{g}{u}", 4 + u % 2)
            hand(f"o{g}", 6 + g % 2)
        for i in range(NT):
            for w in range(3):
                hand(f"tok{i}{w}", w)
            hand(f"atok{i}", 3)
            for h in range(RH):
                hand(f"A{i}{h}", 4 + h % 2)
            for grp in range(2):
                hand(f"XZ{i}{grp}", 0)
                for n in range(5):
                    hand(f"W{i}{grp}{n}", 1)
                    if n < 4:
                        hand(f"X{i}{grp}{n}", 3)
                    hand(f"Z{i}{grp}{n}", 2)
            hand(f"w0{i}", 0)
            for n in range(2):
                hand(f"xu{i}{n}", 1 + n)
            for n in range(2):
                hand(f"rx{i}{n}", 3 + n)
            for c in range(2):
                hand(f"fc{i}{c}", 5 + c)
            for c in range(2):
                if 2 * i + c < NCH - 1:
                    hand(f"st{i}{c}", 7)
            for p in range(2):
                hand(f"y{i}{p}", 1 + p)
            hand(f"yT{i}", 0)
            hand(f"gup{i}", 3)
        for n in range(4):
            for b in range(3):
                hand(f"mg{n}{b}", b)
            for b in range(3):
                hand(f"mb{n}{b}", 3 + b)
        for n in range(4):
            hand(f"out{n}", 6 + n % 2)
        for n in range(4):
            hand(f"hT2{n}", n)
        hand("router", 4)
        hand("places", 5)
        before_loop = [nth(b) for b in range(8)]


        def full(eng, name):
            b, n = plan[name]
            eng.wait_ge(bank_full[b], n + 1)
            return bank[b]

        def free(ins, name):
            ins.then_inc(bank_free[plan[name][0]], 1)

        def chainer(eng, own):
            count = {}

            def chain(ins, name=None, hold=True):
                name = name or own
                count[name] = count.get(name, 0) + 1
                ins.then_inc(q[name], 1)
                if hold:
                    eng.wait_ge(q[name], count[name])
            chain.count = count
            return chain

        block = ctx.enter_context(nc.Block())

        @block.sync
        def _(sp):
            sp.dma_start(tok[:, :, :], x.rearrange("(i p) d -> p i d", p=P)).then_inc(q["x_loaded"], 16)
            sp.dma_start(con[:, :], consts).then_inc(q["small_loaded"], 16)
            sp.dma_start(par[:, :], params).then_inc(q["small_loaded"], 16)
            for s in range(FRING):
                sp.dma_start(ring[:, s * SLOT:(s + 1) * SLOT], front[s]).then_inc(loaded[s], 16)
            sp.wait_ge(q["win_row"], 1)
            sp.dma_start(bias_rows, arbk[0:NH, 0:2, :].rearrange("p a b -> p (a b)")[:, 0:384])\
                .then_inc(q["win_stored"], 16)
            sp.wait_ge(q["win_stored"], 16)
            sp.dma_start(window, bass.AP(bias_rows.tensor, 0, [[1, P], [384, NH], [1, 256]]))\
                .then_inc(q["win_ready"], 16)
            with sp.Fori(1, NFRONT // FRING) as rnd:
                for s in range(FRING):
                    sp.wait_ge(taken, rnd * FRING + (s + 1 - FRING))
                    sp.dma_start(ring[:, s * SLOT:(s + 1) * SLOT], front[rnd * FRING + s]).then_inc(loaded[s], 16)
            for s in range(FRING):
                sp.wait_ge(taken, NFRONT + s + 1 - FRING)
                sp.dma_start(ring[:, s * SLOT:(s + 1) * SLOT], experts[0, s]).then_inc(loaded[s], 16)
            with sp.Fori(1, NGANG) as gang:
                for s in range(GCH):
                    sp.wait_ge(taken, gang * GCH + (NFRONT - GCH + s + 1))
                    sp.dma_start(ring[:, s * SLOT:(s + 1) * SLOT], experts[gang, s]).then_inc(loaded[s], 16)
            sp.wait_ge(q["final_ready"], 2)
            sp.dma_start(out.rearrange("(i p) d -> p i d", p=P), hT[:, :, :].rearrange("p c t -> p (c t)")
                         .rearrange("p (i d) -> p i d", i=2)).then_inc(q["stored"], 16)
            sp.wait_ge(q["stored"], 16)

        @block.tensor
        def _(pe):
            def begin(name):
                b, n = plan[name]
                if n:
                    pe.wait_ge(bank_free[b], n)
                return bank[b]

            def end(ins, name):
                ins.then_inc(bank_full[plan[name][0]], 1)

            def chunk(n):
                pe.wait_ge(loaded[n % FRING], 16 * (n // FRING + 1))
                return ring[:, (n % FRING) * SLOT:(n % FRING + 1) * SLOT]

            owed = [0]

            def pe_take():
                owed[0] += 1

            def first(ins):
                if owed[0]:
                    ins.then_inc(taken, owed[0])
                    owed[0] = 0
                return ins

            def mm(o, l, r, k, n):
                return first(pe.matmul(o, l, r, start=(k == 0), stop=(k == n - 1)))

            def project(name, n):
                w = chunk(n).rearrange("p (k c) -> p k c", k=KD)
                o = begin(name)
                for m in range(2):
                    for k in range(KD):
                        last = mm(o[:, m * S:(m + 1) * S], w[:, k, m * P:(m + 1) * P], hT[:, k, :], k, KD)
                end(last, name)
                pe_take()

            for n in range(4):
                i = n // 2
                pe.wait_ge(q["xn_ready"], i + 1)
                if n == 0:
                    pe.wait_ge(q["small_loaded"], 32)
                o = begin(f"xT{n}")
                for k in range(4):
                    kk = (n % 2) * 4 + k
                    last = pe.transpose(o[:, k * P:(k + 1) * P], xn[:, i, kk * P:(kk + 1) * P], ident)
                end(last, f"xT{n}")
            o = begin("brow")
            end(pe.matmul(o[0:NH, 0:384], pr("rel", NB + 1), cn("onehot", NB + 1), start=True, stop=True), "brow")
            pe.wait_ge(q["hT_ready"], 4)

            w = chunk(C_LORA).rearrange("p (k c) -> p k c", k=KD)
            o = begin("lora_in")
            for lo, n, col in ((0, 64, 0), (64, 96, S)):
                for k in range(KD):
                    last = mm(o[0:n, col:col + S], w[:, k, lo:lo + n], hT[:, k, :], k, KD)
            end(last, "lora_in")
            o = begin("gates")
            for i in range(NT):
                for k in range(KD):
                    last = mm(o[:, i * 48:(i + 1) * 48], hT[:, k, i * P:(i + 1) * P], w[:, k, 160:208], k, KD)
            end(last, "gates")
            pe_take()
            for c in range(1, 7):
                project(f"rkv{c}", c)

            project("kc", C_KC)
            project("vc", C_VC)
            pe.wait_ge(q["win_ready"], 16)
            wf = window.rearrange("p a b -> p (a b)")
            for n in range(8):
                o = begin(f"bias{n}")
                end(pe.matmul(o[:, :], cn("flip"), wf[:, n * 512:(n + 1) * 512], start=True, stop=True), f"bias{n}")
            for n in range(4):
                project(f"q{n}", C_Q + n)
            project("ks", C_KS)
            project("kw", C_KW)
            for name, c in (("vs", C_VS), ("vw", C_VW)):
                w = chunk(c).rearrange("p (k c) -> p k c", k=KD)
                o = begin(name)
                for i in range(NT):
                    for k in range(KD):
                        last = mm(o[:, i * 256:(i + 1) * 256], hT[:, k, i * P:(i + 1) * P], w[:, k, :], k, KD)
                end(last, name)
                pe_take()
            project("pool0", C_POOL)
            project("pool1", C_POOL + 1)

            for b, (name, c0) in enumerate((("mlp_k", C_W1K), ("mlp_v", C_W1V))):
                pe.wait_ge(q["xcmp_ready"], b + 1)
                o = begin(name)
                for half in range(2):
                    w = chunk(c0 + half).rearrange("p (k c) -> p k c", k=KD)
                    for j in range(8):
                        last = mm(o[0:60, 0:256], xcmp[:, b, half * 8 + j, :], w[:, j, :], half * 8 + j, 16)
                    if half:
                        end(last, name)
                    pe_take()

            pe.wait_ge(q["lora_w_ready"], 1)
            for n in range(2):
                o = begin(f"wup{n}")
                for m in range(2):
                    c = (2 * n + m) * P
                    last = pe.matmul(o[:, m * S:(m + 1) * S], pr("lora_up")[0:32, c:c + P], mix[0:32, 12, :],
                                     start=True, stop=True)
                end(last, f"wup{n}")
            for n in range(2):
                o = begin(f"aup{n}")
                for m in range(2):
                    c = (2 * n + m) * P
                    last = pe.matmul(o[:, m * S:(m + 1) * S], pr("lora_up")[32:64, c:c + P], mix[32:64, 12, :],
                                     start=True, stop=True)
                end(last, f"aup{n}")
            pe.wait_ge(q["kk_sq_ready"], 1)
            for n in range(2):
                o = begin(f"kk{n}")
                end(pe.matmul(o[:, :], cn("headsum"), t3[:, 2 * n:2 * n + 2, :], start=True, stop=True), f"kk{n}")

            pe.wait_ge(q["pool_ready"], 1)
            for n in range(2):
                o = begin(f"poolmix{n}")
                for m in range(2):
                    gi = 2 * n + m
                    last = pe.matmul(o[:, m * S:(m + 1) * S], pr("pool_w")[:, gi * P:(gi + 1) * P],
                                     yT[:, gi, :], start=True, stop=True)
                end(last, f"poolmix{n}")

            pe.wait_ge(q["gelu_ready"], 1)
            o = begin("hidT")
            for f in range(4):
                last = pe.transpose(o[:, f * 60:(f + 1) * 60], gx[:, f * P:(f + 1) * P], ident[0:60, 0:60])
            end(last, "hidT")
            pe.wait_ge(q["hidT_ready"], 1)
            w2k = pr("w2_k").rearrange("p (f v) -> p f v", f=2)
            w2v = pr("w2_v").rearrange("p (f v) -> p f v", f=2)
            o = begin("kcb")
            for p in range(2):
                for f in range(2):
                    last = mm(o[64 * p:64 * p + 64, 0:60], w2k[:, f, :], hidT[:, f, :], f, 2)
            end(last, "kcb")
            o = begin("vcb")
            for g in range(NG):
                for f in range(2):
                    last = mm(o[0:NCMP, g * 64:g * 64 + 64], hidT[:, 2 + f, g * NCMP:(g + 1) * NCMP], w2v[:, f, :], f, 2)
            end(last, "vcb")

            pe.wait_ge(q["bonus_ready"], 1)
            for n in range(2):
                o = begin(f"bonus{n}")
                end(pe.matmul(o[:, :], cn("headsum"), mix[:, 4 + 2 * n:6 + 2 * n, :], start=True, stop=True), f"bonus{n}")

            pe.wait_ge(q["gates_ready"], 1)
            pe.wait_ge(q["q_ready"], 4)
            pe.wait_ge(q["k_ready"], 2)
            pe.wait_ge(q["v_ready"], 2)
            pe.wait_ge(q["cmp_kv_ready"], 2)
            for u in range(4):
                i, p = u // 2, u % 2
                nc_ = 7 if i == 0 else NCMP
                o = begin(f"cs{u}")
                for m in range(8):
                    g = (2 * m + p) // 4
                    last = pe.matmul(o[:, m * nc_:(m + 1) * nc_], qT[64 * p:64 * p + 64, m, i * P:(i + 1) * P],
                                     kcb[64 * p:64 * p + 64, g * NCMP:g * NCMP + nc_], start=True, stop=True)
                end(last, f"cs{u}")
            def scores(g, u):
                p = u % 2
                o = begin(f"s{g}{u}")
                rows = slice(64 * p, 64 * p + 64)
                for b in range(4):
                    if u < 2:
                        br, hp = b // 2, b % 2
                        last = pe.matmul(o[:, b * P:(b + 1) * P], qT[rows, 2 * g + hp, 0:P], kT[rows, br, g, 0:P],
                                         start=True, stop=True)
                    elif b < 2:
                        last = pe.matmul(o[:, b * S:(b + 1) * S], qT[rows, 2 * g + b, P:S],
                                         kT[rows, (u - 2) // 2, g, :], start=True, stop=True)
                end(last, f"s{g}{u}")

            def turn(g, u):
                n = g * 6 + u
                pe.wait_ge(q["prob_ready"], n + 1)
                o = begin(f"pT{g}{u}")
                for b in range(4):
                    src = b if u < 2 else (b % 2) * 2 + b // 2
                    last = pe.transpose(o[:, b * P:(b + 1) * P], prob[:, n % 2, src * P:(src + 1) * P], ident)
                end(last, f"pT{g}{u}")

            def weigh(g, u, o):
                n = g * 6 + u
                p = u % 2
                pe.wait_ge(q["probT_ready"], n + 1)
                i = 0 if u < 2 else 1
                for b in range(2):
                    br, kb = (b, 0) if u < 2 else ((u - 2) // 2, b)
                    last = pe.matmul(o[64 * p:64 * p + 64, :].rearrange("p (h t) -> p h t", h=2)[:, :, i * P:(i + 1) * P],
                                     vtok[:, br, kb, g * DH:(g + 1) * DH], probT[:, n % 2, b * 2 * P:(b + 1) * 2 * P],
                                     start=False, stop=(b == 1 and (u < 2 or u >= 4)), skip_group_check=True)
                return last

            for g in range(NG):
                pe.wait_ge(q["cprob_ready"], 4)
                for i in range(NT):
                    nc_ = 7 if i == 0 else NCMP
                    o = begin(f"cT{g}{i}")
                    for b in range(4):
                        p, hp = b // 2, b % 2
                        last = pe.transpose(o[0:nc_, b * P:(b + 1) * P], cprob[:, 2 * i + p, 2 * g + hp, 0:nc_], ident)
                    end(last, f"cT{g}{i}")
                scores(g, 0)
                scores(g, 1)
                acc = begin(f"o{g}")
                for i in range(NT):
                    nc_ = 7 if i == 0 else NCMP
                    pe.wait_ge(q["cprobT_ready"], 2 * g + i + 1)
                    for p in range(2):
                        last = pe.matmul(acc[64 * p:64 * p + 64, :].rearrange("p (h t) -> p h t", h=2)[:, :, i * P:(i + 1) * P],
                                         vcb[0:nc_, g, :], cprobT[0:nc_, i, 2 * p:2 * p + 2, :], start=(i == 0), stop=False,
                                         skip_group_check=True)
                for u in range(6):
                    turn(g, u)
                    if u + 2 < 6:
                        scores(g, u + 2)
                    last = weigh(g, u, acc)
                end(last, f"o{g}")

            pe.wait_ge(q["rwkv_ready"], 1)
            for i in range(NT):
                ts = slice(i * P, (i + 1) * P)
                for w_, src in enumerate((bf, kf, mix[:, 8:12, :])):
                    o = begin(f"tok{i}{w_}")
                    for m in range(4):
                        last = pe.transpose(o[:, m * P:(m + 1) * P], src[:, m, ts], ident)
                    end(last, f"tok{i}{w_}")
                o = begin(f"atok{i}")
                for m in range(4):
                    last = pe.transpose(o[:, m * P:(m + 1) * P], ar[:, m, i, 0, :], ident)
                end(last, f"atok{i}")
                for h in range(RH):
                    m, p = h // 2, h % 2
                    rows = slice(64 * p, 64 * p + 64)
                    o = begin(f"A{i}{h}")
                    for j, left in enumerate((bf, kf)):
                        last = pe.matmul(o[:, j * S:(j + 1) * S], left[rows, m, ts], ar[rows, m, i, :, :],
                                         start=True, stop=True)
                    end(last, f"A{i}{h}")
                for grp in range(2):
                    z = zinv[grp]
                    turn_ = 2 * i + grp
                    pe.wait_ge(q["z_ready"], 6 * turn_ + 1)
                    o = begin(f"XZ{i}{grp}")
                    for h in range(4):
                        last = pe.transpose(o[:, h * P:(h + 1) * P], z[:, h, :], ident)
                    end(last, f"XZ{i}{grp}")
                    for n in range(5):
                        pe.wait_ge(q["x_ready"], 5 * turn_ + n + 1)
                        pe.wait_ge(q["lmask_ready"], 6 * turn_ + n + 2)
                        o = begin(f"W{i}{grp}{n}")
                        for h in range(4):
                            last = pe.matmul(o[:, h * P:(h + 1) * P], lmask[:, h, :], xinv[:, h, :], start=True, stop=True)
                        end(last, f"W{i}{grp}{n}")
                        pe.wait_ge(q["w_ready"], 5 * turn_ + n + 1)
                        pe.wait_ge(q["z_ready"], 6 * turn_ + n + 1)
                        if n < 4:
                            o = begin(f"X{i}{grp}{n}")
                            for h in range(4):
                                last = pe.matmul(o[:, h * P:(h + 1) * P], z[:, h, :], winv[:, h, :], start=True, stop=True)
                            end(last, f"X{i}{grp}{n}")
                        o = begin(f"Z{i}{grp}{n}")
                        for h in range(4):
                            last = pe.matmul(o[:, h * P:(h + 1) * P], winv[:, h, :], z[:, h, :], start=True, stop=True)
                        end(last, f"Z{i}{grp}{n}")
                pe.wait_ge(q["z_ready"], 12 * (i + 1))
                pe.wait_ge(q["tok_ready"], 4 * (i + 1))
                o = begin(f"w0{i}")
                for h in range(RH):
                    last = pe.matmul(o[:, h * DH:(h + 1) * DH], amat[:, h, 2, :], vrow[:, h * DH:(h + 1) * DH],
                                     start=True, stop=True)
                end(last, f"w0{i}")
                pe.wait_ge(q["rhs_ready"], i + 1)
                for n in range(2):
                    z = zinv[n]
                    o = begin(f"xu{i}{n}")
                    for h in range(4):
                        last = pe.matmul(o[:, h * P:(h + 1) * P], z[:, h, :], rhs[:, 4 * n + h, :, :], start=True, stop=True)
                    end(last, f"xu{i}{n}")
                pe.wait_ge(q["xu_ready"], 2 * (i + 1))
                for n in range(2):
                    o = begin(f"rx{i}{n}")
                    for hh in range(4):
                        h = 4 * n + hh
                        last = pe.matmul(o[64 * (h % 2):64 * (h % 2) + 64, (hh // 2) * P:(hh // 2 + 1) * P],
                                         rhs[:, h, 0, :], amat[:, h, 1, :], start=True, stop=True)
                    end(last, f"rx{i}{n}")
                for c in range(2):
                    rows = slice(64 * c, 64 * c + 64)
                    o = begin(f"fc{i}{c}")
                    for h in range(RH):
                        m, p = h // 2, h % 2
                        oo = o[64 * p:64 * p + 64, m * P:(m + 1) * P]
                        hs = slice(h * DH, (h + 1) * DH)
                        pe.matmul(oo[:, 0:64], rhs[rows, h, 0, :], btok[rows, hs], start=True, stop=True)
                        pe.matmul(oo[:, 64:128], btok[rows, hs], rhs[rows, h, 1, :], start=True, stop=False)
                        last = pe.matmul(oo[:, 64:128], ktok[rows, hs], vrow[rows, hs], start=False, stop=True)
                    end(last, f"fc{i}{c}")
                ybank = [begin(f"y{i}{p}") for p in range(2)]
                for h in range(RH):
                    m, p = h // 2, h % 2
                    oo = ybank[p][:, m * DH:(m + 1) * DH]
                    pe.matmul(oo, amat[:, h, 1, :], rhs[:, h, 1, :], start=(m == 0), stop=False, skip_group_check=True)
                    pe.matmul(oo, amat[:, h, 3, :], vrow[:, h * DH:(h + 1) * DH], start=False, stop=False,
                              skip_group_check=True)
                pe.wait_ge(q["rx_ready"], 2 * (i + 1))
                for c in range(2):
                    n = 2 * i + c
                    pe.wait_ge(q["fc_ready"], n + 1)
                    pe.wait_ge(q["state_zeroed"], 1)
                    if n:
                        pe.wait_ge(q["state_ready"], n)
                    if n < NCH - 1:
                        o = begin(f"st{i}{c}")
                        for h in range(RH):
                            m, p = h // 2, h % 2
                            rows = slice(64 * p, 64 * p + 64)
                            last = pe.matmul(o[rows, m * DH:(m + 1) * DH], fc[rows, c, m, 0, :], state[rows, n % 2, m, :],
                                             start=True, stop=True)
                        end(last, f"st{i}{c}")
                    for p in range(2):
                        rows = slice(64 * p, 64 * p + 64)
                        for m in range(4):
                            last = pe.matmul(ybank[p][64 * c:64 * c + 64, m * DH:(m + 1) * DH],
                                             ar[rows, m, i, 1, 64 * c:64 * c + 64], state[rows, n % 2, m, :],
                                             start=False, stop=True, skip_group_check=True)
                        if c == 1:
                            end(last, f"y{i}{p}")
                pe.wait_ge(q["ynorm_ready"], i + 1)
                o = begin(f"yT{i}")
                for m in range(4):
                    last = pe.transpose(o[:, m * P:(m + 1) * P], ynorm[:, m * P:(m + 1) * P], ident)
                end(last, f"yT{i}")
                pe.wait_ge(q["lora_g_ready"], 1)
                o = begin(f"gup{i}")
                for m in range(4):
                    last = pe.matmul(o[:, m * P:(m + 1) * P], pr("g_up", 96)[:, m * P:(m + 1) * P], mix[0:96, 13, ts],
                                     start=True, stop=True)
                end(last, f"gup{i}")

            pe.wait_ge(q["pool_out"], 2)
            pe.wait_ge(q["nsa_ready"], NG)
            pe.wait_ge(q["yrw_ready"], NT)
            for n in range(4):
                for b in range(3):
                    project(f"mg{n}{b}", C_MERGE + 5 * n + b)
                for c in range(2):
                    w = chunk(C_MERGE + 5 * n + 3 + c).rearrange("p (k c) -> p k c", k=KD)
                    for b in ((0, 1) if c == 0 else (2,)):
                        o = begin(f"mb{n}{b}")
                        k0, nk = ((0, 4), (4, 4), (0, 8))[b]
                        for m in range(2):
                            for k in range(nk):
                                last = mm(o[:, m * S:(m + 1) * S], w[:, k0 + k, m * P:(m + 1) * P],
                                          yT[:, 8 * c + k0 + k, :], k, nk)
                        end(last, f"mb{n}{b}")
                    pe_take()
            pe.wait_ge(q["merged_ready"], 4)
            for n in range(4):
                w = chunk(C_OUT + n).rearrange("p (k c) -> p k c", k=KD)
                o = begin(f"out{n}")
                for i in range(NT):
                    for k in range(KD):
                        last = mm(o[:, i * 256:(i + 1) * 256], merged[:, k, i * P:(i + 1) * P], w[:, k, :], k, KD)
                end(last, f"out{n}")
                pe_take()

            for n in range(4):
                i = n // 2
                pe.wait_ge(q["xn_ready"], 2 + i + 1)
                o = begin(f"hT2{n}")
                for k in range(4):
                    kk = (n % 2) * 4 + k
                    last = first(pe.transpose(o[:, k * P:(k + 1) * P], xn[:, i, kk * P:(kk + 1) * P], ident))
                end(last, f"hT2{n}")
            pe.wait_ge(q["hT_ready"], 8)
            w = chunk(C_ROUTER)[:, 0:8 * 36].rearrange("p (k c) -> p k c", k=KD)
            o = begin("router")
            for i in range(NT):
                oo = o[:, i * 36:(i + 1) * 36]
                for k in range(KD):
                    pe.matmul(oo, hT[:, k, i * P:(i + 1) * P], w[:, k, :], start=(k == 0), stop=False)
                last = pe.matmul(oo, cn("ones", 1), pr("b_router", 1), start=False, stop=True)
            end(last, "router")
            full(pe, "router")
            pe.sem_inc(taken, 1)
            pe.wait_ge(q["member_ready"], 1)
            o = begin("places")
            pe.matmul(o[:, 0:E], cn("earlier"), member[:, 0, :], start=True, stop=True)
            pe.matmul(o[:, E:2 * E], cn("ones"), member[:, 0, :], start=True, stop=False)
            pe.matmul(o[:, E:2 * E], cn("earlier"), member[:, 1, :], start=False, stop=True)
            pe.matmul(o[:, 2 * E:3 * E], cn("ones"), member[:, 0, :], start=True, stop=False)
            end(pe.matmul(o[:, 2 * E:3 * E], cn("ones"), member[:, 1, :], start=False, stop=True), "places")

            pe.wait_ge(q["crowd_ready"], 1)
            most = pe.value_load(crowd[0:1, 0:1], min_val=0, max_val=S)

            def gathered_experts():
                with pe.Fori(0, NGANG) as gang:
                    pe.wait_ge(q["sel_ready"], gang + 1)
                    for b in range(2):
                        if b == 0:
                            for j in range(8):
                                pe.wait_ge(bank_free[j], before_loop[j])
                        for kk in range(4):
                            k = 4 * b + kk
                            for i in range(NT):
                                last = pe.matmul(bank[b][:, kk * P:(kk + 1) * P], xn[:, i, k * P:(k + 1) * P],
                                                 sel[:, i, :], start=(i == 0), stop=(i == 1))
                        last.then_inc(q["gathered"], 1)
                    for i in range(NT):
                        last = pe.transpose(bank[3][:, (2 + i) * P:(3 + i) * P], wsel[:, i, :], ident)
                    last.then_inc(q["wsel_turned"], 1)
                    for k in range(KD):
                        pe.wait_ge(loaded[k], gang * 16 + 16 * ((NFRONT // FRING if k < FRING else 0) + 1))
                        if k % 4 == 0:
                            pe.wait_ge(q["gath_ready"], gang * 2 + (k // 4 + 1))
                        w = ring[:, k * SLOT:(k + 1) * SLOT].rearrange("p (e n) -> p e n", e=GANG)
                        for e in range(GANG):
                            last = pe.matmul(bank[2][CAP * e:CAP * (e + 1), :], gath[:, k, CAP * e:CAP * (e + 1)],
                                             w[:, e, :], start=(k == 0), stop=(k == KD - 1))
                            if k and e == 0:
                                last.then_inc(taken, 1)
                    last.then_inc(q["gate_up"], 1)
                    pe.wait_ge(q["ghid_ready"], gang + 1)
                    pe.wait_ge(q["wselT_ready"], gang + 1)
                    for f in range(2):
                        last = pe.transpose(bank[3][:, f * P:(f + 1) * P], ghid[:, f * P:(f + 1) * P], ident)
                        if f == 0:
                            last.then_inc(taken, 1)
                    last.then_inc(q["hid_turned"], 1)
                    for e in range(GANG):
                        pe.wait_ge(loaded[8 + e], gang * 16 + 16)
                    pe.wait_ge(q["ghidT_ready"], gang + 1)
                    for n in range(2):
                        for f in range(2):
                            for e in range(GANG):
                                w = ring[:, (8 + e) * SLOT:(9 + e) * SLOT].rearrange("p (f d) -> p f d", f=2)
                                last = pe.matmul(bank[4 + n][CAP * e:CAP * (e + 1), :], ghidT[:, f, CAP * e:CAP * (e + 1)],
                                                 w[:, f, n * 512:(n + 1) * 512], start=(f == 0), stop=(f == 1))
                        last.then_inc(q["downed"], 1)
                    for j in range(4):
                        n, i = j // 2, j % 2
                        if i == 0:
                            pe.wait_ge(q["ydown_ready"], gang * 2 + n + 1)
                        if j >= 2:
                            pe.wait_ge(q["summed"], gang * 4 + (j - 1))
                        last = pe.matmul(bank[6 + i][:, :], wselT[:, i, :], ydown[:, n * 512:(n + 1) * 512],
                                         start=True, stop=True)
                        last.then_inc(q["scattered"], 1)
                    pe.wait_ge(q["scattered"], gang * 4 + 4)
                    pe.sem_inc(taken, 4)
                    pe.wait_ge(q["summed"], gang * 4 + 4)

            def dense_experts():
                with pe.Fori(0, NGANG) as gang:
                    for c in range(GCH):
                        first = NFRONT // FRING if c < FRING else 0
                        pe.wait_ge(loaded[c], gang * 16 + 16 * (first + 1))
                    for i in range(NT):
                        slot = [ring[:, c * SLOT:(c + 1) * SLOT].rearrange("p (e n) -> p e n", e=GANG) for c in range(8)]
                        for e in range(GANG):
                            pe.wait_ge(bank_free[e], gang * 2 + (before_loop[e] + i))
                            for k in range(KD):
                                last = pe.matmul(bank[e][:, :], hT[:, k, i * P:(i + 1) * P], slot[k][:, e, :],
                                                 start=(k == 0), stop=(k == KD - 1))
                            last.then_inc(bank_full[e], 1)
                        for half in range(2):
                            pe.wait_ge(q["hid_ready"], gang * 8 + (4 * i + 2 * half + 2))
                            pe.wait_ge(bank_free[4 + half], gang * 2 + (before_loop[4 + half] + i))
                            for e in range(2):
                                for f in range(2):
                                    last = pe.transpose(bank[4 + half][:, (2 * e + f) * P:(2 * e + f + 1) * P],
                                                        hid[:, 2 * half + e, f * P:(f + 1) * P], ident)
                            last.then_inc(bank_full[4 + half], 1)
                        pe.wait_ge(q["hidT2_ready"], gang * 4 + (2 * i + 2))
                        for n in range(2):
                            pe.wait_ge(bank_free[6 + n], gang * 2 + (before_loop[6 + n] + i))
                            for e in range(GANG):
                                down = ring[:, (8 + e) * SLOT:(9 + e) * SLOT].rearrange("p (f d) -> p f d", f=2)
                                for f in range(2):
                                    last = pe.matmul(bank[6 + n][:, :], hidm[:, e, f, :], down[:, f, n * 512:(n + 1) * 512],
                                                     start=(e == 0 and f == 0), stop=(e == GANG - 1 and f == 1))
                            last.then_inc(bank_full[6 + n], 1)
                    pe.wait_ge(bank_full[7], gang * 2 + (before_loop[7] + 2))
                    pe.sem_inc(taken, GCH)

            with pe.If(most <= CAP):
                gathered_experts()
            with pe.Else():
                dense_experts()

        @block.gpsimd
        def _(pool):
            pool.memset(rawf[:, :], 0.0).then_inc(q["raw_zeroed"], 1)
            pool.memset(state[:, 0, :, :], 0.0).then_inc(q["state_zeroed"], 1)
            pool.wait_ge(q["small_loaded"], 32)

            def inverse_root(n, width):
                pool.wait_ge(q["rms_in"], n + 1)
                pool.tensor_tensor(stat[:, 8:8 + width], stat[:, 0:width], cn("neghalf")[:, 0:width], ALU.pow)\
                    .then_inc(q["root_ready"], 1)

            inverse_root(0, 2)
            level = cn("level").rearrange("p (n t) -> p n t", n=6)
            for i in range(NT):
                for grp in range(2):
                    turn_ = 2 * i + grp
                    for n in range(6):
                        if n == 0:
                            pool.wait_ge(q["amat_ready"], 8 * (i + 1))
                            if grp:
                                full(pool, f"W{i}{grp - 1}4")
                        elif n == 1:
                            pool.wait_ge(q["z_ready"], 6 * turn_ + 1)
                        else:
                            full(pool, f"W{i}{grp}{n - 2}")
                        pool.tensor_tensor(lmask, amat[:, 4 * grp:4 * grp + 4, 0, :],
                                           like(level[:, n:n + 1, :], [P, 4, P]), ALU.mult)\
                            .then_inc(q["lmask_ready"], 1)
                inverse_root(1 + i, 8)
            inverse_root(3, 2)
            inverse_root(4, 2)

        @block.scalar
        def _(act):
            def copy(o, i_, scale=1.0):
                return act.activation(o, i_, ACT.Copy, scale=scale)

            def flat(o):
                return o[:, :].rearrange("p (a t) -> p a t", a=2)

            count = {}

            def give(ins, name, job):
                count[name] = count.get(name, 0) + 1
                ins.then_inc(q[name], 1)
                act.wait_ge(q[name], count[name])
                act.sem_inc(bank_free[plan[job][0]], 1)

            act.wait_ge(q["small_loaded"], 32)
            act.wait_ge(q["raw_zeroed"], 1)
            b0 = full(act, "lora_in")
            copy(raw[0:64, 0, 0, 1:S + 1], b0[0:64, 0:S])
            ins = copy(raw[0:96, 0, 1, 1:S + 1], b0[0:96, S:2 * S])
            give(ins, "raw_ready", "lora_in")
            b0 = full(act, "gates")
            give(act.activation(gate_t[:, :, :].rearrange("p i n -> p (i n)"), b0[:, 0:96], ACT.Tanh, scale=0.5), "gate_tanh", "gates")
            for c in range(1, 7):
                if c >= 2:
                    act.wait_ge(q["raw_used"], c - 1)
                b0 = full(act, f"rkv{c}")
                give(copy(raw[:, c % 2, :, 1:S + 1], flat(b0)), "raw_ready", f"rkv{c}")
                if c == 2:
                    act.wait_ge(q["mix_ready"], 1)
                    act.activation(mix[0:32, 12, :], mix[0:32, 12, :], ACT.Tanh).then_inc(q["lora_w_ready"], 1)
                    act.activation(mix[0:96, 13, :], mix[0:96, 13, :], ACT.Tanh, scale=0.5)\
                        .then_inc(q["lora_g_tanh"], 1)
            for b, name in enumerate(("kc", "vc")):
                b0 = full(act, name)
                for gp in range(2):
                    src = flat(b0[64 * gp:64 * gp + 64, :])
                    copy(kshift[0:64, b, gp::2, :], src)
                    ins = copy(kshift[64:128, b, gp::2, 0:S - 1], src[:, :, 1:S])
                give(ins, "kshift_ready", name)
            for n in range(8):
                b0 = full(act, f"bias{n}")
                give(copy(bias[:, 2 * n:2 * n + 2, :], flat(b0)), "bias_ready", f"bias{n}")
            for n in range(4):
                b0 = full(act, f"q{n}")
                give(copy(qT[:, 2 * n:2 * n + 2, :], flat(b0), scale=DH ** -0.5), "q_ready", f"q{n}")
            for b, name in enumerate(("ks", "kw")):
                b0 = full(act, name)
                for gp in range(2):
                    src = flat(b0[64 * gp:64 * gp + 64, :])
                    copy(kT[0:64, b, gp::2, :], src)
                    ins = copy(kT[64:128, b, gp::2, :], src)
                give(ins, "k_ready", name)
            for b, name in enumerate(("vs", "vw")):
                b0 = full(act, name)
                give(copy(vtok[:, b, :, :], flat(b0)), "v_ready", name)
            for n in range(2):
                b0 = full(act, f"pool{n}")
                give(copy(t1[:, 2 * n:2 * n + 2, :], flat(b0)), "u_ready", f"pool{n}")
            for b, name in enumerate(("mlp_k", "mlp_v")):
                b0 = full(act, name)
                give(copy(gx[:, b * 256:(b + 1) * 256], b0[0:60, 0:256]), "gx_ready", name)
            act.wait_ge(q["gelu_in"], 1)
            act.activation(gy, gy, ACT.Tanh, scale=GELU_C).then_inc(q["gelu_tanh"], 1)
            act.wait_ge(q["halves_ready"], 1)
            act.wait_ge(q["pool_ready"], 1)
            for n in range(2):
                b0 = full(act, f"wup{n}")
                for m in range(2):
                    c = 2 * n + m
                    ins = act.activation(t1[:, c, :], b0[:, m * S:(m + 1) * S], ACT.Tanh, bias=halves[:, c:c + 1], scale=0.5)
                give(ins, "decay_tanh", f"wup{n}")
            for n in range(2):
                b0 = full(act, f"aup{n}")
                for m in range(2):
                    c = 2 * n + m
                    ins = act.activation(kf[:, c, :], b0[:, m * S:(m + 1) * S], ACT.Tanh, bias=halves[:, 4 + c:5 + c],
                                         scale=0.5)
                give(ins, "rate_tanh", f"aup{n}")
            act.wait_ge(q["kk_max"], 2)
            act.activation(t3[:, :, :], t3[:, :, :], ACT.Sqrt).then_inc(q["kk_root"], 1)
            b0 = full(act, "hidT")
            give(copy(hidT, b0[:, 0:240].rearrange("p (f n) -> p f n", f=4)), "hidT_ready", "hidT")
            b0 = full(act, "kcb")
            give(copy(kcb, b0[:, 0:60]), "cmp_kv_ready", "kcb")
            b0 = full(act, "vcb")
            give(copy(vcb, b0[0:NCMP, 0:256].rearrange("p (g v) -> p g v", g=NG)), "cmp_kv_ready", "vcb")
            act.wait_ge(q["log_ready"], 1)
            act.activation(t3[:, :, :], t2[:, :, :], ACT.Exp).then_inc(q["decay_exp"], 1)
            act.wait_ge(q["log_ready"], 2)
            act.activation(t1[:, :, :], t1[:, :, :], ACT.Exp).then_inc(q["decay_exp"], 1)
            act.activation(t2[:, :, :], t2[:, :, :], ACT.Exp, scale=-1.0).then_inc(q["decay_exp"], 1)

            for u in range(4):
                nc_ = 7 if u < 2 else NCMP
                act.wait_ge(q["cexp_in"], u + 1)
                act.activation(cprob[:, u, :, 0:nc_], cprob[:, u, :, 0:nc_], ACT.Exp).then_inc(q["cexp_ready"], 1)

            def exps(g, u):
                n = 6 * g + u
                act.wait_ge(q["exp_in"], n + 1)
                nb, w = (4, P) if u < 2 else (2, S)
                for b in range(nb):
                    pb = prob[:, n % 2, b * w:(b + 1) * w]
                    ins = act.activation(pb, pb, ACT.Exp, bias=astat[:, 8 * (n % 2) + b:8 * (n % 2) + b + 1],
                                         accum_out=astat[:, 16 + 8 * (n % 2) + b:17 + 8 * (n % 2) + b])
                ins.then_inc(q["exp_ready"], 1)

            for g in range(NG):
                for i in range(NT):
                    nc_ = 7 if i == 0 else NCMP
                    b0 = full(act, f"cT{g}{i}")
                    give(copy(cprobT[0:nc_, i, :, :], b0[0:nc_, :].rearrange("p (h t) -> p h t", h=4)), "cprobT_ready", f"cT{g}{i}")
                exps(g, 0)
                for u in range(6):
                    if u < 5:
                        exps(g, u + 1)
                    n = 6 * g + u
                    b0 = full(act, f"pT{g}{u}")
                    give(copy(probT[:, n % 2, :], b0[:, :]), "probT_ready", f"pT{g}{u}")

            act.wait_ge(q["nsa_ready"], NG)
            act.dma_start(tok[:, :, :], x.rearrange("(i p) d -> p i d", p=P)).then_inc(q["x_again"], 16)

            for i in range(NT):
                for w_, dst in enumerate((btok, ktok, vrow)):
                    b0 = full(act, f"tok{i}{w_}")
                    give(copy(dst, b0[:, :]), "tok_ready", f"tok{i}{w_}")
                b0 = full(act, f"atok{i}")
                give(copy(rhs[:, :, 0, :], b0[:, :].rearrange("p (h v) -> p h v", h=RH)), "tok_ready", f"atok{i}")
                for grp in range(2):
                    for n in range(5):
                        b0 = full(act, f"W{i}{grp}{n}")
                        give(copy(winv, b0[:, :].rearrange("p (h t) -> p h t", h=4)), "w_ready", f"W{i}{grp}{n}")
                b0 = full(act, f"w0{i}")
                give(copy(rhs[:, :, 1, :], b0[:, :].rearrange("p (h v) -> p h v", h=RH)), "rhs_ready", f"w0{i}")
                for n in range(2):
                    b0 = full(act, f"xu{i}{n}")
                    give(copy(rhs[:, 4 * n:4 * n + 4, :, :], b0[:, :].rearrange("p (h j v) -> p h j v", h=4, j=2)), "xu_ready", f"xu{i}{n}")
                b0 = full(act, f"yT{i}")
                for m in range(4):
                    ins = act.activation(yT[:, 4 + m, i * P:(i + 1) * P], b0[:, m * P:(m + 1) * P], ACT.Identity,
                                         bias=pr("gn_b")[:, m:m + 1], scale=pr("gn_w")[:, m:m + 1])
                give(ins, "gn_ready", f"yT{i}")

            act.wait_ge(q["yrw_ready"], NT)
            for s in range(FRING, GCH):
                act.dma_start(ring[:, s * SLOT:(s + 1) * SLOT], experts[0, s]).then_inc(loaded[s], 16)

            for n in range(4):
                for b in range(3):
                    if n:
                        act.wait_ge(q["gated"], 3 * (n - 1) + b + 1)
                    b0 = full(act, f"mg{n}{b}")
                    for m in range(2):
                        c = 8 + 8 * b + 2 * n + m
                        ins = act.activation(gsig[b][:, m, :], b0[:, m * S:(m + 1) * S], ACT.Tanh,
                                             bias=halves[:, c:c + 1], scale=0.5)
                    give(ins, "gsig_ready", f"mg{n}{b}")

            act.wait_ge(q["merged_ready"], 4)
            act.dma_start(gfin, g_final).then_inc(q["gfin_loaded"], 16)

            act.wait_ge(q["router_in"], 1)
            act.activation(rt("ge"), rt("ge"), ACT.Exp).then_inc(q["router_exp"], 1)
            act.wait_ge(q["router_in"], 2)
            act.activation(rt("w2"), rt("w2"), ACT.Exp).then_inc(q["router_exp"], 1)

            act.wait_ge(q["crowd_ready"], 1)
            most = act.value_load(crowd[0:1, 0:1], min_val=0, max_val=S)

            def gathered_experts():
                with act.Fori(0, NGANG) as gang:
                    act.wait_ge(q["wsel_turned"], gang + 1)
                    copy(wselT, bank[3][:, 2 * P:4 * P].rearrange("p (i t) -> p i t", i=2)).then_inc(q["wselT_ready"], 1)
                    act.wait_ge(q["gate_up"], gang + 1)
                    act.activation(gtanh, bank[2][:, 0:DE], ACT.Tanh, scale=0.5).then_inc(q["gtanh_ready"], 1)
                    act.wait_ge(q["hid_turned"], gang + 1)
                    copy(ghidT, bank[3][:, 0:2 * P].rearrange("p (f s) -> p f s", f=2)).then_inc(q["ghidT_ready"], 1)
                    for n in range(2):
                        act.wait_ge(q["downed"], gang * 2 + n + 1)
                        copy(ydown[:, n * 512:(n + 1) * 512], bank[4 + n][:, :]).then_inc(q["ydown_ready"], 1)

            def dense_experts():
                with act.Fori(0, NGANG) as gang:
                    for i in range(NT):
                        for e in range(GANG):
                            act.wait_ge(bank_full[e], gang * 2 + (before_loop[e] + i + 1))
                            act.activation(gsi[:, e, :], bank[e][:, 0:DE], ACT.Tanh, scale=0.5).then_inc(q["silu_tanh"], 1)
                        for half in range(2):
                            act.wait_ge(bank_full[4 + half], gang * 2 + (before_loop[4 + half] + i + 1))
                            copy(hidm[:, 2 * half:2 * half + 2, :, :],
                                 bank[4 + half][:, :].rearrange("p (e f t) -> p e f t", e=2, f=2))\
                                .then_inc(q["hidT2_ready"], 1)

            with act.If(most <= CAP):
                gathered_experts()
            with act.Else():
                dense_experts()

        @block.vector
        def _(dve):
            chain = chainer(dve, "dve_chain")

            def flat(o):
                return o[:, :].rearrange("p (a t) -> p a t", a=2)

            def tt(o, a, b, op):
                return dve.tensor_tensor(o, a, b, op)

            def ts(o, a, s1, s2, op0, op1=None):
                return dve.tensor_scalar(o, a, s1, s2, op0, op1) if op1 is not None else \
                    dve.tensor_scalar(o, a, s1, None, op0)

            def stt(o, a, s1, b, op0, op1):
                return dve.scalar_tensor_tensor(out=o, in0=a, scalar=s1, in1=b, op0=op0, op1=op1)

            roots = [0]

            def normalise(src):
                for i in range(NT):
                    chain(dve.tensor_tensor_reduce(t1[:, :, :].rearrange("p c t -> p (c t)"), src[:, i, :], src[:, i, :],
                                                   1.0, 0.0, ALU.mult, ALU.add, stat[:, 16 + i:17 + i]))
                roots[0] += 1
                chain(ts(stat[:, 0:2], stat[:, 16:18], 1.0 / D, 1e-6, ALU.mult, ALU.add), "rms_in")
                dve.wait_ge(q["root_ready"], roots[0])
                for i in range(NT):
                    chain(ts(xn[:, i, :], src[:, i, :], stat[:, 8 + i:9 + i], None, ALU.mult), "xn_ready")

            def to_hT(jobs, gain):
                for n in range(4):
                    i, k0 = n // 2, (n % 2) * 4
                    b0 = full(dve, f"{jobs}{n}")
                    chain(tt(hT[:, k0:k0 + 4, i * P:(i + 1) * P], b0[:, :].rearrange("p (k t) -> p k t", k=4),
                             like(pr(gain)[:, k0:k0 + 4, None], [P, 4, P]), ALU.mult), "hT_ready")
                    dve.sem_inc(bank_free[plan[f"{jobs}{n}"][0]], 1)

            dve.wait_ge(q["x_loaded"], 16)
            dve.wait_ge(q["small_loaded"], 32)
            for lo, hi, name in ((0, 4, "w0"), (4, 8, "a0"), (8, 32, "b_merge")):
                ins = ts(halves[:, lo:hi], pr(name), 0.5, None, ALU.mult)
                chain(ins, "halves_ready" if name == "b_merge" else None)
            normalise(tok)
            to_hT("xT", "g_mix")
            b0 = full(dve, "brow")
            ins = dve.tensor_copy(arbk[0:NH, 0:2, :].rearrange("p a b -> p (a b)")[:, 0:384], b0[0:NH, 0:384])
            chain(ins, "win_row")
            dve.sem_inc(bank_free[plan["brow"][0]], 1)

            def shift(rows, c, j, tiles):
                r_ = raw[rows, c % 2, j, :]
                chain(tt(mix[rows, tiles, :], r_[:, :, 0:S], r_[:, :, 1:S + 1], ALU.subtract))
                for k in range(tiles.stop - tiles.start):
                    t = tiles.start + k
                    chain(stt(mix[rows, t, :], mix[rows, t, :], pr("mu")[rows, t:t + 1], r_[:, k, 1:S + 1],
                              ALU.mult, ALU.add))

            dve.wait_ge(q["raw_ready"], 1)
            shift(slice(0, 64), 0, slice(0, 1), slice(12, 13))
            shift(slice(0, 96), 0, slice(1, 2), slice(13, 14))
            dve.sem_inc(q["raw_used"], 1)
            dve.sem_inc(q["mix_ready"], 1)
            dve.wait_ge(q["gate_tanh"], 1)
            ins = ts(gate_t[:, :, :].rearrange("p i n -> p (i n)"), gate_t[:, :, :].rearrange("p i n -> p (i n)"),
                     0.5, 0.5, ALU.mult, ALU.add)
            free_after = chain(ins, "gates_ready")
            for c in range(1, 7):
                dve.wait_ge(q["raw_ready"], c + 1)
                shift(slice(0, P), c, slice(0, 2), slice(2 * c - 2, 2 * c))
                dve.sem_inc(q["raw_used"], 1)
            dve.wait_ge(q["lora_g_tanh"], 1)
            chain(ts(mix[0:96, 13, :], mix[0:96, 13, :], 0.5, 0.5, ALU.mult, ALU.add), "lora_g_ready")

            for b, name in enumerate(("kc", "vc")):
                dve.wait_ge(q["kshift_ready"], b + 1)
                base = kshift[:, b, :, :]
                src = bass.AP(base.tensor, base.offset, [list(base.ap[0]), [2, 16], [S, NG], [CSTRIDE, NCMP]])
                pos = pr("pos_k" if b == 0 else "pos_v")
                chain(tt(xcmp[:, b, :, :].rearrange("p j (g n) -> p j g n", g=NG), src,
                         like(pos[:, :, None, None], [P, 16, NG, NCMP]), ALU.add), "xcmp_ready")
            dve.wait_ge(q["u_ready"], 2)

            sums = [None, t2, t3, t2, t3]
            for lv in range(1, 5):
                w = 2 ** (lv - 1)
                src, dst = (t1 if lv == 1 else sums[lv - 1]), sums[lv]
                gs = slice(lv - 1, 4)
                chain(dve.tensor_copy(dst[:, gs, 0:w], src[:, gs, 0:w]), hold=False)
                chain(tt(dst[:, gs, w:S], src[:, gs, w:S], src[:, gs, 0:S - w], ALU.add))
            cnt = cn("count").rearrange("p (g t) -> p g t", g=4)
            for gi in range(4):
                src = sums[gi + 1]
                chain(stt(yT[:, gi, :], src[:, gi, :], 0.5 ** (gi + 1), t1[:, gi, :], ALU.mult, ALU.subtract))
                chain(tt(src[:, gi, 0:16], src[:, gi, 0:16], cnt[:, gi, :], ALU.mult))
                ins = tt(yT[:, gi, 0:16], src[:, gi, 0:16], t1[:, gi, 0:16], ALU.subtract)
                chain(ins, "pool_ready" if gi == 3 else None)

            for m in range(4):
                chain(ts(bf[:, m, :], mix[:, m, :], pr("k_k")[:, m:m + 1], None, ALU.mult), hold=(m == 3))
            chain(tt(t3[:, :, :], bf, bf, ALU.mult), "kk_sq_ready")

            dve.wait_ge(q["gx_ready"], 2)
            chain(tt(gy, gx, gx, ALU.mult))
            chain(ts(gy, gy, 0.044715, 1.0, ALU.mult, ALU.add))
            chain(tt(gy, gy, gx, ALU.mult), "gelu_in")
            dve.wait_ge(q["gelu_tanh"], 1)
            chain(stt(gy, gy, 1.0, gx, ALU.add, ALU.mult))
            chain(ts(gx, gy, 0.5, None, ALU.mult), "gelu_ready")

            dve.wait_ge(q["decay_tanh"], 2)
            chain(ts(t1[:, :, :], t1[:, :, :], 1.0, -0.5 * DECAY, ALU.add, ALU.mult))
            dve.wait_ge(q["rate_tanh"], 2)
            for m in range(4):
                for c in range(NCH):
                    cs = slice(c * CH, (c + 1) * CH)
                    chain(dve.tensor_tensor_scan(t2[:, m, cs], cn("ones")[:, 0:CH], t1[:, m, cs], 0.0, ALU.mult, ALU.add),
                          hold=(m == 3 and c == 3))
            for n in range(2):
                b0 = full(dve, f"kk{n}")
                ins = ts(t3[:, 2 * n:2 * n + 2, :], flat(b0), 1e-24, None, ALU.max)
                chain(ins, "kk_max")
                dve.sem_inc(bank_free[plan[f"kk{n}"][0]], 1)
            dve.wait_ge(q["kk_root"], 1)
            chain(dve.reciprocal(t3[:, :, :], t3[:, :, :]))
            chain(tt(bf, bf, t3[:, :, :], ALU.mult))
            dve.sem_inc(q["log_ready"], 1)
            for n in range(2):
                b0 = full(dve, f"poolmix{n}")
                chain(tt(yT[:, 2 * n:2 * n + 2, :], flat(b0),
                         like(pr("pool_scale")[:, 2 * n:2 * n + 2, None], [P, 2, S]), ALU.mult), "pool_out")
                dve.sem_inc(bank_free[plan[f"poolmix{n}"][0]], 1)
            chain(tt(t1[:, :, :], t2[:, :, :], t1[:, :, :], ALU.subtract), "log_ready") if False else None
            ins = tt(t1[:, :, :], t2[:, :, :], t1[:, :, :], ALU.subtract)
            chain(ins)
            dve.sem_inc(q["log_ready"], 1)
            chain(ts(kf, kf, 0.5, 0.5, ALU.mult, ALU.add))
            dve.wait_ge(q["decay_exp"], 3)
            a_f = ar[:, :, :, 0, :]
            r_f = ar[:, :, :, 1, :]

            def tiles(t):
                return t.rearrange("p m (i t) -> p m i t", i=2)

            chain(stt(a_f.rearrange("p m i t -> p (m i) t"), bf.rearrange("p m (i t) -> p (m i) t", i=2), -1.0,
                      t1[:, :, :].rearrange("p m (i t) -> p (m i) t", i=2), ALU.mult, ALU.mult), hold=False)
            chain(tt(r_f.rearrange("p m i t -> p (m i) t"), mix[:, 4:8, :].rearrange("p m (i t) -> p (m i) t", i=2),
                     t3[:, :, :].rearrange("p m (i t) -> p (m i) t", i=2), ALU.mult))
            chain(dve.tensor_copy(pend, t3[:, :, :].rearrange("p m (c t) -> p m c t", c=NCH)[:, :, :, CH - 1]))
            chain(tt(bf, bf, kf, ALU.mult))
            chain(tt(bf, bf, t2[:, :, :], ALU.mult))
            for m in range(4):
                chain(ts(kf[:, m, :], kf[:, m, :], -1.0, pr("k_a")[:, m:m + 1], ALU.add, ALU.mult), hold=(m == 3))
            chain(stt(kf, kf, 1.0, mix[:, 0:4, :], ALU.add, ALU.mult))
            for m in range(4):
                ins = stt(mix[:, 4 + m, :], mix[:, 4 + m, :], pr("r_k")[:, m:m + 1], kf[:, m, :], ALU.mult, ALU.mult)
                chain(ins, "bonus_ready" if m == 3 else None)
            chain(tt(kf, kf, t2[:, :, :], ALU.mult), "rwkv_ready")
            for n in range(2):
                b0 = full(dve, f"bonus{n}")
                chain(tt(mix[:, 4 + 2 * n:6 + 2 * n, :], flat(b0), mix[:, 8 + 2 * n:10 + 2 * n, :], ALU.mult))
                dve.sem_inc(bank_free[plan[f"bonus{n}"][0]], 1)

            for u in range(4):
                i, p = u // 2, u % 2
                nc_ = 7 if i == 0 else NCMP
                b0 = full(dve, f"cs{u}")
                cp = cprob[:, u, :, 0:nc_]
                first = CBLOCK - 1 + (P if i == 0 else 0)
                chain(tt(cp, b0[:, 0:8 * nc_].rearrange("p (m n) -> p m n", m=8),
                         bias[:, p::2, first:first + CSTRIDE * (nc_ - 1) + 1:CSTRIDE], ALU.add))
                dve.sem_inc(bank_free[plan[f"cs{u}"][0]], 1)
                mx = astat[:, 32:40]
                chain(dve.tensor_reduce(mx, cp, AXX, ALU.max))
                chain(ts(mx, mx, -1.0e20, None, ALU.max))
                chain(tt(cp, cp, like(mx[:, :, None], [P, 8, nc_]), ALU.subtract), "cexp_in")
            for u in range(4):
                i, p = u // 2, u % 2
                nc_ = 7 if i == 0 else NCMP
                cp = cprob[:, u, :, 0:nc_]
                dve.wait_ge(q["cexp_ready"], u + 1)
                sm = astat[:, 32:40]
                chain(dve.tensor_reduce(sm, cp, AXX, ALU.add))
                chain(ts(sm, sm, 1e-30, None, ALU.max))
                chain(dve.reciprocal(sm, sm))
                chain(tt(sm, sm, gate_t[:, i, 3 * p::6], ALU.mult))
                chain(tt(cp, cp, like(sm[:, :, None], [P, 8, nc_]), ALU.mult), "cprob_ready")

            def logits(g, u):
                n = 6 * g + u
                p = u % 2
                b0 = full(dve, f"s{g}{u}")
                if n >= 2:
                    b, cnt_ = plan[f"pT{(n - 2) // 6}{(n - 2) % 6}"]
                    dve.wait_ge(bank_full[b], cnt_ + 1)
                h0 = 4 * g + p
                if u < 2:
                    for br in range(2):
                        o = prob[:, n % 2, br * 256:(br + 1) * 256].rearrange("p (h k) -> p h k", h=2)
                        chain(tt(o, b0[:, br * 256:(br + 1) * 256].rearrange("p (h k) -> p h k", h=2),
                                 bias[:, h0:h0 + 3:2, P:2 * P], ALU.add), hold=(br == 1))
                    nb, w = 4, P
                else:
                    o = prob[:, n % 2, :].rearrange("p (h k) -> p h k", h=2)
                    chain(tt(o, b0[:, :].rearrange("p (h k) -> p h k", h=2), bias[:, h0:h0 + 3:2, :], ALU.add))
                    nb, w = 2, S
                dve.sem_inc(bank_free[plan[f"s{g}{u}"][0]], 1)
                mx = astat[:, 8 * (n % 2):8 * (n % 2) + nb]
                chain(dve.tensor_reduce(mx, prob[:, n % 2, :].rearrange("p (b k) -> p b k", b=nb), AXX, ALU.max))
                chain(ts(mx, mx, -1.0, None, ALU.mult), "exp_in")

            def gated(g, u):
                n = 6 * g + u
                p = u % 2
                dve.wait_ge(q["exp_ready"], n + 1)
                nb, w = (4, P) if u < 2 else (2, S)
                sm = astat[:, 16 + 8 * (n % 2):16 + 8 * (n % 2) + nb]
                chain(dve.reciprocal(sm, sm))
                c0 = 12 * g + 3 * p + 1
                if u < 2:
                    for br in range(2):
                        chain(tt(sm[:, 2 * br:2 * br + 2], sm[:, 2 * br:2 * br + 2],
                                 gate_t[:, 0, c0 + br:c0 + br + 7:6], ALU.mult), hold=(br == 1))
                else:
                    br = (u - 2) // 2
                    chain(tt(sm, sm, gate_t[:, 1, c0 + br:c0 + br + 7:6], ALU.mult))
                pv = prob[:, n % 2, :].rearrange("p (b k) -> p b k", b=nb)
                chain(tt(pv, pv, like(sm[:, :, None], [P, nb, w]), ALU.mult), "prob_ready")

            for g in range(NG):
                logits(g, 0)
                for u in range(6):
                    if u < 5:
                        logits(g, u + 1)
                    gated(g, u)
                b0 = full(dve, f"o{g}")
                ins = dve.tensor_copy(yT[:, 8 + 2 * g:10 + 2 * g, :], flat(b0))
                chain(ins, "nsa_ready")
                dve.sem_inc(bank_free[plan[f"o{g}"][0]], 1)

            for i in range(NT):
                for h in range(RH):
                    b0 = full(dve, f"A{i}{h}")
                    chain(tt(amat[:, h, :, :].rearrange("p j t -> p (j t)"), b0[:, :], cn("intra"), ALU.mult), "amat_ready")
                    dve.sem_inc(bank_free[plan[f"A{i}{h}"][0]], 1)
                for grp in range(2):
                    z = zinv[grp]
                    turn_ = 2 * i + grp
                    dve.wait_ge(q["lmask_ready"], 6 * turn_ + 1)
                    chain(tt(z, lmask, like(ident[:, None, :], [P, 4, P]), ALU.add), "z_ready")
                    b0 = full(dve, f"XZ{i}{grp}")
                    chain(dve.tensor_copy(xinv, b0[:, :].rearrange("p (h t) -> p h t", h=4)), "x_ready")
                    dve.sem_inc(bank_free[plan[f"XZ{i}{grp}"][0]], 1)
                    for n in range(5):
                        if n < 4:
                            b0 = full(dve, f"X{i}{grp}{n}")
                            chain(tt(xinv, xinv, b0[:, :].rearrange("p (h t) -> p h t", h=4), ALU.add), "x_ready")
                            dve.sem_inc(bank_free[plan[f"X{i}{grp}{n}"][0]], 1)
                        b0 = full(dve, f"Z{i}{grp}{n}")
                        chain(tt(z, z, b0[:, :].rearrange("p (h t) -> p h t", h=4), ALU.add), "z_ready")
                        dve.sem_inc(bank_free[plan[f"Z{i}{grp}{n}"][0]], 1)
                for n in range(2):
                    b0 = full(dve, f"rx{i}{n}")
                    rv = ar[:, 2 * n:2 * n + 2, i, 1, :]
                    chain(tt(rv, rv, b0[:, 0:2 * P].rearrange("p (m t) -> p m t", m=2), ALU.add), "rx_ready")
                    dve.sem_inc(bank_free[plan[f"rx{i}{n}"][0]], 1)
                for c in range(2):
                    b0 = full(dve, f"fc{i}{c}")
                    bv = b0[:, :].rearrange("p (m j v) -> p m j v", m=4, j=2)
                    chain(tt(fc[:, c, :, 0, :], bv[:, :, 0, :], like(cn("eye64")[:, None, :], [P, 4, DH]), ALU.add), hold=False)
                    chain(dve.tensor_copy(fc[:, c, :, 1, :], bv[:, :, 1, :]), "fc_ready")
                    dve.sem_inc(bank_free[plan[f"fc{i}{c}"][0]], 1)
                for c in range(2):
                    n = 2 * i + c
                    if n == NCH - 1:
                        break
                    b0 = full(dve, f"st{i}{c}")
                    sv = state[:, (n + 1) % 2, :, :]
                    if n:
                        pass
                    chain(tt(fc[:, c, :, 1, :], b0[:, 0:4 * DH].rearrange("p (m v) -> p m v", m=4), fc[:, c, :, 1, :], ALU.add))
                    dve.sem_inc(bank_free[plan[f"st{i}{c}"][0]], 1)
                    chain(tt(sv, fc[:, c, :, 1, :], like(pend[:, :, n:n + 1], [P, 4, DH]), ALU.mult), "state_ready")
                yv = ynorm.rearrange("p (m j v) -> p m j v", m=4, j=2)
                for p in range(2):
                    b0 = full(dve, f"y{i}{p}")
                    chain(dve.tensor_copy(yv[:, :, p, :], b0[:, 0:4 * DH].rearrange("p (m v) -> p m v", m=4)))
                    dve.sem_inc(bank_free[plan[f"y{i}{p}"][0]], 1)
                yh = ynorm.rearrange("p (h v) -> p h v", h=RH)
                ys = ysq.rearrange("p (h v) -> p h v", h=RH)
                mean = stat[:, 16:24]
                chain(dve.tensor_reduce(mean, yh, AXX, ALU.add))
                chain(ts(mean, mean, 1.0 / DH, None, ALU.mult))
                chain(tt(yh, yh, like(mean[:, :, None], [P, RH, DH]), ALU.subtract))
                chain(tt(ys, yh, yh, ALU.mult))
                chain(dve.tensor_reduce(mean, ys, AXX, ALU.add))
                roots[0] += 1
                chain(ts(stat[:, 0:8], mean, 1.0 / DH, 64e-5, ALU.mult, ALU.add), "rms_in")
                dve.wait_ge(q["root_ready"], roots[0])
                chain(tt(yh, yh, like(stat[:, 8:16][:, :, None], [P, RH, DH]), ALU.mult), "ynorm_ready")
                dve.wait_ge(q["gn_ready"], i + 1)
                yr = yT[:, 4:8, i * P:(i + 1) * P]
                chain(tt(yr, yr, bonus[:, :, i * P:(i + 1) * P], ALU.add))
                b0 = full(dve, f"gup{i}")
                chain(tt(yr, yr, b0[:, :].rearrange("p (m t) -> p m t", m=4), ALU.mult), "yrw_ready")
                dve.sem_inc(bank_free[plan[f"gup{i}"][0]], 1)

            for n in range(4):
                for b in range(3):
                    dve.wait_ge(q["gsig_ready"], 3 * n + b + 1)
                    b0 = full(dve, f"mb{n}{b}")
                    o = macc if b == 0 else mtmp
                    chain(stt(o, gsig[b], 1.0, flat(b0), ALU.add, ALU.mult), "gated")
                    dve.sem_inc(bank_free[plan[f"mb{n}{b}"][0]], 1)
                    if b == 1:
                        chain(tt(macc, macc, mtmp, ALU.add))
                    if b == 2:
                        chain(tt(merged[:, 2 * n:2 * n + 2, :], macc, mtmp, ALU.add), "merged_ready")
            dve.wait_ge(q["x_again"], 16)
            for n in range(4):
                b0 = full(dve, f"out{n}")
                o = tok[:, :, n * 256:(n + 1) * 256]
                chain(stt(o, flat(b0), 0.5, o, ALU.mult, ALU.add))
                dve.sem_inc(bank_free[plan[f"out{n}"][0]], 1)
            normalise(tok)
            to_hT("hT2", "g_ffn")

            b0 = full(dve, "router")
            lg = rt("lg")
            chain(dve.tensor_copy(lg, b0[:, 0:72].rearrange("p (i n) -> p i n", i=2)))
            dve.sem_inc(bank_free[plan["router"][0]], 1)
            fall = cn("falling")

            def first_best(values, width, best, hot, tmp):
                shape = [P, 2, width]
                f = like(fall[:, None, 0:width], shape)
                chain(dve.tensor_reduce(best, values, AXX, ALU.max))
                chain(tt(hot, values, like(best[:, :, None], shape), ALU.is_equal))
                chain(tt(hot, hot, f, ALU.mult))
                chain(dve.tensor_reduce(tmp, hot, AXX, ALU.max))
                chain(tt(hot, f, like(tmp[:, :, None], shape), ALU.is_equal))

            gl, el = lg[:, :, 0:NGRP], lg[:, :, NGRP:NGRP + E]
            first_best(gl, NGRP, rt("gm"), rt("gh"), rt("tmp"))
            chain(tt(rt("ge"), gl, like(rt("gm")[:, :, None], [P, 2, NGRP]), ALU.subtract), "router_in")
            chain(ts(rt("gh"), rt("gh"), 1.0, 1.0e30, ALU.subtract, ALU.mult))
            el4 = el.rearrange("p i (g e) -> p i g e", g=NGRP)
            chain(tt(el4, el4, like(rt("gh")[:, :, :, None], [P, 2, NGRP, EPG]), ALU.add))
            first_best(el, E, rt("m1"), rt("h1"), rt("tmp"))
            chain(stt(el, rt("h1"), -2.0e30, el, ALU.mult, ALU.add))
            first_best(el, E, rt("m2"), rt("h2"), rt("tmp"))
            chain(tt(rt("w2"), rt("m2"), rt("m1"), ALU.subtract), "router_in")
            dve.wait_ge(q["router_exp"], 2)
            chain(dve.tensor_reduce(rt("tmp"), rt("ge"), AXX, ALU.add))
            chain(ts(rt("w1"), rt("w2"), 1.0, None, ALU.add))
            chain(tt(rt("w1"), rt("w1"), rt("tmp"), ALU.mult))
            chain(dve.reciprocal(rt("w1"), rt("w1")))
            chain(tt(member, rt("h1"), rt("h2"), ALU.add), "member_ready")
            chain(ts(rt("w1"), rt("w1"), 0.5, None, ALU.mult))
            chain(tt(rt("w2"), rt("w2"), rt("w1"), ALU.mult))
            chain(tt(rt("h1"), rt("h1"), like(rt("w1")[:, :, None], [P, 2, E]), ALU.mult))
            chain(tt(rt("h2"), rt("h2"), like(rt("w2")[:, :, None], [P, 2, E]), ALU.mult))
            chain(dve.memset(small[:, 112:112 + 2 * (E + GANG)], 0.0))
            chain(tt(combine[:, :, 0:E], rt("h1"), rt("h2"), ALU.add), "combine_ready")
            b0 = full(dve, "places")
            chain(dve.memset(place[:, :, :], 99.0))
            at = place[:, :, 0:E]
            chain(stt(at, b0[:, 0:2 * E].rearrange("p (i e) -> p i e", i=2), 99.0 - CAP, member, ALU.add, ALU.mult))
            chain(ts(at, at, -1.0, 99.0, ALU.mult, ALU.add))
            chain(dve.tensor_reduce(crowd[:, :], b0[:, 2 * E:3 * E], AXX, ALU.max), "crowd_ready")
            dve.sem_inc(bank_free[plan["places"][0]], 1)
            most = dve.value_load(crowd[0:1, 0:1], min_val=0, max_val=S)

            def seat(gang):
                slots = like(cn("falling")[:, None, 0:CAP], [P, GANG, CAP])
                for i in range(NT):
                    o = sel[:, i, :].rearrange("p (e s) -> p e s", e=GANG)
                    tt(o, slots, like(place[:, i, bass.ds(gang * GANG, GANG)][:, :, None], [P, GANG, CAP]),
                       ALU.is_equal).then_inc(q["moe_ready"], 1)

            def weigh_seats(gang):
                for i in range(NT):
                    o = sel[:, i, :].rearrange("p (e s) -> p e s", e=GANG)
                    w = wsel[:, i, :].rearrange("p (e s) -> p e s", e=GANG)
                    ins = tt(w, o, like(combine[:, i, bass.ds(gang * GANG, GANG)][:, :, None], [P, GANG, CAP]), ALU.mult)
                    if i == 1:
                        ins.then_inc(q["sel_ready"], 1)

            def gathered_experts():
                seat(0)
                dve.wait_ge(q["moe_ready"], 2)
                weigh_seats(0)
                with dve.Fori(0, NGANG) as gang:
                    for b in range(2):
                        dve.wait_ge(q["gathered"], gang * 2 + b + 1)
                        tt(gath[:, 4 * b:4 * b + 4, :], bank[b][:, :].rearrange("p (k s) -> p k s", k=4),
                           like(pr("g_ffn")[:, 4 * b:4 * b + 4, None], [P, 4, P]), ALU.mult).then_inc(q["gath_ready"], 1)
                    dve.wait_ge(q["gtanh_ready"], gang + 1)
                    stt(ghid, gtanh, 1.0, bank[2][:, 0:DE], ALU.add, ALU.mult).then_inc(q["moe_ready"], 1)
                    dve.wait_ge(q["moe_ready"], gang * 3 + 3)
                    tt(ghid, ghid, bank[2][:, DE:2 * DE], ALU.mult).then_inc(q["ghid_ready"], 1)
                    dve.wait_ge(q["wsel_turned"], gang + 1)
                    seat(gang + 1)
                    dve.wait_ge(q["moe_ready"], gang * 3 + 5)
                    weigh_seats(gang + 1)
                    for j in range(4):
                        n, i = j // 2, j % 2
                        dve.wait_ge(q["scattered"], gang * 4 + j + 1)
                        o = tok[:, i, n * 512:(n + 1) * 512]
                        tt(o, o, bank[6 + i][:, :], ALU.add).then_inc(q["summed"], 1)

            def dense_experts():
                loop_chain = q["moe_ready"]
                with dve.Fori(0, NGANG) as gang:
                    step = 0
                    for i in range(NT):
                        for e in range(GANG):
                            dve.wait_ge(q["silu_tanh"], gang * 8 + (4 * i + e + 1))
                            h_ = hid[:, e, :]
                            for k in range(2):
                                if k == 0:
                                    ins = stt(h_, gsi[:, e, :], 1.0, bank[e][:, 0:DE], ALU.add, ALU.mult)
                                else:
                                    ins = tt(h_, h_, bank[e][:, DE:2 * DE], ALU.mult)
                                ins.then_inc(loop_chain, 1)
                                step += 1
                                dve.wait_ge(loop_chain, gang * 20 + step)
                            dve.sem_inc(bank_free[e], 1)
                            ts(h_, h_, combine[:, i, bass.ds(gang * GANG + e, 1)], None, ALU.mult).then_inc(q["hid_ready"], 1)
                        for half in range(2):
                            dve.wait_ge(q["hidT2_ready"], gang * 4 + (2 * i + half + 1))
                            dve.sem_inc(bank_free[4 + half], 1)
                        for n in range(2):
                            dve.wait_ge(bank_full[6 + n], gang * 2 + (before_loop[6 + n] + i + 1))
                            o = tok[:, i, n * 512:(n + 1) * 512]
                            tt(o, o, bank[6 + n][:, :], ALU.add).then_inc(loop_chain, 1)
                            step += 1
                            dve.wait_ge(loop_chain, gang * 20 + step)
                            dve.sem_inc(bank_free[6 + n], 1)
                    assert step == 20

            with dve.If(most <= CAP):
                gathered_experts()
            with dve.Else():
                dense_experts()
            chain(dve.memset(stat[:, 24:25], 0.0))

            normalise(tok)
            dve.wait_ge(q["gfin_loaded"], 16)
            res = hT[:, :, :].rearrange("p c t -> p (c t)").rearrange("p (i d) -> p i d", i=2)
            for i in range(NT):
                chain(tt(res[:, i, :], xn[:, i, :], gfin, ALU.mult), "final_ready")


def kernel(**inputs):
    import concourse.bacc as _bacc
    from concourse.bass_utils import run_bass_kernel_spmd as _run

    a = {k: np.asarray(v) for k, v in inputs.items()}

    def channels(v):
        return v.reshape(-1, P).T

    par = np.zeros((P, NPARAMS), np.float32)

    def put(name, v):
        lo, hi = PARAMS[name]
        par[:v.shape[0], lo:hi] = v

    rk, kk, vv = (slice(n * RW, (n + 1) * RW) for n in range(3))
    lo_ = 3 * RW
    mu = a["rw_mu"][0]
    put("g_mix", channels(a["norm_mix"][0]))
    put("g_ffn", channels(a["norm_ffn"][0]))
    put("mu", np.concatenate([channels(mu[kk]), channels(mu[rk]), channels(mu[vv]),
                              np.pad(mu[lo_:lo_ + 64], (0, 64))[:, None], np.pad(mu[lo_ + 64:], (0, 32))[:, None]], 1))
    for name, key in (("w0", "rw_w0"), ("a0", "rw_a0"), ("k_k", "rw_k_k"), ("k_a", "rw_k_a"), ("r_k", "rw_r_k"),
                      ("gn_w", "rw_gn_w"), ("gn_b", "rw_gn_b"), ("pool_scale", "pool_scale"), ("b_merge", "b_merge")):
        put(name, channels(a[key][0].reshape(-1)))
    put("lora_up", np.concatenate([a["rw_w_up"][0], a["rw_a_up"][0]]))
    put("g_up", a["rw_g_up"][0])
    put("pool_w", a["pool_w"][0].transpose(1, 0, 2).reshape(P, -1))
    for b in "kv":
        put(f"w2_{b}", a[f"cmp_w2_{b}"][0].reshape(2, P, DH).transpose(1, 0, 2).reshape(P, -1))
        put(f"pos_{b}", a[f"cmp_pos_{b}"][0].reshape(16, P).T)
    put("rel", np.concatenate([a["rel_bias"], np.ones((1, NH), np.float32)]))
    put("b_router", np.concatenate([a["b_router_grp"][0], a["b_router_exp"][0]])[None])

    front = np.zeros((NFRONT, P, SLOT), np.float32)

    def chunk(n, w):
        c = w.shape[1]
        front[n].reshape(P, KD, -1)[:, :, :c] = w.reshape(KD, P, c).transpose(1, 0, 2)

    w_in = a["w_in"][0]
    r0 = PW
    n0 = PW + 3 * RW + 160
    chunk(C_LORA, np.concatenate([w_in[:, r0 + 3 * RW:r0 + 3 * RW + 160], w_in[:, n0 + 1024 + 6 * 256:]], 1))
    for c0, at, n in ((C_K, r0 + RW, 2), (C_R, r0, 2), (C_V, r0 + 2 * RW, 2), (C_KC, n0 + 1024, 1), (C_VC, n0 + 1280, 1),
                      (C_Q, n0, 4), (C_KS, n0 + 1536, 1), (C_KW, n0 + 2048, 1), (C_VS, n0 + 1792, 1),
                      (C_VW, n0 + 2304, 1), (C_POOL, 0, 2)):
        for j in range(n):
            chunk(c0 + j, w_in[:, at + 256 * j:at + 256 * (j + 1)])
    for c0, key in ((C_W1K, "cmp_w1_k"), (C_W1V, "cmp_w1_v")):
        for j in range(2):
            chunk(c0 + j, a[key][0][1024 * j:1024 * (j + 1)])
    for n in range(4):
        cs = slice(256 * n, 256 * (n + 1))
        for b in range(3):
            chunk(C_MERGE + 5 * n + b, a["w_merge"][0][:, D * b:D * (b + 1)][:, cs])
        for j in range(2):
            chunk(C_MERGE + 5 * n + 3 + j, a["w_branch"][0][1024 * j:1024 * (j + 1), cs])
        chunk(C_OUT + n, a["w_out"][0][:, cs])
    wr = np.concatenate([a["w_router_grp"][0], a["w_router_exp"][0]], 1)
    front[C_ROUTER][:, 0:KD * 36] = wr.reshape(KD, P, 36).transpose(1, 0, 2).reshape(P, -1)

    ex = np.empty((NGANG, GCH, P, SLOT), np.float32)
    gu = ex[:, 0:8].reshape(NGANG, 8, P, GANG, 2, DE)
    for j, key in enumerate(("w_exp_gate", "w_exp_up")):
        gu[:, :, :, :, j] = a[key][0].reshape(NGANG, GANG, KD, P, DE).transpose(0, 2, 3, 1, 4)
    ex[:, 8:12] = a["w_exp_down"][0].reshape(NGANG, GANG, 2, P, D).transpose(0, 1, 3, 2, 4).reshape(NGANG, GANG, P, -1)

    arrays = {
        "x": a["x"][0], "params": par, "consts": constants(), "front": front, "experts": ex,
        "g_final": np.ascontiguousarray(np.broadcast_to(a["norm_final"], (P, D))),
    }
    nc = _bacc.Bacc("TRN2", target_bir_lowering=False, num_devices=1)
    args = [nc.dram_tensor(n, v.shape, F32, kind="ExternalInput").ap() for n, v in arrays.items()]
    out = nc.dram_tensor("out", (S, D), F32, kind="ExternalOutput").ap()
    rows = nc.dram_tensor("bias_rows", (NH, 384), F32, kind="Internal").ap()
    build_layer(nc, *args, out, rows)
    r = _run(nc, [arrays], core_ids=[0])
    return r.results[0]["out"].reshape(1, S, D)
```

```python
import math
from contextlib import ExitStack

import numpy as np

import concourse.bass as bass
from concourse import mybir

F32 = mybir.dt.float32
ALU = mybir.AluOpType
ACT = mybir.ActivationFunctionType
AXX = mybir.AxisListType.X

P = 128
D = 1024
S = 256
NT = S // P
KD = D // P
PW = 512
RW = 512
RH = 8
NH, NG = 16, 4
DH = 64
NCMP, CSTRIDE, CBLOCK = 15, 16, 32
NB = 32
E, EPG, NGRP = 32, 8, 4
DE = 256
CH = 64
NCH = S // CH
NEG = -1.0e30
DECAY = math.exp(-0.5)
GELU_C = math.sqrt(2.0 / math.pi)

SLOT = 2048
RING = 12
FRING = 6
C_LORA = 0
C_POOL = 1
C_K, C_R, C_V = 3, 5, 7
C_KC, C_VC, C_Q = 9, 10, 11
C_W1K, C_W1V = 15, 17
C_KS, C_KW, C_VS, C_VW = 19, 20, 21, 22
C_GATE = 23
C_BRANCH = 35
C_OUT = 43
C_ROUTER = 47
NFRONT = 48
GANG = 4
NGANG = E // GANG
CAP = 32
GCH = 12


RWKV_STEPS = []
for _i in range(NT):
    RWKV_STEPS += [("turn", _i, 0)] + ([("finish", _i - 1, 0)] if _i else [])
    RWKV_STEPS += [("products", _i, _half) for _half in range(2)]
    for _grp in range(2):
        RWKV_STEPS += [("seed", _i, (_grp, 0))] + [("level", _i, (_grp, _n)) for _n in range(5)]
    RWKV_STEPS += [("solve", _i, 0), ("local", _i, 0), ("scan", _i, 0), ("scan", _i, 1)]
RWKV_STEPS += [("finish", NT - 1, 0)]
UNITS = [(_g, _u) for _g in range(NG) for _u in range(6)]
BEFORE = 1
DURING = BEFORE + NG + len(UNITS)
NGATE = 12
LAST = len(RWKV_STEPS) - 1


def columns(parts):
    at, out = 0, {}
    for name, n in parts:
        out[name] = (at, at + n)
        at += n
    return out, at


PARAMS, NPARAMS = columns([
    ("g_mix", 8), ("g_ffn", 8), ("mu", 14), ("w0", 4), ("a0", 4), ("k_k", 4), ("k_a", 4), ("r_k", 4),
    ("gn_w", 4), ("gn_b", 4), ("pool_scale", 4), ("b_merge", 24),
    ("lora_up", RW), ("g_up", RW), ("pool_w", PW), ("w2_k", 2 * DH), ("w2_v", 2 * DH),
    ("pos_k", 16), ("pos_v", 16), ("rel", NH), ("b_router", NGRP + E)])
CONSTS, NCONSTS = columns([
    ("ident", P), ("flip", P), ("headsum", P), ("intra", 4 * P), ("level", 6 * P),
    ("onehot", 384), ("eye64", DH), ("count", 4 * 16), ("ones", P), ("earlier", P),
    ("neghalf", 8), ("falling", E)])


def t5_bucket(dist):
    n = np.maximum(dist, 0)
    nf = np.maximum(n, 1).astype(np.float32)
    large = 16 + (np.log(nf / np.float32(16)) / np.float32(math.log(8)) * np.float32(16)).astype(np.int32)
    return np.where(n < 16, n, np.minimum(large, NB - 1))


def constants():
    c = np.zeros((P, NCONSTS), np.float32)

    def put(name, a):
        lo, hi = CONSTS[name]
        c[:a.shape[0], lo:hi] = a.reshape(a.shape[0], hi - lo)

    r = np.arange(P)
    put("ident", np.eye(P))
    put("flip", np.eye(P)[::-1])
    put("headsum", (r[:, None] // DH == r[None, :] // DH) * 1.0)
    same = r[:, None] // CH == r[None, :] // CH
    before, upto = same & (r[:, None] < r[None, :]), same & (r[:, None] <= r[None, :])
    put("intra", np.concatenate([before, upto, before, upto], 1) * 1.0)
    level = []
    for n in (1, 2, 4, 8, 16, 32):
        level.append((r[:, None] // (2 * n) == r[None, :] // (2 * n))
                     & (r[:, None] % (2 * n) < n) & (r[None, :] % (2 * n) >= n))
    put("level", np.concatenate(level, 1) * 1.0)
    dist = 255 - np.arange(384)
    put("onehot", np.concatenate([(np.arange(NB)[:, None] == t5_bucket(dist)[None, :]) * 1.0,
                                  np.where(dist < 0, NEG, 0.0)[None]]))
    put("eye64", np.eye(P)[:, :DH] + np.eye(P)[:, DH:])
    w = np.array([2, 4, 8, 16])
    put("count", np.broadcast_to(1.0 / np.minimum(np.arange(16)[None] + 1, w[:, None]), (P, 4, 16)))
    put("ones", np.ones((P, P)))
    put("earlier", (r[:, None] < r[None, :]) * 1.0)
    put("neghalf", np.full((P, 8), -0.5))
    put("falling", np.broadcast_to(E - np.arange(E), (P, E)) * 1.0)
    return c


def build_layer(nc, x, params, consts, front, experts, g_final, out, bias_rows):
    ctx = ExitStack()
    with ctx:
        def sb(name, shape):
            return ctx.enter_context(nc.sbuf_tensor(name, shape, F32))

        def sem(name):
            return ctx.enter_context(nc.semaphore(name))

        def like(ap, shape):
            return ap.to_broadcast(shape)

        ring = sb("ring", [P, RING * SLOT])
        par = sb("par", [P, NPARAMS])
        con = sb("con", [P, NCONSTS])
        tok = sb("tok", [P, NT, D])
        hT = sb("hT", [P, KD, S])
        yT = sb("yT", [P, 16, S])
        rawf = sb("raw", [P, 4 * (S + 1)])
        raw = rawf[:, :].rearrange("p (b m t) -> p b m t", b=2, m=2)
        mix = sb("mix", [P, 14, S])
        t1 = sb("t1", [P, 4, S])
        t2 = sb("t2", [P, 4, S])
        t3 = sb("t3", [P, 4, S])
        arbk = sb("arbk", [P, 16, S])
        xcmp = sb("xcmp", [P, 2, 16, NG * NCMP])
        vtok = sb("vtok", [P, 2, NT, 256])
        small = sb("small", [P, 256])
        state = sb("state", [P, 2, 4, DH])
        gate_t = sb("gate_t", [P, NT, 3 * NH])

        def pr(name, rows=P):
            lo, hi = PARAMS[name]
            return par[0:rows, lo:hi]

        def cn(name, rows=P):
            lo, hi = CONSTS[name]
            return con[0:rows, lo:hi]

        ident = cn("ident")
        spare = ring[:, FRING * SLOT:RING * SLOT]
        bias = spare[:, 0:4096].rearrange("p (h m) -> p h m", h=NH)
        amat = spare[:, 4096:8192].rearrange("p (h j t) -> p h j t", h=RH, j=4)
        qT = spare[:, 8192:10240].rearrange("p (m t) -> p m t", m=8)
        kT = spare[:, 10240:12288].rearrange("p (b g t) -> p b g t", b=2, g=NG)
        window = arbk[:, :, :]
        ar = arbk[:, 0:8, :].rearrange("p c t -> p (c t)").rearrange("p (m i j t) -> p m i j t", m=4, i=2, j=2)
        bf = arbk[:, 8:12, :]
        kf = arbk[:, 12:16, :]
        kshift = yT[:, 8:16, :].rearrange("p (b g) t -> p b g t", b=2)
        btok = t1[:, 0:2, :].rearrange("p c t -> p (c t)")
        ktok = t1[:, 2:4, :].rearrange("p c t -> p (c t)")
        vrow = t2[:, 0:2, :].rearrange("p c t -> p (c t)")
        lmask = t2[:, 2:4, :].rearrange("p c t -> p (c t)").rearrange("p (h t) -> p h t", h=4)
        xinv = t3[:, 0:2, :].rearrange("p c t -> p (c t)").rearrange("p (h t) -> p h t", h=4)
        zinv = [rawf[:, g * 512:(g + 1) * 512].rearrange("p (h t) -> p h t", h=4) for g in range(2)]
        winv = t3[:, 2:4, :].rearrange("p c t -> p (c t)").rearrange("p (h t) -> p h t", h=4)
        rhs = mix[:, 0:4, :].rearrange("p c t -> p (c t)").rearrange("p (h j v) -> p h j v", h=RH, j=2)
        bonus = mix[:, 4:8, :]
        fc = t3[:, :, :].rearrange("p c t -> p (c t)").rearrange("p (c m j v) -> p c m j v", c=2, m=4, j=2)
        ynorm = t2[:, 2:4, :].rearrange("p c t -> p (c t)")
        ysq = t3[:, 0:2, :].rearrange("p c t -> p (c t)")
        pend = small[:, 0:16].rearrange("p (m c) -> p m c", m=4)
        stat = small[:, 16:64]
        tokf = tok[:, :, :].rearrange("p i d -> p (i d)")
        prob = tokf[:, 0:1024].rearrange("p (b n) -> p b n", b=2)
        probT = tokf[:, 1024:2048].rearrange("p (b n) -> p b n", b=2)
        xf = xcmp[:, :, :, :].rearrange("p b j n -> p (b j n)")
        gx = xf[0:60, 0:512]
        gy = xf[0:60, 512:1024]
        hidT = xf[:, 1024:1264].rearrange("p (f n) -> p f n", f=4)
        kcb = xf[:, 1264:1324]
        vcb = xf[0:NCMP, 1324:1580].rearrange("p (g v) -> p g v", g=NG)
        cprob = [xf[:, lo:lo + 8 * n].rearrange("p (m n) -> p m n", m=8)
                 for lo, n in ((1580, 7), (1636, 7), (1024, NCMP), (1144, NCMP))]
        cprobT = xf[0:NCMP, 0:1024].rearrange("p (i h t) -> p i h t", i=2, h=4)
        astat = small[:, 64:128]
        gsig = [spare[:, lo:lo + 512].rearrange("p (m t) -> p m t", m=2)
                for lo in list(range(0, 4096, 512)) + list(range(8192, 10240, 512))]
        merged = arbk[:, 0:8, :]
        macc = t2[:, 0:2, :]
        mtmp = t2[:, 2:4, :]
        xn = mix[:, 0:8, :].rearrange("p c t -> p (c t)").rearrange("p (i d) -> p i d", i=2)
        arf = arbk[:, :, :].rearrange("p c t -> p (c t)")
        gath = arf[:, 0:1024].rearrange("p (k s) -> p k s", k=KD)
        ydown = arf[:, 1024:2048]
        gtanh = arf[:, 2048:2304]
        ghid = arf[:, 2304:2560]
        ghidT = arf[:, 2560:2816].rearrange("p (f s) -> p f s", f=2)
        sel = arf[:, 2816:3072].rearrange("p (i s) -> p i s", i=2)
        wsel = arf[:, 3072:3328].rearrange("p (i s) -> p i s", i=2)
        wselT = arf[:, 3328:3584].rearrange("p (i t) -> p i t", i=2)
        place = arf[:, 3584:3584 + 2 * (E + GANG)].rearrange("p (i e) -> p i e", i=2)
        gsi = arbk[:, 8:12, :].rearrange("p c t -> p (c t)").rearrange("p (e n) -> p e n", e=GANG)
        hid = arbk[:, 12:16, :].rearrange("p c t -> p (c t)").rearrange("p (e n) -> p e n", e=GANG)
        hidm = t1[:, :, :].rearrange("p c t -> p (c t)").rearrange("p (e f t) -> p e f t", e=GANG, f=2)
        combine = small[:, 112:112 + 2 * (E + GANG)].rearrange("p (i e) -> p i e", i=2)
        member = mix[:, 8, 0:2 * E].rearrange("p (i e) -> p i e", i=2)
        crowd = ctx.enter_context(nc.sbuf_tensor("crowd", [P, 1], mybir.dt.int32))
        halves = small[:, 192:224]
        rtf = t3[:, :, :].rearrange("p c t -> p (c t)")
        rt_at, _ = columns([("lg", 72), ("gh", 8), ("ge", 8), ("h1", 64), ("h2", 64), ("gm", 2), ("m1", 2), ("m2", 2),
                            ("tmp", 2), ("w1", 2), ("w2", 2)])

        def rt(name):
            lo, hi = rt_at[name]
            return rtf[:, lo:hi] if hi - lo == 2 else rtf[:, lo:hi].rearrange("p (i n) -> p i n", i=2)

        gfin = yT[:, 0:4, :].rearrange("p c t -> p (c t)")

        bank = [ctx.enter_context(nc.psum_tensor(f"bank{b}", [P, 512], F32)) for b in range(8)]

        loaded = [sem(f"slot_loaded{s}") for s in range(RING)]
        taken = sem("chunks_taken")
        bank_full = [sem(f"bank_full{b}") for b in range(8)]
        bank_free = [sem(f"bank_free{b}") for b in range(8)]
        names = [
            "small_loaded", "x_loaded", "x_again", "stored", "gfin_loaded", "win_stored", "win_ready",
            "raw_zeroed", "root_ready", "lmask_ready", "state_zeroed",
            "raw_ready", "gate_tanh", "lora_w_ready", "lora_g_tanh", "kshift_ready", "bias_ready", "q_ready",
            "k_ready", "v_ready", "u_ready", "gx_ready", "gelu_tanh", "decay_tanh", "rate_tanh", "kk_root",
            "hidT_ready", "cmp_kv_ready", "decay_exp", "cexp_ready", "cprobT_ready", "exp_ready", "probT_ready",
            "tok_ready", "w_ready", "rhs_ready", "xu_ready", "gn_ready", "gsig_ready", "router_exp",
            "silu_tanh", "hidT2_ready", "act_chain", "gtanh_ready", "wselT_ready", "ghidT_ready",
            "ydown_ready",
            "gathered", "wsel_turned", "gate_up", "hid_turned", "downed", "scattered",
            "halves_ready", "rms_in", "xn_ready", "hT_ready", "raw_used", "mix_ready", "win_row", "gates_ready",
            "xcmp_ready", "pool_ready", "kk_sq_ready", "kk_max", "gelu_in", "gelu_ready", "log_ready",
            "lora_g_ready", "pool_out", "bonus_ready", "rwkv_ready", "cexp_in", "cprob_ready", "exp_in",
            "prob_ready", "nsa_ready", "amat_ready", "z_ready", "x_ready", "rx_ready", "fc_ready",
            "state_ready", "ynorm_ready", "yrw_ready", "gated", "merged_ready", "sum_ready", "router_in",
            "combine_ready", "hid_ready", "moe_ready", "member_ready", "crowd_ready", "sel_ready", "gath_ready",
            "ghid_ready", "summed", "final_ready", "dve_chain"]
        q = {n: sem(n) for n in names}

        def ordinal():
            seen = {}

            def nth(b):
                seen[b] = seen.get(b, -1) + 1
                return seen[b]
            return nth

        plan = {}
        nth = ordinal()

        def hand(name, b):
            assert name not in plan
            plan[name] = (b, nth(b))

        for n in range(4):
            hand(f"xT{n}", n)
        hand("brow", 4)
        hand("lora_in", 0), hand("gates", 1)
        hand("pool0", 2), hand("pool1", 3)
        for c in range(1, 7):
            hand(f"rkv{c}", 4 + c % 2)
        hand("poolmix0", 2), hand("poolmix1", 3)
        for n in range(8):
            hand(f"bias{n}", 6 + n % 2)
        for n in range(2):
            hand(f"wup{n}", n)
        for n in range(2):
            hand(f"aup{n}", 2 + n)
        hand("kc", 0), hand("vc", 1)
        hand("kk0", 4), hand("kk1", 5)
        for n in range(4):
            hand(f"q{n}", 2 + n % 2)
        hand("mlp_k", 6), hand("mlp_v", 7)
        hand("ks", 0), hand("kw", 1)
        hand("bonus0", 4), hand("bonus1", 5)
        hand("vs", 2)
        hand("hidT", 6)
        hand("vw", 3)
        hand("kcb", 7), hand("vcb", 6)

        def hand_early(step):
            kind, i, which = step
            if kind == "turn":
                hand(f"tok{i}0", 4), hand(f"tok{i}1", 5)
            elif kind == "finish":
                hand(f"gup{i}", 7)
            elif kind == "products":
                for h in range(4 * which, 4 * which + 2):
                    hand(f"A{i}{h}", 4 + h % 4)
            elif kind == "level":
                hand("W%d%d%d" % (i, *which), 5)
            elif kind == "solve":
                hand(f"w0{i}", 4)
            elif kind == "local":
                hand(f"rx{i}0", 7), hand(f"rx{i}1", 4)
            elif kind == "scan" and 2 * i + which < NCH - 1:
                hand(f"st{i}{which}", 7)

        def hand_late(step):
            kind, i, which = step
            if kind == "turn":
                hand(f"tok{i}2", 6), hand(f"atok{i}", 7)
            elif kind == "finish":
                hand(f"yT{i}", 4)
            elif kind == "products":
                for h in range(4 * which + 2, 4 * which + 4):
                    hand(f"A{i}{h}", 4 + h % 4)
            elif kind == "seed":
                hand("XZ%d%d" % (i, which[0]), 4)
            elif kind == "level":
                if which[1] < 4:
                    hand("X%d%d%d" % (i, *which), 6)
                hand("Z%d%d%d" % (i, *which), 7)
            elif kind == "solve":
                hand(f"xu{i}0", 5), hand(f"xu{i}1", 6)
            elif kind == "local":
                hand(f"fc{i}0", 7), hand(f"fc{i}1", 4)
                hand(f"y{i}0", 5), hand(f"y{i}1", 6)

        for s in range(BEFORE):
            hand_early(RWKV_STEPS[s]), hand_late(RWKV_STEPS[s])
        for u in range(4):
            hand(f"cs{u}", u % 2)
        hand("s00", 0), hand("s01", 1)
        steps = iter(RWKV_STEPS[BEFORE:DURING])
        for n, (g, u) in enumerate(UNITS):
            if u == 0:
                step = next(steps)
                hand(f"cT{g}0", 2)
                hand_early(step)
                hand(f"cT{g}1", 2)
                hand_late(step)
                hand(f"o{g}", 3)
            step = next(steps)
            hand_early(step)
            hand(f"pT{g}{u}", 2)
            hand_late(step)
            if n + 2 < len(UNITS):
                hand("s%d%d" % UNITS[n + 2], n % 2)
        beside = {j: RWKV_STEPS[DURING + j] for j in range(LAST - DURING)}
        beside[NGATE - 1] = RWKV_STEPS[LAST]
        for j in range(NGATE):
            if j in beside:
                hand_early(beside[j])
            hand(f"mg{j}", j % 4)
            if j in beside:
                hand_late(beside[j])
        for n in range(4):
            for b in range(3):
                hand(f"mb{n}{b}", (3 * n + b) % 6)
        for n in range(4):
            hand(f"out{n}", 6 + n % 2)
        for n in range(4):
            hand(f"hT2{n}", n)
        hand("router", 4)
        hand("places", 5)
        before_loop = [nth(b) for b in range(8)]


        def full(eng, name):
            b, n = plan[name]
            eng.wait_ge(bank_full[b], n + 1)
            return bank[b]

        def free(ins, name):
            ins.then_inc(bank_free[plan[name][0]], 1)

        def chainer(eng, own):
            count = {}

            def chain(ins, name=None, hold=True):
                name = name or own
                count[name] = count.get(name, 0) + 1
                ins.then_inc(q[name], 1)
                if hold:
                    eng.wait_ge(q[name], count[name])
            chain.count = count
            return chain

        block = ctx.enter_context(nc.Block())

        @block.sync
        def _(sp):
            sp.dma_start(tok[:, :, :], x.rearrange("(i p) d -> p i d", p=P)).then_inc(q["x_loaded"], 16)
            sp.dma_start(con[:, :], consts).then_inc(q["small_loaded"], 16)
            sp.dma_start(par[:, :], params).then_inc(q["small_loaded"], 16)
            for s in range(FRING):
                sp.dma_start(ring[:, s * SLOT:(s + 1) * SLOT], front[s]).then_inc(loaded[s], 16)
            sp.wait_ge(q["win_row"], 1)
            sp.dma_start(bias_rows, arbk[0:NH, 0:2, :].rearrange("p a b -> p (a b)")[:, 0:384])\
                .then_inc(q["win_stored"], 16)
            sp.wait_ge(q["win_stored"], 16)
            sp.dma_start(window, bass.AP(bias_rows.tensor, 0, [[1, P], [384, NH], [1, 256]]))\
                .then_inc(q["win_ready"], 16)
            with sp.Fori(1, NFRONT // FRING) as rnd:
                for s in range(FRING):
                    sp.wait_ge(taken, rnd * FRING + (s + 1 - FRING))
                    sp.dma_start(ring[:, s * SLOT:(s + 1) * SLOT], front[rnd * FRING + s]).then_inc(loaded[s], 16)
            for s in range(FRING):
                sp.wait_ge(taken, NFRONT + s + 1 - FRING)
                sp.dma_start(ring[:, s * SLOT:(s + 1) * SLOT], experts[0, s]).then_inc(loaded[s], 16)
            with sp.Fori(1, NGANG) as gang:
                for s in range(GCH):
                    sp.wait_ge(taken, gang * GCH + (NFRONT - GCH + s + 1))
                    sp.dma_start(ring[:, s * SLOT:(s + 1) * SLOT], experts[gang, s]).then_inc(loaded[s], 16)
            sp.wait_ge(q["final_ready"], 2)
            sp.dma_start(out.rearrange("(i p) d -> p i d", p=P), hT[:, :, :].rearrange("p c t -> p (c t)")
                         .rearrange("p (i d) -> p i d", i=2)).then_inc(q["stored"], 16)
            sp.wait_ge(q["stored"], 16)

        @block.tensor
        def _(pe):
            def begin(name):
                b, n = plan[name]
                if n:
                    pe.wait_ge(bank_free[b], n)
                return bank[b]

            def end(ins, name):
                ins.then_inc(bank_full[plan[name][0]], 1)

            def chunk(n):
                pe.wait_ge(loaded[n % FRING], 16 * (n // FRING + 1))
                return ring[:, (n % FRING) * SLOT:(n % FRING + 1) * SLOT]

            owed = [0]

            def pe_take():
                owed[0] += 1

            def first(ins):
                if owed[0]:
                    ins.then_inc(taken, owed[0])
                    owed[0] = 0
                return ins

            def mm(o, l, r, k, n):
                return first(pe.matmul(o, l, r, start=(k == 0), stop=(k == n - 1)))

            def project(name, n):
                w = chunk(n).rearrange("p (k c) -> p k c", k=KD)
                o = begin(name)
                for m in range(2):
                    for k in range(KD):
                        last = mm(o[:, m * S:(m + 1) * S], w[:, k, m * P:(m + 1) * P], hT[:, k, :], k, KD)
                end(last, name)
                pe_take()

            for n in range(4):
                i = n // 2
                pe.wait_ge(q["xn_ready"], i + 1)
                if n == 0:
                    pe.wait_ge(q["small_loaded"], 32)
                o = begin(f"xT{n}")
                for k in range(4):
                    kk = (n % 2) * 4 + k
                    last = pe.transpose(o[:, k * P:(k + 1) * P], xn[:, i, kk * P:(kk + 1) * P], ident)
                end(last, f"xT{n}")
            o = begin("brow")
            end(pe.matmul(o[0:NH, 0:384], pr("rel", NB + 1), cn("onehot", NB + 1), start=True, stop=True), "brow")
            pe.wait_ge(q["hT_ready"], 4)

            w = chunk(C_LORA).rearrange("p (k c) -> p k c", k=KD)
            o = begin("lora_in")
            for lo, n, col in ((0, 64, 0), (64, 96, S)):
                for k in range(KD):
                    last = mm(o[0:n, col:col + S], w[:, k, lo:lo + n], hT[:, k, :], k, KD)
            end(last, "lora_in")
            o = begin("gates")
            for i in range(NT):
                for k in range(KD):
                    last = mm(o[:, i * 48:(i + 1) * 48], hT[:, k, i * P:(i + 1) * P], w[:, k, 160:208], k, KD)
            end(last, "gates")
            pe_take()
            project("pool0", C_POOL)
            project("pool1", C_POOL + 1)
            for c in range(1, 7):
                project(f"rkv{c}", C_K + c - 1)

            pe.wait_ge(q["pool_ready"], 1)
            for n in range(2):
                o = begin(f"poolmix{n}")
                for m in range(2):
                    gi = 2 * n + m
                    last = first(pe.matmul(o[:, m * S:(m + 1) * S], pr("pool_w")[:, gi * P:(gi + 1) * P],
                                           yT[:, gi, :], start=True, stop=True))
                end(last, f"poolmix{n}")

            pe.wait_ge(q["win_ready"], 16)
            wf = window.rearrange("p a b -> p (a b)")
            for n in range(8):
                o = begin(f"bias{n}")
                end(pe.matmul(o[:, :], cn("flip"), wf[:, n * 512:(n + 1) * 512], start=True, stop=True), f"bias{n}")

            pe.wait_ge(q["lora_w_ready"], 1)
            for n in range(2):
                o = begin(f"wup{n}")
                for m in range(2):
                    c = (2 * n + m) * P
                    last = pe.matmul(o[:, m * S:(m + 1) * S], pr("lora_up")[0:32, c:c + P], mix[0:32, 12, :],
                                     start=True, stop=True)
                end(last, f"wup{n}")
            for n in range(2):
                o = begin(f"aup{n}")
                for m in range(2):
                    c = (2 * n + m) * P
                    last = pe.matmul(o[:, m * S:(m + 1) * S], pr("lora_up")[32:64, c:c + P], mix[32:64, 12, :],
                                     start=True, stop=True)
                end(last, f"aup{n}")

            project("kc", C_KC)
            project("vc", C_VC)
            pe.wait_ge(q["kk_sq_ready"], 1)
            for n in range(2):
                o = begin(f"kk{n}")
                end(pe.matmul(o[:, :], cn("headsum"), t3[:, 2 * n:2 * n + 2, :], start=True, stop=True), f"kk{n}")
            for n in range(4):
                project(f"q{n}", C_Q + n)

            for b, (name, c0) in enumerate((("mlp_k", C_W1K), ("mlp_v", C_W1V))):
                pe.wait_ge(q["xcmp_ready"], b + 1)
                o = begin(name)
                for half in range(2):
                    w = chunk(c0 + half).rearrange("p (k c) -> p k c", k=KD)
                    for j in range(8):
                        last = mm(o[0:60, 0:256], xcmp[:, b, half * 8 + j, :], w[:, j, :], half * 8 + j, 16)
                    if half:
                        end(last, name)
                    pe_take()
            project("ks", C_KS)
            project("kw", C_KW)
            pe.wait_ge(q["bonus_ready"], 1)
            for n in range(2):
                o = begin(f"bonus{n}")
                end(pe.matmul(o[:, :], cn("headsum"), mix[:, 4 + 2 * n:6 + 2 * n, :], start=True, stop=True), f"bonus{n}")

            def values(name, c):
                w = chunk(c).rearrange("p (k c) -> p k c", k=KD)
                o = begin(name)
                for i in range(NT):
                    for k in range(KD):
                        last = mm(o[:, i * 256:(i + 1) * 256], hT[:, k, i * P:(i + 1) * P], w[:, k, :], k, KD)
                end(last, name)
                pe_take()

            values("vs", C_VS)
            pe.wait_ge(q["gelu_ready"], 1)
            o = begin("hidT")
            for f in range(4):
                last = first(pe.transpose(o[:, f * 60:(f + 1) * 60], gx[:, f * P:(f + 1) * P], ident[0:60, 0:60]))
            end(last, "hidT")
            values("vw", C_VW)
            pe.wait_ge(q["hidT_ready"], 1)
            w2k = pr("w2_k").rearrange("p (f v) -> p f v", f=2)
            w2v = pr("w2_v").rearrange("p (f v) -> p f v", f=2)
            o = begin("kcb")
            for p in range(2):
                for f in range(2):
                    last = mm(o[64 * p:64 * p + 64, 0:60], w2k[:, f, :], hidT[:, f, :], f, 2)
            end(last, "kcb")
            o = begin("vcb")
            for g in range(NG):
                for f in range(2):
                    last = mm(o[0:NCMP, g * 64:g * 64 + 64], hidT[:, 2 + f, g * NCMP:(g + 1) * NCMP], w2v[:, f, :], f, 2)
            end(last, "vcb")

            def early(step):
                kind, i, which = step
                ts = slice(i * P, (i + 1) * P)
                if kind == "turn":
                    if i == 0:
                        pe.wait_ge(q["rwkv_ready"], 1)
                    for w_, src in enumerate((bf, kf)):
                        turned(f"tok{i}{w_}", [src[:, m, ts] for m in range(4)])
                elif kind == "products":
                    products(i, range(4 * which, 4 * which + 2))
                elif kind == "level":
                    grp, n = which
                    turn_ = 2 * i + grp
                    pe.wait_ge(q["x_ready"], 5 * turn_ + n + 1)
                    pe.wait_ge(q["lmask_ready"], 6 * turn_ + n + 2)
                    o = begin(f"W{i}{grp}{n}")
                    for h in range(4):
                        last = pe.matmul(o[:, h * P:(h + 1) * P], lmask[:, h, :], xinv[:, h, :], start=True, stop=True)
                    end(last, f"W{i}{grp}{n}")
                elif kind == "solve":
                    pe.wait_ge(q["z_ready"], 12 * (i + 1))
                    pe.wait_ge(q["tok_ready"], 4 * (i + 1))
                    o = begin(f"w0{i}")
                    for h in range(RH):
                        last = pe.matmul(o[:, h * DH:(h + 1) * DH], amat[:, h, 2, :], vrow[:, h * DH:(h + 1) * DH],
                                         start=True, stop=True)
                    end(last, f"w0{i}")
                elif kind == "local":
                    pe.wait_ge(q["xu_ready"], 2 * (i + 1))
                    for n in range(2):
                        o = begin(f"rx{i}{n}")
                        for hh in range(4):
                            h = 4 * n + hh
                            last = pe.matmul(o[64 * (h % 2):64 * (h % 2) + 64, (hh // 2) * P:(hh // 2 + 1) * P],
                                             rhs[:, h, 0, :], amat[:, h, 1, :], start=True, stop=True)
                        end(last, f"rx{i}{n}")
                elif kind == "scan":
                    n = 2 * i + which
                    pe.wait_ge(q["rx_ready"], 2 * (i + 1))
                    pe.wait_ge(q["fc_ready"], n + 1)
                    pe.wait_ge(q["state_zeroed"], 1)
                    if n:
                        pe.wait_ge(q["state_ready"], n)
                    if n < NCH - 1:
                        o = begin(f"st{i}{which}")
                        for h in range(RH):
                            m, p = h // 2, h % 2
                            rows = slice(64 * p, 64 * p + 64)
                            last = pe.matmul(o[rows, m * DH:(m + 1) * DH], fc[rows, which, m, 0, :],
                                             state[rows, n % 2, m, :], start=True, stop=True)
                        end(last, f"st{i}{which}")
                elif kind == "finish":
                    pe.wait_ge(q["lora_g_ready"], 1)
                    o = begin(f"gup{i}")
                    for m in range(4):
                        last = pe.matmul(o[:, m * P:(m + 1) * P], pr("g_up", 96)[:, m * P:(m + 1) * P], mix[0:96, 13, ts],
                                         start=True, stop=True)
                    end(last, f"gup{i}")

            def late(step):
                kind, i, which = step
                ts = slice(i * P, (i + 1) * P)
                if kind == "turn":
                    turned(f"tok{i}2", [mix[:, 8 + m, ts] for m in range(4)])
                    turned(f"atok{i}", [ar[:, m, i, 0, :] for m in range(4)])
                elif kind == "products":
                    products(i, range(4 * which + 2, 4 * which + 4))
                elif kind == "seed":
                    grp = which[0]
                    pe.wait_ge(q["z_ready"], 6 * (2 * i + grp) + 1)
                    turned(f"XZ{i}{grp}", [zinv[grp][:, h, :] for h in range(4)])
                elif kind == "level":
                    grp, n = which
                    turn_ = 2 * i + grp
                    z = zinv[grp]
                    pe.wait_ge(q["w_ready"], 5 * turn_ + n + 1)
                    pe.wait_ge(q["z_ready"], 6 * turn_ + n + 1)
                    if n < 4:
                        o = begin(f"X{i}{grp}{n}")
                        for h in range(4):
                            last = pe.matmul(o[:, h * P:(h + 1) * P], z[:, h, :], winv[:, h, :], start=True, stop=True)
                        end(last, f"X{i}{grp}{n}")
                    o = begin(f"Z{i}{grp}{n}")
                    for h in range(4):
                        last = pe.matmul(o[:, h * P:(h + 1) * P], winv[:, h, :], z[:, h, :], start=True, stop=True)
                    end(last, f"Z{i}{grp}{n}")
                elif kind == "solve":
                    pe.wait_ge(q["rhs_ready"], i + 1)
                    for n in range(2):
                        o = begin(f"xu{i}{n}")
                        for h in range(4):
                            last = pe.matmul(o[:, h * P:(h + 1) * P], zinv[n][:, h, :], rhs[:, 4 * n + h, :, :],
                                             start=True, stop=True)
                        end(last, f"xu{i}{n}")
                elif kind == "local":
                    for c in range(2):
                        rows = slice(64 * c, 64 * c + 64)
                        o = begin(f"fc{i}{c}")
                        for h in range(RH):
                            m, p = h // 2, h % 2
                            oo = o[64 * p:64 * p + 64, m * P:(m + 1) * P]
                            hs = slice(h * DH, (h + 1) * DH)
                            pe.matmul(oo[:, 0:64], rhs[rows, h, 0, :], btok[rows, hs], start=True, stop=True)
                            pe.matmul(oo[:, 64:128], btok[rows, hs], rhs[rows, h, 1, :], start=True, stop=False)
                            last = pe.matmul(oo[:, 64:128], ktok[rows, hs], vrow[rows, hs], start=False, stop=True)
                        end(last, f"fc{i}{c}")
                    ybank = [begin(f"y{i}{p}") for p in range(2)]
                    for h in range(RH):
                        m, p = h // 2, h % 2
                        oo = ybank[p][:, m * DH:(m + 1) * DH]
                        pe.matmul(oo, amat[:, h, 1, :], rhs[:, h, 1, :], start=(m == 0), stop=False, skip_group_check=True)
                        pe.matmul(oo, amat[:, h, 3, :], vrow[:, h * DH:(h + 1) * DH], start=False, stop=False,
                                  skip_group_check=True)
                elif kind == "scan":
                    c = which
                    for p in range(2):
                        rows = slice(64 * p, 64 * p + 64)
                        yb = bank[plan[f"y{i}{p}"][0]]
                        for m in range(4):
                            last = pe.matmul(yb[64 * c:64 * c + 64, m * DH:(m + 1) * DH],
                                             ar[rows, m, i, 1, 64 * c:64 * c + 64], state[rows, (2 * i + c) % 2, m, :],
                                             start=False, stop=True, skip_group_check=True)
                        if c == 1:
                            end(last, f"y{i}{p}")
                elif kind == "finish":
                    pe.wait_ge(q["ynorm_ready"], i + 1)
                    turned(f"yT{i}", [ynorm[:, m * P:(m + 1) * P] for m in range(4)])

            def turned(name, parts):
                o = begin(name)
                for b, part in enumerate(parts):
                    last = pe.transpose(o[:, b * P:(b + 1) * P], part, ident)
                end(last, name)

            def products(i, heads):
                for h in heads:
                    m, p = h // 2, h % 2
                    rows = slice(64 * p, 64 * p + 64)
                    o = begin(f"A{i}{h}")
                    for j, left in enumerate((bf, kf)):
                        last = pe.matmul(o[:, j * S:(j + 1) * S], left[rows, m, i * P:(i + 1) * P], ar[rows, m, i, :, :],
                                         start=True, stop=True)
                    end(last, f"A{i}{h}")

            def scores(g, u):
                p = u % 2
                o = begin(f"s{g}{u}")
                rows = slice(64 * p, 64 * p + 64)
                for b in range(4):
                    if u < 2:
                        br, hp = b // 2, b % 2
                        last = pe.matmul(o[:, b * P:(b + 1) * P], qT[rows, 2 * g + hp, 0:P], kT[rows, br, g, 0:P],
                                         start=True, stop=True)
                    elif b < 2:
                        last = pe.matmul(o[:, b * S:(b + 1) * S], qT[rows, 2 * g + b, P:S],
                                         kT[rows, (u - 2) // 2, g, :], start=True, stop=True)
                end(last, f"s{g}{u}")

            def turn(g, u):
                n = g * 6 + u
                pe.wait_ge(q["prob_ready"], n + 1)
                turned(f"pT{g}{u}", [prob[:, n % 2, s * P:(s + 1) * P] for s in ((0, 1, 2, 3) if u < 2 else (0, 2, 1, 3))])

            def weigh(g, u, o):
                n = g * 6 + u
                p = u % 2
                pe.wait_ge(q["probT_ready"], n + 1)
                i = 0 if u < 2 else 1
                for b in range(2):
                    br, kb = (b, 0) if u < 2 else ((u - 2) // 2, b)
                    last = pe.matmul(o[64 * p:64 * p + 64, :].rearrange("p (h t) -> p h t", h=2)[:, :, i * P:(i + 1) * P],
                                     vtok[:, br, kb, g * DH:(g + 1) * DH], probT[:, n % 2, b * 2 * P:(b + 1) * 2 * P],
                                     start=False, stop=(b == 1 and (u < 2 or u >= 4)), skip_group_check=True)
                return last

            def turn_compressed(g, i):
                nc_ = 7 if i == 0 else NCMP
                o = begin(f"cT{g}{i}")
                for b in range(4):
                    p, hp = b // 2, b % 2
                    last = pe.transpose(o[0:nc_, b * P:(b + 1) * P], cprob[2 * i + p][:, 2 * g + hp, :], ident)
                end(last, f"cT{g}{i}")

            for step in RWKV_STEPS[0:BEFORE]:
                early(step)
                late(step)
            pe.wait_ge(q["gates_ready"], 1)
            pe.wait_ge(q["q_ready"], 4)
            pe.wait_ge(q["k_ready"], 2)
            pe.wait_ge(q["v_ready"], 2)
            pe.wait_ge(q["cmp_kv_ready"], 2)
            for u in range(4):
                i, p = u // 2, u % 2
                nc_ = 7 if i == 0 else NCMP
                o = begin(f"cs{u}")
                for m in range(8):
                    g = (2 * m + p) // 4
                    last = pe.matmul(o[:, m * nc_:(m + 1) * nc_], qT[64 * p:64 * p + 64, m, i * P:(i + 1) * P],
                                     kcb[64 * p:64 * p + 64, g * NCMP:g * NCMP + nc_], start=True, stop=True)
                end(last, f"cs{u}")
            scores(0, 0)
            scores(0, 1)
            pe.wait_ge(q["cprob_ready"], 4)
            steps = iter(RWKV_STEPS[BEFORE:DURING])
            for n, (g, u) in enumerate(UNITS):
                if u == 0:
                    step = next(steps)
                    turn_compressed(g, 0)
                    early(step)
                    turn_compressed(g, 1)
                    late(step)
                    acc = begin(f"o{g}")
                    for i in range(NT):
                        nc_ = 7 if i == 0 else NCMP
                        pe.wait_ge(q["cprobT_ready"], 2 * g + i + 1)
                        for p in range(2):
                            last = pe.matmul(acc[64 * p:64 * p + 64, :].rearrange("p (h t) -> p h t", h=2)[:, :, i * P:(i + 1) * P],
                                             vcb[0:nc_, g, :], cprobT[0:nc_, i, 2 * p:2 * p + 2, :], start=(i == 0),
                                             stop=False, skip_group_check=True)
                step = next(steps)
                early(step)
                turn(g, u)
                late(step)
                if n + 2 < len(UNITS):
                    scores(*UNITS[n + 2])
                last = weigh(g, u, acc)
                if u == 5:
                    end(last, f"o{g}")

            for j in range(NGATE):
                w = chunk(C_GATE + j).rearrange("p (k c) -> p k c", k=KD)
                if j in beside:
                    early(beside[j])
                o = begin(f"mg{j}")
                for m in range(2):
                    for k in range(KD):
                        last = mm(o[:, m * S:(m + 1) * S], w[:, k, m * P:(m + 1) * P], hT[:, k, :], k, KD)
                    if m == 0 and j in beside and j < NGATE - 1:
                        late(beside[j])
                end(last, f"mg{j}")
                pe_take()
                if j == NGATE - 1:
                    late(beside[j])

            pe.wait_ge(q["pool_out"], 2)
            pe.wait_ge(q["nsa_ready"], NG)
            pe.wait_ge(q["yrw_ready"], NT)
            for n in range(4):
                for c in range(2):
                    w = chunk(C_BRANCH + 2 * n + c).rearrange("p (k c) -> p k c", k=KD)
                    for b in ((0, 1) if c == 0 else (2,)):
                        o = begin(f"mb{n}{b}")
                        k0, nk = ((0, 4), (4, 4), (0, 8))[b]
                        for m in range(2):
                            for k in range(nk):
                                last = mm(o[:, m * S:(m + 1) * S], w[:, k0 + k, m * P:(m + 1) * P],
                                          yT[:, 8 * c + k0 + k, :], k, nk)
                        end(last, f"mb{n}{b}")
                    pe_take()
            pe.wait_ge(q["merged_ready"], 4)
            for n in range(4):
                w = chunk(C_OUT + n).rearrange("p (k c) -> p k c", k=KD)
                o = begin(f"out{n}")
                for i in range(NT):
                    for k in range(KD):
                        last = mm(o[:, i * 256:(i + 1) * 256], merged[:, k, i * P:(i + 1) * P], w[:, k, :], k, KD)
                end(last, f"out{n}")
                pe_take()

            for n in range(4):
                i = n // 2
                pe.wait_ge(q["xn_ready"], 2 + i + 1)
                o = begin(f"hT2{n}")
                for k in range(4):
                    kk = (n % 2) * 4 + k
                    last = first(pe.transpose(o[:, k * P:(k + 1) * P], xn[:, i, kk * P:(kk + 1) * P], ident))
                end(last, f"hT2{n}")
            pe.wait_ge(q["hT_ready"], 8)
            w = chunk(C_ROUTER)[:, 0:8 * 36].rearrange("p (k c) -> p k c", k=KD)
            o = begin("router")
            for i in range(NT):
                oo = o[:, i * 36:(i + 1) * 36]
                for k in range(KD):
                    pe.matmul(oo, hT[:, k, i * P:(i + 1) * P], w[:, k, :], start=(k == 0), stop=False)
                last = pe.matmul(oo, cn("ones", 1), pr("b_router", 1), start=False, stop=True)
            end(last, "router")
            full(pe, "router")
            pe.sem_inc(taken, 1)
            pe.wait_ge(q["member_ready"], 1)
            o = begin("places")
            pe.matmul(o[:, 0:E], cn("earlier"), member[:, 0, :], start=True, stop=True)
            pe.matmul(o[:, E:2 * E], cn("ones"), member[:, 0, :], start=True, stop=False)
            pe.matmul(o[:, E:2 * E], cn("earlier"), member[:, 1, :], start=False, stop=True)
            pe.matmul(o[:, 2 * E:3 * E], cn("ones"), member[:, 0, :], start=True, stop=False)
            end(pe.matmul(o[:, 2 * E:3 * E], cn("ones"), member[:, 1, :], start=False, stop=True), "places")

            pe.wait_ge(q["crowd_ready"], 1)
            most = pe.value_load(crowd[0:1, 0:1], min_val=0, max_val=S)

            def gathered_experts():
                with pe.Fori(0, NGANG) as gang:
                    pe.wait_ge(q["sel_ready"], gang + 1)
                    for b in range(2):
                        if b == 0:
                            for j in range(8):
                                pe.wait_ge(bank_free[j], before_loop[j])
                        for kk in range(4):
                            k = 4 * b + kk
                            for i in range(NT):
                                last = pe.matmul(bank[b][:, kk * P:(kk + 1) * P], xn[:, i, k * P:(k + 1) * P],
                                                 sel[:, i, :], start=(i == 0), stop=(i == 1))
                        last.then_inc(q["gathered"], 1)
                    for i in range(NT):
                        last = pe.transpose(bank[3][:, (2 + i) * P:(3 + i) * P], wsel[:, i, :], ident)
                    last.then_inc(q["wsel_turned"], 1)
                    for k in range(KD):
                        pe.wait_ge(loaded[k], gang * 16 + 16 * ((NFRONT // FRING if k < FRING else 0) + 1))
                        if k % 4 == 0:
                            pe.wait_ge(q["gath_ready"], gang * 2 + (k // 4 + 1))
                        w = ring[:, k * SLOT:(k + 1) * SLOT].rearrange("p (e n) -> p e n", e=GANG)
                        for e in range(GANG):
                            last = pe.matmul(bank[2][CAP * e:CAP * (e + 1), :], gath[:, k, CAP * e:CAP * (e + 1)],
                                             w[:, e, :], start=(k == 0), stop=(k == KD - 1))
                            if k and e == 0:
                                last.then_inc(taken, 1)
                    last.then_inc(q["gate_up"], 1)
                    pe.wait_ge(q["ghid_ready"], gang + 1)
                    pe.wait_ge(q["wselT_ready"], gang + 1)
                    for f in range(2):
                        last = pe.transpose(bank[3][:, f * P:(f + 1) * P], ghid[:, f * P:(f + 1) * P], ident)
                        if f == 0:
                            last.then_inc(taken, 1)
                    last.then_inc(q["hid_turned"], 1)
                    for e in range(GANG):
                        pe.wait_ge(loaded[8 + e], gang * 16 + 16)
                    pe.wait_ge(q["ghidT_ready"], gang + 1)
                    for n in range(2):
                        for f in range(2):
                            for e in range(GANG):
                                w = ring[:, (8 + e) * SLOT:(9 + e) * SLOT].rearrange("p (f d) -> p f d", f=2)
                                last = pe.matmul(bank[4 + n][CAP * e:CAP * (e + 1), :], ghidT[:, f, CAP * e:CAP * (e + 1)],
                                                 w[:, f, n * 512:(n + 1) * 512], start=(f == 0), stop=(f == 1))
                        last.then_inc(q["downed"], 1)
                    for j in range(4):
                        n, i = j // 2, j % 2
                        if i == 0:
                            pe.wait_ge(q["ydown_ready"], gang * 2 + n + 1)
                        if j >= 2:
                            pe.wait_ge(q["summed"], gang * 4 + (j - 1))
                        last = pe.matmul(bank[6 + i][:, :], wselT[:, i, :], ydown[:, n * 512:(n + 1) * 512],
                                         start=True, stop=True)
                        last.then_inc(q["scattered"], 1)
                    pe.wait_ge(q["scattered"], gang * 4 + 4)
                    pe.sem_inc(taken, 4)
                    pe.wait_ge(q["summed"], gang * 4 + 4)

            def dense_experts():
                with pe.Fori(0, NGANG) as gang:
                    for c in range(GCH):
                        first = NFRONT // FRING if c < FRING else 0
                        pe.wait_ge(loaded[c], gang * 16 + 16 * (first + 1))
                    for i in range(NT):
                        slot = [ring[:, c * SLOT:(c + 1) * SLOT].rearrange("p (e n) -> p e n", e=GANG) for c in range(8)]
                        for e in range(GANG):
                            pe.wait_ge(bank_free[e], gang * 2 + (before_loop[e] + i))
                            for k in range(KD):
                                last = pe.matmul(bank[e][:, :], hT[:, k, i * P:(i + 1) * P], slot[k][:, e, :],
                                                 start=(k == 0), stop=(k == KD - 1))
                            last.then_inc(bank_full[e], 1)
                        for half in range(2):
                            pe.wait_ge(q["hid_ready"], gang * 8 + (4 * i + 2 * half + 2))
                            pe.wait_ge(bank_free[4 + half], gang * 2 + (before_loop[4 + half] + i))
                            for e in range(2):
                                for f in range(2):
                                    last = pe.transpose(bank[4 + half][:, (2 * e + f) * P:(2 * e + f + 1) * P],
                                                        hid[:, 2 * half + e, f * P:(f + 1) * P], ident)
                            last.then_inc(bank_full[4 + half], 1)
                        pe.wait_ge(q["hidT2_ready"], gang * 4 + (2 * i + 2))
                        for n in range(2):
                            pe.wait_ge(bank_free[6 + n], gang * 2 + (before_loop[6 + n] + i))
                            for e in range(GANG):
                                down = ring[:, (8 + e) * SLOT:(9 + e) * SLOT].rearrange("p (f d) -> p f d", f=2)
                                for f in range(2):
                                    last = pe.matmul(bank[6 + n][:, :], hidm[:, e, f, :], down[:, f, n * 512:(n + 1) * 512],
                                                     start=(e == 0 and f == 0), stop=(e == GANG - 1 and f == 1))
                            last.then_inc(bank_full[6 + n], 1)
                    pe.wait_ge(bank_full[7], gang * 2 + (before_loop[7] + 2))
                    pe.sem_inc(taken, GCH)

            with pe.If(most <= CAP):
                gathered_experts()
            with pe.Else():
                dense_experts()

        @block.gpsimd
        def _(pool):
            pool.memset(rawf[:, :], 0.0).then_inc(q["raw_zeroed"], 1)
            pool.memset(state[:, 0, :, :], 0.0).then_inc(q["state_zeroed"], 1)
            pool.wait_ge(q["small_loaded"], 32)

            def inverse_root(n, width):
                pool.wait_ge(q["rms_in"], n + 1)
                pool.tensor_tensor(stat[:, 8:8 + width], stat[:, 0:width], cn("neghalf")[:, 0:width], ALU.pow)\
                    .then_inc(q["root_ready"], 1)

            inverse_root(0, 2)
            level = cn("level").rearrange("p (n t) -> p n t", n=6)
            for i in range(NT):
                for grp in range(2):
                    turn_ = 2 * i + grp
                    for n in range(6):
                        if n == 0:
                            pool.wait_ge(q["amat_ready"], 8 * i + 8)
                            if grp:
                                full(pool, f"W{i}{grp - 1}4")
                        elif n == 1:
                            pool.wait_ge(q["z_ready"], 6 * turn_ + 1)
                        else:
                            full(pool, f"W{i}{grp}{n - 2}")
                        pool.tensor_tensor(lmask, amat[:, 4 * grp:4 * grp + 4, 0, :],
                                           like(level[:, n:n + 1, :], [P, 4, P]), ALU.mult)\
                            .then_inc(q["lmask_ready"], 1)
                inverse_root(1 + i, 8)
            inverse_root(3, 2)
            inverse_root(4, 2)

        @block.scalar
        def _(act):
            def copy(o, i_, scale=1.0):
                return act.activation(o, i_, ACT.Copy, scale=scale)

            def flat(o):
                return o[:, :].rearrange("p (a t) -> p a t", a=2)

            count = {}

            def give(ins, name, job):
                count[name] = count.get(name, 0) + 1
                ins.then_inc(q[name], 1)
                act.wait_ge(q[name], count[name])
                act.sem_inc(bank_free[plan[job][0]], 1)

            act.wait_ge(q["small_loaded"], 32)
            act.wait_ge(q["raw_zeroed"], 1)
            b0 = full(act, "lora_in")
            copy(raw[0:64, 0, 0, 1:S + 1], b0[0:64, 0:S])
            ins = copy(raw[0:96, 0, 1, 1:S + 1], b0[0:96, S:2 * S])
            give(ins, "raw_ready", "lora_in")
            b0 = full(act, "gates")
            give(act.activation(gate_t[:, :, :].rearrange("p i n -> p (i n)"), b0[:, 0:96], ACT.Tanh, scale=0.5), "gate_tanh", "gates")
            for n in range(2):
                b0 = full(act, f"pool{n}")
                give(copy(t1[:, 2 * n:2 * n + 2, :], flat(b0)), "u_ready", f"pool{n}")
            for c in range(1, 7):
                if c >= 2:
                    act.wait_ge(q["raw_used"], c - 1)
                b0 = full(act, f"rkv{c}")
                give(copy(raw[:, c % 2, :, 1:S + 1], flat(b0)), "raw_ready", f"rkv{c}")
                if c == 2:
                    act.wait_ge(q["mix_ready"], 1)
                    act.activation(mix[0:32, 12, :], mix[0:32, 12, :], ACT.Tanh).then_inc(q["lora_w_ready"], 1)
                    act.activation(mix[0:96, 13, :], mix[0:96, 13, :], ACT.Tanh, scale=0.5)\
                        .then_inc(q["lora_g_tanh"], 1)
            for n in range(8):
                b0 = full(act, f"bias{n}")
                give(copy(bias[:, 2 * n:2 * n + 2, :], flat(b0)), "bias_ready", f"bias{n}")
            act.wait_ge(q["halves_ready"], 1)
            act.wait_ge(q["pool_ready"], 1)
            for n in range(2):
                b0 = full(act, f"wup{n}")
                for m in range(2):
                    c = 2 * n + m
                    ins = act.activation(t1[:, c, :], b0[:, m * S:(m + 1) * S], ACT.Tanh, bias=halves[:, c:c + 1], scale=0.5)
                give(ins, "decay_tanh", f"wup{n}")
            for n in range(2):
                b0 = full(act, f"aup{n}")
                for m in range(2):
                    c = 2 * n + m
                    ins = act.activation(kf[:, c, :], b0[:, m * S:(m + 1) * S], ACT.Tanh, bias=halves[:, 4 + c:5 + c],
                                         scale=0.5)
                give(ins, "rate_tanh", f"aup{n}")
            for b, name in enumerate(("kc", "vc")):
                b0 = full(act, name)
                for gp in range(2):
                    src = flat(b0[64 * gp:64 * gp + 64, :])
                    copy(kshift[0:64, b, gp::2, :], src)
                    ins = copy(kshift[64:128, b, gp::2, 0:S - 1], src[:, :, 1:S])
                give(ins, "kshift_ready", name)
            act.wait_ge(q["kk_max"], 2)
            act.activation(t3[:, :, :], t3[:, :, :], ACT.Sqrt).then_inc(q["kk_root"], 1)
            act.wait_ge(q["log_ready"], 1)
            act.activation(t3[:, :, :], t2[:, :, :], ACT.Exp).then_inc(q["decay_exp"], 1)
            act.wait_ge(q["log_ready"], 2)
            act.activation(t1[:, :, :], t1[:, :, :], ACT.Exp).then_inc(q["decay_exp"], 1)
            act.activation(t2[:, :, :], t2[:, :, :], ACT.Exp, scale=-1.0).then_inc(q["decay_exp"], 1)
            for n in range(4):
                b0 = full(act, f"q{n}")
                give(copy(qT[:, 2 * n:2 * n + 2, :], flat(b0), scale=DH ** -0.5), "q_ready", f"q{n}")
            for b, name in enumerate(("mlp_k", "mlp_v")):
                b0 = full(act, name)
                give(copy(gx[:, b * 256:(b + 1) * 256], b0[0:60, 0:256]), "gx_ready", name)
            for b, name in enumerate(("ks", "kw")):
                b0 = full(act, name)
                for gp in range(2):
                    src = flat(b0[64 * gp:64 * gp + 64, :])
                    copy(kT[0:64, b, gp::2, :], src)
                    ins = copy(kT[64:128, b, gp::2, :], src)
                give(ins, "k_ready", name)
                if b == 0:
                    act.wait_ge(q["gelu_in"], 1)
                    act.activation(gy, gy, ACT.Tanh, scale=GELU_C).then_inc(q["gelu_tanh"], 1)
            b0 = full(act, "vs")
            give(copy(vtok[:, 0, :, :], flat(b0)), "v_ready", "vs")
            b0 = full(act, "hidT")
            give(copy(hidT, b0[:, 0:240].rearrange("p (f n) -> p f n", f=4)), "hidT_ready", "hidT")
            b0 = full(act, "vw")
            give(copy(vtok[:, 1, :, :], flat(b0)), "v_ready", "vw")
            b0 = full(act, "kcb")
            give(copy(kcb, b0[:, 0:60]), "cmp_kv_ready", "kcb")
            b0 = full(act, "vcb")
            give(copy(vcb, b0[0:NCMP, 0:256].rearrange("p (g v) -> p g v", g=NG)), "cmp_kv_ready", "vcb")

            def early(step):
                kind, i, which = step
                if kind == "turn":
                    for w_, dst in enumerate((btok, ktok)):
                        b0 = full(act, f"tok{i}{w_}")
                        give(copy(dst, b0[:, :]), "tok_ready", f"tok{i}{w_}")
                elif kind == "level":
                    name = "W%d%d%d" % (i, *which)
                    b0 = full(act, name)
                    give(copy(winv, b0[:, :].rearrange("p (h t) -> p h t", h=4)), "w_ready", name)
                elif kind == "solve":
                    b0 = full(act, f"w0{i}")
                    give(copy(rhs[:, :, 1, :], b0[:, :].rearrange("p (h v) -> p h v", h=RH)), "rhs_ready", f"w0{i}")

            def late(step):
                kind, i, which = step
                if kind == "turn":
                    b0 = full(act, f"tok{i}2")
                    give(copy(vrow, b0[:, :]), "tok_ready", f"tok{i}2")
                    b0 = full(act, f"atok{i}")
                    give(copy(rhs[:, :, 0, :], b0[:, :].rearrange("p (h v) -> p h v", h=RH)), "tok_ready", f"atok{i}")
                elif kind == "solve":
                    for n in range(2):
                        b0 = full(act, f"xu{i}{n}")
                        give(copy(rhs[:, 4 * n:4 * n + 4, :, :], b0[:, :].rearrange("p (h j v) -> p h j v", h=4, j=2)),
                             "xu_ready", f"xu{i}{n}")
                elif kind == "finish":
                    b0 = full(act, f"yT{i}")
                    for m in range(4):
                        ins = act.activation(yT[:, 4 + m, i * P:(i + 1) * P], b0[:, m * P:(m + 1) * P], ACT.Identity,
                                             bias=pr("gn_b")[:, m:m + 1], scale=pr("gn_w")[:, m:m + 1])
                    give(ins, "gn_ready", f"yT{i}")

            def exps(g, u):
                n = 6 * g + u
                act.wait_ge(q["exp_in"], n + 1)
                nb, w = (4, P) if u < 2 else (2, S)
                for b in range(nb):
                    pb = prob[:, n % 2, b * w:(b + 1) * w]
                    ins = act.activation(pb, pb, ACT.Exp, bias=astat[:, 8 * (n % 2) + b:8 * (n % 2) + b + 1],
                                         accum_out=astat[:, 16 + 8 * (n % 2) + b:17 + 8 * (n % 2) + b])
                ins.then_inc(q["exp_ready"], 1)

            def turned_compressed(g, i):
                nc_ = 7 if i == 0 else NCMP
                b0 = full(act, f"cT{g}{i}")
                give(copy(cprobT[0:nc_, i, :, :], b0[0:nc_, :].rearrange("p (h t) -> p h t", h=4)), "cprobT_ready",
                     f"cT{g}{i}")

            for step in RWKV_STEPS[0:BEFORE]:
                early(step)
                late(step)
            for u in range(4):
                act.wait_ge(q["cexp_in"], u + 1)
                act.activation(cprob[u], cprob[u], ACT.Exp).then_inc(q["cexp_ready"], 1)
            exps(0, 0)
            steps = iter(RWKV_STEPS[BEFORE:DURING])
            for n, (g, u) in enumerate(UNITS):
                if u == 0:
                    step = next(steps)
                    turned_compressed(g, 0)
                    early(step)
                    turned_compressed(g, 1)
                    late(step)
                step = next(steps)
                early(step)
                if n + 1 < len(UNITS):
                    exps(*UNITS[n + 1])
                b0 = full(act, f"pT{g}{u}")
                give(copy(probT[:, n % 2, :], b0[:, :]), "probT_ready", f"pT{g}{u}")
                late(step)

            act.wait_ge(q["nsa_ready"], NG)
            act.dma_start(tok[:, :, :], x.rearrange("(i p) d -> p i d", p=P)).then_inc(q["x_again"], 16)

            def first_gang(s):
                act.dma_start(ring[:, s * SLOT:(s + 1) * SLOT], experts[0, s]).then_inc(loaded[s], 16)

            first_gang(11)
            for j in range(NGATE):
                if j in beside:
                    early(beside[j])
                    if j < NGATE - 1:
                        late(beside[j])
                b0 = full(act, f"mg{j}")
                for m in range(2):
                    c = 8 + 8 * (j % 3) + 2 * (j // 3) + m
                    ins = act.activation(gsig[j][:, m, :], b0[:, m * S:(m + 1) * S], ACT.Tanh,
                                         bias=halves[:, c:c + 1], scale=0.5)
                give(ins, "gsig_ready", f"mg{j}")
            late(beside[NGATE - 1])

            act.wait_ge(q["yrw_ready"], NT)
            first_gang(8)
            first_gang(9)
            act.wait_ge(q["gated"], NGATE)
            for s in (6, 7, 10):
                first_gang(s)
            act.wait_ge(q["merged_ready"], 4)
            act.dma_start(gfin, g_final).then_inc(q["gfin_loaded"], 16)

            act.wait_ge(q["router_in"], 1)
            act.activation(rt("ge"), rt("ge"), ACT.Exp).then_inc(q["router_exp"], 1)
            act.wait_ge(q["router_in"], 2)
            act.activation(rt("w2"), rt("w2"), ACT.Exp).then_inc(q["router_exp"], 1)

            act.wait_ge(q["crowd_ready"], 1)
            most = act.value_load(crowd[0:1, 0:1], min_val=0, max_val=S)

            def gathered_experts():
                with act.Fori(0, NGANG) as gang:
                    act.wait_ge(q["wsel_turned"], gang + 1)
                    copy(wselT, bank[3][:, 2 * P:4 * P].rearrange("p (i t) -> p i t", i=2)).then_inc(q["wselT_ready"], 1)
                    act.wait_ge(q["gate_up"], gang + 1)
                    act.activation(gtanh, bank[2][:, 0:DE], ACT.Tanh, scale=0.5).then_inc(q["gtanh_ready"], 1)
                    act.wait_ge(q["hid_turned"], gang + 1)
                    copy(ghidT, bank[3][:, 0:2 * P].rearrange("p (f s) -> p f s", f=2)).then_inc(q["ghidT_ready"], 1)
                    for n in range(2):
                        act.wait_ge(q["downed"], gang * 2 + n + 1)
                        copy(ydown[:, n * 512:(n + 1) * 512], bank[4 + n][:, :]).then_inc(q["ydown_ready"], 1)

            def dense_experts():
                with act.Fori(0, NGANG) as gang:
                    for i in range(NT):
                        for e in range(GANG):
                            act.wait_ge(bank_full[e], gang * 2 + (before_loop[e] + i + 1))
                            act.activation(gsi[:, e, :], bank[e][:, 0:DE], ACT.Tanh, scale=0.5).then_inc(q["silu_tanh"], 1)
                        for half in range(2):
                            act.wait_ge(bank_full[4 + half], gang * 2 + (before_loop[4 + half] + i + 1))
                            copy(hidm[:, 2 * half:2 * half + 2, :, :],
                                 bank[4 + half][:, :].rearrange("p (e f t) -> p e f t", e=2, f=2))\
                                .then_inc(q["hidT2_ready"], 1)

            with act.If(most <= CAP):
                gathered_experts()
            with act.Else():
                dense_experts()

        @block.vector
        def _(dve):
            chain = chainer(dve, "dve_chain")

            def flat(o):
                return o[:, :].rearrange("p (a t) -> p a t", a=2)

            def tt(o, a, b, op):
                return dve.tensor_tensor(o, a, b, op)

            def ts(o, a, s1, s2, op0, op1=None):
                return dve.tensor_scalar(o, a, s1, s2, op0, op1) if op1 is not None else \
                    dve.tensor_scalar(o, a, s1, None, op0)

            def stt(o, a, s1, b, op0, op1):
                return dve.scalar_tensor_tensor(out=o, in0=a, scalar=s1, in1=b, op0=op0, op1=op1)

            roots = [0]

            def normalise(src):
                for i in range(NT):
                    chain(dve.tensor_tensor_reduce(t1[:, :, :].rearrange("p c t -> p (c t)"), src[:, i, :], src[:, i, :],
                                                   1.0, 0.0, ALU.mult, ALU.add, stat[:, 16 + i:17 + i]))
                roots[0] += 1
                chain(ts(stat[:, 0:2], stat[:, 16:18], 1.0 / D, 1e-6, ALU.mult, ALU.add), "rms_in")
                dve.wait_ge(q["root_ready"], roots[0])
                for i in range(NT):
                    chain(ts(xn[:, i, :], src[:, i, :], stat[:, 8 + i:9 + i], None, ALU.mult), "xn_ready")

            def to_hT(jobs, gain):
                for n in range(4):
                    i, k0 = n // 2, (n % 2) * 4
                    b0 = full(dve, f"{jobs}{n}")
                    chain(tt(hT[:, k0:k0 + 4, i * P:(i + 1) * P], b0[:, :].rearrange("p (k t) -> p k t", k=4),
                             like(pr(gain)[:, k0:k0 + 4, None], [P, 4, P]), ALU.mult), "hT_ready")
                    dve.sem_inc(bank_free[plan[f"{jobs}{n}"][0]], 1)

            dve.wait_ge(q["x_loaded"], 16)
            dve.wait_ge(q["small_loaded"], 32)
            for lo, hi, name in ((0, 4, "w0"), (4, 8, "a0"), (8, 32, "b_merge")):
                ins = ts(halves[:, lo:hi], pr(name), 0.5, None, ALU.mult)
                chain(ins, "halves_ready" if name == "b_merge" else None)
            normalise(tok)
            to_hT("xT", "g_mix")
            b0 = full(dve, "brow")
            ins = dve.tensor_copy(arbk[0:NH, 0:2, :].rearrange("p a b -> p (a b)")[:, 0:384], b0[0:NH, 0:384])
            chain(ins, "win_row")
            dve.sem_inc(bank_free[plan["brow"][0]], 1)

            def shift(rows, c, j, tiles):
                r_ = raw[rows, c % 2, j, :]
                chain(tt(mix[rows, tiles, :], r_[:, :, 0:S], r_[:, :, 1:S + 1], ALU.subtract))
                for k in range(tiles.stop - tiles.start):
                    t = tiles.start + k
                    chain(stt(mix[rows, t, :], mix[rows, t, :], pr("mu")[rows, t:t + 1], r_[:, k, 1:S + 1],
                              ALU.mult, ALU.add))

            dve.wait_ge(q["raw_ready"], 1)
            shift(slice(0, 64), 0, slice(0, 1), slice(12, 13))
            shift(slice(0, 96), 0, slice(1, 2), slice(13, 14))
            dve.sem_inc(q["raw_used"], 1)
            dve.sem_inc(q["mix_ready"], 1)
            dve.wait_ge(q["gate_tanh"], 1)
            ins = ts(gate_t[:, :, :].rearrange("p i n -> p (i n)"), gate_t[:, :, :].rearrange("p i n -> p (i n)"),
                     0.5, 0.5, ALU.mult, ALU.add)
            chain(ins, "gates_ready")

            dve.wait_ge(q["u_ready"], 2)
            sums = [None, t2, t3, t2, t3]
            for lv in range(1, 5):
                w = 2 ** (lv - 1)
                src, dst = (t1 if lv == 1 else sums[lv - 1]), sums[lv]
                gs = slice(lv - 1, 4)
                chain(dve.tensor_copy(dst[:, gs, 0:w], src[:, gs, 0:w]), hold=False)
                chain(tt(dst[:, gs, w:S], src[:, gs, w:S], src[:, gs, 0:S - w], ALU.add))
            cnt = cn("count").rearrange("p (g t) -> p g t", g=4)
            for gi in range(4):
                src = sums[gi + 1]
                chain(stt(yT[:, gi, :], src[:, gi, :], 0.5 ** (gi + 1), t1[:, gi, :], ALU.mult, ALU.subtract))
                chain(tt(src[:, gi, 0:16], src[:, gi, 0:16], cnt[:, gi, :], ALU.mult))
                ins = tt(yT[:, gi, 0:16], src[:, gi, 0:16], t1[:, gi, 0:16], ALU.subtract)
                chain(ins, "pool_ready" if gi == 3 else None)

            for c in range(1, 7):
                dve.wait_ge(q["raw_ready"], c + 1)
                shift(slice(0, P), c, slice(0, 2), slice(2 * c - 2, 2 * c))
                dve.sem_inc(q["raw_used"], 1)
            dve.wait_ge(q["lora_g_tanh"], 1)
            chain(ts(mix[0:96, 13, :], mix[0:96, 13, :], 0.5, 0.5, ALU.mult, ALU.add), "lora_g_ready")
            for n in range(2):
                b0 = full(dve, f"poolmix{n}")
                chain(tt(yT[:, 2 * n:2 * n + 2, :], flat(b0),
                         like(pr("pool_scale")[:, 2 * n:2 * n + 2, None], [P, 2, S]), ALU.mult), "pool_out")
                dve.sem_inc(bank_free[plan[f"poolmix{n}"][0]], 1)

            dve.wait_ge(q["bias_ready"], 8)
            for m in range(4):
                chain(ts(bf[:, m, :], mix[:, m, :], pr("k_k")[:, m:m + 1], None, ALU.mult), hold=(m == 3))
            chain(tt(t3[:, :, :], bf, bf, ALU.mult), "kk_sq_ready")

            dve.wait_ge(q["decay_tanh"], 2)
            chain(ts(t1[:, :, :], t1[:, :, :], 1.0, -0.5 * DECAY, ALU.add, ALU.mult))
            dve.wait_ge(q["rate_tanh"], 2)
            for m in range(4):
                for c in range(NCH):
                    cs = slice(c * CH, (c + 1) * CH)
                    chain(dve.tensor_tensor_scan(t2[:, m, cs], cn("ones")[:, 0:CH], t1[:, m, cs], 0.0, ALU.mult, ALU.add),
                          hold=(m == 3 and c == 3))
            for b, name in enumerate(("kc", "vc")):
                dve.wait_ge(q["kshift_ready"], b + 1)
                base = kshift[:, b, :, :]
                src = bass.AP(base.tensor, base.offset, [list(base.ap[0]), [2, 16], [S, NG], [CSTRIDE, NCMP]])
                pos = pr("pos_k" if b == 0 else "pos_v")
                chain(tt(xcmp[:, b, :, :].rearrange("p j (g n) -> p j g n", g=NG), src,
                         like(pos[:, :, None, None], [P, 16, NG, NCMP]), ALU.add), "xcmp_ready")
            for n in range(2):
                b0 = full(dve, f"kk{n}")
                ins = ts(t3[:, 2 * n:2 * n + 2, :], flat(b0), 1e-24, None, ALU.max)
                chain(ins, "kk_max")
                dve.sem_inc(bank_free[plan[f"kk{n}"][0]], 1)
            dve.wait_ge(q["kk_root"], 1)
            chain(dve.reciprocal(t3[:, :, :], t3[:, :, :]))
            chain(tt(bf, bf, t3[:, :, :], ALU.mult))
            dve.sem_inc(q["log_ready"], 1)
            ins = tt(t1[:, :, :], t2[:, :, :], t1[:, :, :], ALU.subtract)
            chain(ins)
            dve.sem_inc(q["log_ready"], 1)
            chain(ts(kf, kf, 0.5, 0.5, ALU.mult, ALU.add))
            dve.wait_ge(q["decay_exp"], 3)
            a_f = ar[:, :, :, 0, :]
            r_f = ar[:, :, :, 1, :]

            def tiles(t):
                return t.rearrange("p m (i t) -> p m i t", i=2)

            chain(stt(a_f.rearrange("p m i t -> p (m i) t"), bf.rearrange("p m (i t) -> p (m i) t", i=2), -1.0,
                      t1[:, :, :].rearrange("p m (i t) -> p (m i) t", i=2), ALU.mult, ALU.mult), hold=False)
            chain(tt(r_f.rearrange("p m i t -> p (m i) t"), mix[:, 4:8, :].rearrange("p m (i t) -> p (m i) t", i=2),
                     t3[:, :, :].rearrange("p m (i t) -> p (m i) t", i=2), ALU.mult))
            chain(dve.tensor_copy(pend, t3[:, :, :].rearrange("p m (c t) -> p m c t", c=NCH)[:, :, :, CH - 1]))
            chain(tt(bf, bf, kf, ALU.mult))
            chain(tt(bf, bf, t2[:, :, :], ALU.mult))
            for m in range(4):
                chain(ts(kf[:, m, :], kf[:, m, :], -1.0, pr("k_a")[:, m:m + 1], ALU.add, ALU.mult), hold=(m == 3))
            chain(stt(kf, kf, 1.0, mix[:, 0:4, :], ALU.add, ALU.mult))
            for m in range(4):
                ins = stt(mix[:, 4 + m, :], mix[:, 4 + m, :], pr("r_k")[:, m:m + 1], kf[:, m, :], ALU.mult, ALU.mult)
                chain(ins, "bonus_ready" if m == 3 else None)
            chain(tt(kf, kf, t2[:, :, :], ALU.mult), "rwkv_ready")
            dve.wait_ge(q["gx_ready"], 2)
            chain(tt(gy, gx, gx, ALU.mult))
            chain(ts(gy, gy, 0.044715, 1.0, ALU.mult, ALU.add))
            chain(tt(gy, gy, gx, ALU.mult), "gelu_in")
            dve.wait_ge(q["gelu_tanh"], 1)
            chain(stt(gy, gy, 1.0, gx, ALU.add, ALU.mult))
            chain(ts(gx, gy, 0.5, None, ALU.mult), "gelu_ready")

            for n in range(2):
                b0 = full(dve, f"bonus{n}")
                chain(tt(mix[:, 4 + 2 * n:6 + 2 * n, :], flat(b0), mix[:, 8 + 2 * n:10 + 2 * n, :], ALU.mult))
                dve.sem_inc(bank_free[plan[f"bonus{n}"][0]], 1)

            def attended(g):
                b0 = full(dve, f"o{g}")
                chain(dve.tensor_copy(yT[:, 8 + 2 * g:10 + 2 * g, :], flat(b0)), "nsa_ready")
                dve.sem_inc(bank_free[plan[f"o{g}"][0]], 1)

            for u in range(4):
                i, p = u // 2, u % 2
                nc_ = 7 if i == 0 else NCMP
                b0 = full(dve, f"cs{u}")
                cp = cprob[u]
                first = CBLOCK - 1 + (P if i == 0 else 0)
                chain(tt(cp, b0[:, 0:8 * nc_].rearrange("p (m n) -> p m n", m=8),
                         bias[:, p::2, first:first + CSTRIDE * (nc_ - 1) + 1:CSTRIDE], ALU.add))
                dve.sem_inc(bank_free[plan[f"cs{u}"][0]], 1)
                mx = astat[:, 32:40]
                chain(dve.tensor_reduce(mx, cp, AXX, ALU.max))
                chain(ts(mx, mx, -1.0e20, None, ALU.max))
                chain(tt(cp, cp, like(mx[:, :, None], [P, 8, nc_]), ALU.subtract), "cexp_in")
            for u in range(4):
                i, p = u // 2, u % 2
                nc_ = 7 if i == 0 else NCMP
                cp = cprob[u]
                dve.wait_ge(q["cexp_ready"], u + 1)
                sm = astat[:, 32:40]
                chain(dve.tensor_reduce(sm, cp, AXX, ALU.add))
                chain(ts(sm, sm, 1e-30, None, ALU.max))
                chain(dve.reciprocal(sm, sm))
                chain(tt(sm, sm, gate_t[:, i, 3 * p::6], ALU.mult))
                chain(tt(cp, cp, like(sm[:, :, None], [P, 8, nc_]), ALU.mult), "cprob_ready")

            def logits(g, u):
                n = 6 * g + u
                p = u % 2
                b0 = full(dve, f"s{g}{u}")
                if n >= 2:
                    b, cnt_ = plan[f"pT{(n - 2) // 6}{(n - 2) % 6}"]
                    dve.wait_ge(bank_full[b], cnt_ + 1)
                h0 = 4 * g + p
                if u < 2:
                    for br in range(2):
                        o = prob[:, n % 2, br * 256:(br + 1) * 256].rearrange("p (h k) -> p h k", h=2)
                        chain(tt(o, b0[:, br * 256:(br + 1) * 256].rearrange("p (h k) -> p h k", h=2),
                                 bias[:, h0:h0 + 3:2, P:2 * P], ALU.add), hold=(br == 1))
                    nb, w = 4, P
                else:
                    o = prob[:, n % 2, :].rearrange("p (h k) -> p h k", h=2)
                    chain(tt(o, b0[:, :].rearrange("p (h k) -> p h k", h=2), bias[:, h0:h0 + 3:2, :], ALU.add))
                    nb, w = 2, S
                dve.sem_inc(bank_free[plan[f"s{g}{u}"][0]], 1)
                mx = astat[:, 8 * (n % 2):8 * (n % 2) + nb]
                chain(dve.tensor_reduce(mx, prob[:, n % 2, :].rearrange("p (b k) -> p b k", b=nb), AXX, ALU.max))
                chain(ts(mx, mx, -1.0, None, ALU.mult), "exp_in")

            def gated(g, u):
                n = 6 * g + u
                p = u % 2
                dve.wait_ge(q["exp_ready"], n + 1)
                nb, w = (4, P) if u < 2 else (2, S)
                sm = astat[:, 16 + 8 * (n % 2):16 + 8 * (n % 2) + nb]
                chain(dve.reciprocal(sm, sm))
                c0 = 12 * g + 3 * p + 1
                if u < 2:
                    for br in range(2):
                        chain(tt(sm[:, 2 * br:2 * br + 2], sm[:, 2 * br:2 * br + 2],
                                 gate_t[:, 0, c0 + br:c0 + br + 7:6], ALU.mult), hold=(br == 1))
                else:
                    br = (u - 2) // 2
                    chain(tt(sm, sm, gate_t[:, 1, c0 + br:c0 + br + 7:6], ALU.mult))
                pv = prob[:, n % 2, :].rearrange("p (b k) -> p b k", b=nb)
                chain(tt(pv, pv, like(sm[:, :, None], [P, nb, w]), ALU.mult), "prob_ready")

            def rwkv(step):
                kind, i, which = step
                if kind == "products":
                    for h in range(4 * which, 4 * which + 4):
                        b0 = full(dve, f"A{i}{h}")
                        chain(tt(amat[:, h, :, :].rearrange("p j t -> p (j t)"), b0[:, :], cn("intra"), ALU.mult),
                              "amat_ready")
                        dve.sem_inc(bank_free[plan[f"A{i}{h}"][0]], 1)
                elif kind == "seed":
                    grp = which[0]
                    dve.wait_ge(q["lmask_ready"], 6 * (2 * i + grp) + 1)
                    chain(tt(zinv[grp], lmask, like(ident[:, None, :], [P, 4, P]), ALU.add), "z_ready")
                    b0 = full(dve, f"XZ{i}{grp}")
                    chain(dve.tensor_copy(xinv, b0[:, :].rearrange("p (h t) -> p h t", h=4)), "x_ready")
                    dve.sem_inc(bank_free[plan[f"XZ{i}{grp}"][0]], 1)
                elif kind == "level":
                    grp, n = which
                    z = zinv[grp]
                    if n < 4:
                        b0 = full(dve, f"X{i}{grp}{n}")
                        chain(tt(xinv, xinv, b0[:, :].rearrange("p (h t) -> p h t", h=4), ALU.add), "x_ready")
                        dve.sem_inc(bank_free[plan[f"X{i}{grp}{n}"][0]], 1)
                    b0 = full(dve, f"Z{i}{grp}{n}")
                    chain(tt(z, z, b0[:, :].rearrange("p (h t) -> p h t", h=4), ALU.add), "z_ready")
                    dve.sem_inc(bank_free[plan[f"Z{i}{grp}{n}"][0]], 1)
                elif kind == "local":
                    for n in range(2):
                        b0 = full(dve, f"rx{i}{n}")
                        rv = ar[:, 2 * n:2 * n + 2, i, 1, :]
                        chain(tt(rv, rv, b0[:, 0:2 * P].rearrange("p (m t) -> p m t", m=2), ALU.add), "rx_ready")
                        dve.sem_inc(bank_free[plan[f"rx{i}{n}"][0]], 1)
                    for c in range(2):
                        b0 = full(dve, f"fc{i}{c}")
                        bv = b0[:, :].rearrange("p (m j v) -> p m j v", m=4, j=2)
                        chain(tt(fc[:, c, :, 0, :], bv[:, :, 0, :], like(cn("eye64")[:, None, :], [P, 4, DH]), ALU.add),
                              hold=False)
                        chain(dve.tensor_copy(fc[:, c, :, 1, :], bv[:, :, 1, :]), "fc_ready")
                        dve.sem_inc(bank_free[plan[f"fc{i}{c}"][0]], 1)
                elif kind == "scan":
                    n = 2 * i + which
                    if n < NCH - 1:
                        b0 = full(dve, f"st{i}{which}")
                        sv = state[:, (n + 1) % 2, :, :]
                        du = fc[:, which, :, 1, :]
                        chain(tt(du, b0[:, 0:4 * DH].rearrange("p (m v) -> p m v", m=4), du, ALU.add))
                        dve.sem_inc(bank_free[plan[f"st{i}{which}"][0]], 1)
                        chain(tt(sv, du, like(pend[:, :, n:n + 1], [P, 4, DH]), ALU.mult), "state_ready")
                    if which == 1:
                        group_norm(i)
                elif kind == "finish":
                    dve.wait_ge(q["gn_ready"], i + 1)
                    yr = yT[:, 4:8, i * P:(i + 1) * P]
                    chain(tt(yr, yr, bonus[:, :, i * P:(i + 1) * P], ALU.add))
                    b0 = full(dve, f"gup{i}")
                    chain(tt(yr, yr, b0[:, :].rearrange("p (m t) -> p m t", m=4), ALU.mult), "yrw_ready")
                    dve.sem_inc(bank_free[plan[f"gup{i}"][0]], 1)

            def group_norm(i):
                yv = ynorm.rearrange("p (m j v) -> p m j v", m=4, j=2)
                for p in range(2):
                    b0 = full(dve, f"y{i}{p}")
                    chain(dve.tensor_copy(yv[:, :, p, :], b0[:, 0:4 * DH].rearrange("p (m v) -> p m v", m=4)))
                    dve.sem_inc(bank_free[plan[f"y{i}{p}"][0]], 1)
                yh = ynorm.rearrange("p (h v) -> p h v", h=RH)
                ys = ysq.rearrange("p (h v) -> p h v", h=RH)
                mean = stat[:, 16:24]
                chain(dve.tensor_reduce(mean, yh, AXX, ALU.add))
                chain(ts(mean, mean, 1.0 / DH, None, ALU.mult))
                chain(tt(yh, yh, like(mean[:, :, None], [P, RH, DH]), ALU.subtract))
                chain(tt(ys, yh, yh, ALU.mult))
                chain(dve.tensor_reduce(mean, ys, AXX, ALU.add))
                roots[0] += 1
                chain(ts(stat[:, 0:8], mean, 1.0 / DH, 64e-5, ALU.mult, ALU.add), "rms_in")
                dve.wait_ge(q["root_ready"], roots[0])
                chain(tt(yh, yh, like(stat[:, 8:16][:, :, None], [P, RH, DH]), ALU.mult), "ynorm_ready")

            logits(0, 0)
            logits(0, 1)
            gated(0, 0)
            steps = iter(RWKV_STEPS[BEFORE:DURING])
            for n, (g, u) in enumerate(UNITS):
                if u == 0:
                    if g:
                        attended(g - 1)
                    rwkv(next(steps))
                rwkv(next(steps))
                if n + 1 < len(UNITS):
                    gated(*UNITS[n + 1])
                if n + 2 < len(UNITS):
                    logits(*UNITS[n + 2])
            attended(NG - 1)
            for j in sorted(beside):
                rwkv(beside[j])

            for n in range(4):
                for b in range(3):
                    dve.wait_ge(q["gsig_ready"], 3 * n + b + 1)
                    b0 = full(dve, f"mb{n}{b}")
                    o = macc if b == 0 else mtmp
                    chain(stt(o, gsig[3 * n + b], 1.0, flat(b0), ALU.add, ALU.mult), "gated")
                    dve.sem_inc(bank_free[plan[f"mb{n}{b}"][0]], 1)
                    if b == 1:
                        chain(tt(macc, macc, mtmp, ALU.add))
                    if b == 2:
                        chain(tt(merged[:, 2 * n:2 * n + 2, :], macc, mtmp, ALU.add), "merged_ready")
            dve.wait_ge(q["x_again"], 16)
            for n in range(4):
                b0 = full(dve, f"out{n}")
                o = tok[:, :, n * 256:(n + 1) * 256]
                chain(stt(o, flat(b0), 0.5, o, ALU.mult, ALU.add))
                dve.sem_inc(bank_free[plan[f"out{n}"][0]], 1)
            normalise(tok)
            to_hT("hT2", "g_ffn")

            b0 = full(dve, "router")
            lg = rt("lg")
            chain(dve.tensor_copy(lg, b0[:, 0:72].rearrange("p (i n) -> p i n", i=2)))
            dve.sem_inc(bank_free[plan["router"][0]], 1)
            fall = cn("falling")

            def first_best(values, width, best, hot, tmp):
                shape = [P, 2, width]
                f = like(fall[:, None, 0:width], shape)
                chain(dve.tensor_reduce(best, values, AXX, ALU.max))
                chain(tt(hot, values, like(best[:, :, None], shape), ALU.is_equal))
                chain(tt(hot, hot, f, ALU.mult))
                chain(dve.tensor_reduce(tmp, hot, AXX, ALU.max))
                chain(tt(hot, f, like(tmp[:, :, None], shape), ALU.is_equal))

            gl, el = lg[:, :, 0:NGRP], lg[:, :, NGRP:NGRP + E]
            first_best(gl, NGRP, rt("gm"), rt("gh"), rt("tmp"))
            chain(tt(rt("ge"), gl, like(rt("gm")[:, :, None], [P, 2, NGRP]), ALU.subtract), "router_in")
            chain(ts(rt("gh"), rt("gh"), 1.0, 1.0e30, ALU.subtract, ALU.mult))
            el4 = el.rearrange("p i (g e) -> p i g e", g=NGRP)
            chain(tt(el4, el4, like(rt("gh")[:, :, :, None], [P, 2, NGRP, EPG]), ALU.add))
            first_best(el, E, rt("m1"), rt("h1"), rt("tmp"))
            chain(stt(el, rt("h1"), -2.0e30, el, ALU.mult, ALU.add))
            first_best(el, E, rt("m2"), rt("h2"), rt("tmp"))
            chain(tt(rt("w2"), rt("m2"), rt("m1"), ALU.subtract), "router_in")
            dve.wait_ge(q["router_exp"], 2)
            chain(dve.tensor_reduce(rt("tmp"), rt("ge"), AXX, ALU.add))
            chain(ts(rt("w1"), rt("w2"), 1.0, None, ALU.add))
            chain(tt(rt("w1"), rt("w1"), rt("tmp"), ALU.mult))
            chain(dve.reciprocal(rt("w1"), rt("w1")))
            chain(tt(member, rt("h1"), rt("h2"), ALU.add), "member_ready")
            chain(ts(rt("w1"), rt("w1"), 0.5, None, ALU.mult))
            chain(tt(rt("w2"), rt("w2"), rt("w1"), ALU.mult))
            chain(tt(rt("h1"), rt("h1"), like(rt("w1")[:, :, None], [P, 2, E]), ALU.mult))
            chain(tt(rt("h2"), rt("h2"), like(rt("w2")[:, :, None], [P, 2, E]), ALU.mult))
            chain(dve.memset(small[:, 112:112 + 2 * (E + GANG)], 0.0))
            chain(tt(combine[:, :, 0:E], rt("h1"), rt("h2"), ALU.add), "combine_ready")
            b0 = full(dve, "places")
            chain(dve.memset(place[:, :, :], 99.0))
            at = place[:, :, 0:E]
            chain(stt(at, b0[:, 0:2 * E].rearrange("p (i e) -> p i e", i=2), 99.0 - CAP, member, ALU.add, ALU.mult))
            chain(ts(at, at, -1.0, 99.0, ALU.mult, ALU.add))
            chain(dve.tensor_reduce(crowd[:, :], b0[:, 2 * E:3 * E], AXX, ALU.max), "crowd_ready")
            dve.sem_inc(bank_free[plan["places"][0]], 1)
            most = dve.value_load(crowd[0:1, 0:1], min_val=0, max_val=S)

            def seat(gang):
                slots = like(cn("falling")[:, None, 0:CAP], [P, GANG, CAP])
                for i in range(NT):
                    o = sel[:, i, :].rearrange("p (e s) -> p e s", e=GANG)
                    tt(o, slots, like(place[:, i, bass.ds(gang * GANG, GANG)][:, :, None], [P, GANG, CAP]),
                       ALU.is_equal).then_inc(q["moe_ready"], 1)

            def weigh_seats(gang):
                for i in range(NT):
                    o = sel[:, i, :].rearrange("p (e s) -> p e s", e=GANG)
                    w = wsel[:, i, :].rearrange("p (e s) -> p e s", e=GANG)
                    ins = tt(w, o, like(combine[:, i, bass.ds(gang * GANG, GANG)][:, :, None], [P, GANG, CAP]), ALU.mult)
                    if i == 1:
                        ins.then_inc(q["sel_ready"], 1)

            def gathered_experts():
                seat(0)
                dve.wait_ge(q["moe_ready"], 2)
                weigh_seats(0)
                with dve.Fori(0, NGANG) as gang:
                    for b in range(2):
                        dve.wait_ge(q["gathered"], gang * 2 + b + 1)
                        tt(gath[:, 4 * b:4 * b + 4, :], bank[b][:, :].rearrange("p (k s) -> p k s", k=4),
                           like(pr("g_ffn")[:, 4 * b:4 * b + 4, None], [P, 4, P]), ALU.mult).then_inc(q["gath_ready"], 1)
                    dve.wait_ge(q["gtanh_ready"], gang + 1)
                    stt(ghid, gtanh, 1.0, bank[2][:, 0:DE], ALU.add, ALU.mult).then_inc(q["moe_ready"], 1)
                    dve.wait_ge(q["moe_ready"], gang * 3 + 3)
                    tt(ghid, ghid, bank[2][:, DE:2 * DE], ALU.mult).then_inc(q["ghid_ready"], 1)
                    dve.wait_ge(q["wsel_turned"], gang + 1)
                    seat(gang + 1)
                    dve.wait_ge(q["moe_ready"], gang * 3 + 5)
                    weigh_seats(gang + 1)
                    for j in range(4):
                        n, i = j // 2, j % 2
                        dve.wait_ge(q["scattered"], gang * 4 + j + 1)
                        o = tok[:, i, n * 512:(n + 1) * 512]
                        tt(o, o, bank[6 + i][:, :], ALU.add).then_inc(q["summed"], 1)

            def dense_experts():
                loop_chain = q["moe_ready"]
                with dve.Fori(0, NGANG) as gang:
                    step = 0
                    for i in range(NT):
                        for e in range(GANG):
                            dve.wait_ge(q["silu_tanh"], gang * 8 + (4 * i + e + 1))
                            h_ = hid[:, e, :]
                            for k in range(2):
                                if k == 0:
                                    ins = stt(h_, gsi[:, e, :], 1.0, bank[e][:, 0:DE], ALU.add, ALU.mult)
                                else:
                                    ins = tt(h_, h_, bank[e][:, DE:2 * DE], ALU.mult)
                                ins.then_inc(loop_chain, 1)
                                step += 1
                                dve.wait_ge(loop_chain, gang * 20 + step)
                            dve.sem_inc(bank_free[e], 1)
                            ts(h_, h_, combine[:, i, bass.ds(gang * GANG + e, 1)], None, ALU.mult).then_inc(q["hid_ready"], 1)
                        for half in range(2):
                            dve.wait_ge(q["hidT2_ready"], gang * 4 + (2 * i + half + 1))
                            dve.sem_inc(bank_free[4 + half], 1)
                        for n in range(2):
                            dve.wait_ge(bank_full[6 + n], gang * 2 + (before_loop[6 + n] + i + 1))
                            o = tok[:, i, n * 512:(n + 1) * 512]
                            tt(o, o, bank[6 + n][:, :], ALU.add).then_inc(loop_chain, 1)
                            step += 1
                            dve.wait_ge(loop_chain, gang * 20 + step)
                            dve.sem_inc(bank_free[6 + n], 1)
                    assert step == 20

            with dve.If(most <= CAP):
                gathered_experts()
            with dve.Else():
                dense_experts()
            chain(dve.memset(stat[:, 24:25], 0.0))

            normalise(tok)
            dve.wait_ge(q["gfin_loaded"], 16)
            res = hT[:, :, :].rearrange("p c t -> p (c t)").rearrange("p (i d) -> p i d", i=2)
            for i in range(NT):
                chain(tt(res[:, i, :], xn[:, i, :], gfin, ALU.mult), "final_ready")


def kernel(**inputs):
    import concourse.bacc as _bacc
    from concourse.bass_utils import run_bass_kernel_spmd as _run

    a = {k: np.asarray(v) for k, v in inputs.items()}

    def channels(v):
        return v.reshape(-1, P).T

    par = np.zeros((P, NPARAMS), np.float32)

    def put(name, v):
        lo, hi = PARAMS[name]
        par[:v.shape[0], lo:hi] = v

    rk, kk, vv = (slice(n * RW, (n + 1) * RW) for n in range(3))
    lo_ = 3 * RW
    mu = a["rw_mu"][0]
    put("g_mix", channels(a["norm_mix"][0]))
    put("g_ffn", channels(a["norm_ffn"][0]))
    put("mu", np.concatenate([channels(mu[kk]), channels(mu[rk]), channels(mu[vv]),
                              np.pad(mu[lo_:lo_ + 64], (0, 64))[:, None], np.pad(mu[lo_ + 64:], (0, 32))[:, None]], 1))
    for name, key in (("w0", "rw_w0"), ("a0", "rw_a0"), ("k_k", "rw_k_k"), ("k_a", "rw_k_a"), ("r_k", "rw_r_k"),
                      ("gn_w", "rw_gn_w"), ("gn_b", "rw_gn_b"), ("pool_scale", "pool_scale"), ("b_merge", "b_merge")):
        put(name, channels(a[key][0].reshape(-1)))
    put("lora_up", np.concatenate([a["rw_w_up"][0], a["rw_a_up"][0]]))
    put("g_up", a["rw_g_up"][0])
    put("pool_w", a["pool_w"][0].transpose(1, 0, 2).reshape(P, -1))
    for b in "kv":
        put(f"w2_{b}", a[f"cmp_w2_{b}"][0].reshape(2, P, DH).transpose(1, 0, 2).reshape(P, -1))
        put(f"pos_{b}", a[f"cmp_pos_{b}"][0].reshape(16, P).T)
    put("rel", np.concatenate([a["rel_bias"], np.ones((1, NH), np.float32)]))
    put("b_router", np.concatenate([a["b_router_grp"][0], a["b_router_exp"][0]])[None])

    front = np.zeros((NFRONT, P, SLOT), np.float32)

    def chunk(n, w):
        c = w.shape[1]
        front[n].reshape(P, KD, -1)[:, :, :c] = w.reshape(KD, P, c).transpose(1, 0, 2)

    w_in = a["w_in"][0]
    r0 = PW
    n0 = PW + 3 * RW + 160
    chunk(C_LORA, np.concatenate([w_in[:, r0 + 3 * RW:r0 + 3 * RW + 160], w_in[:, n0 + 1024 + 6 * 256:]], 1))
    for c0, at, n in ((C_K, r0 + RW, 2), (C_R, r0, 2), (C_V, r0 + 2 * RW, 2), (C_KC, n0 + 1024, 1), (C_VC, n0 + 1280, 1),
                      (C_Q, n0, 4), (C_KS, n0 + 1536, 1), (C_KW, n0 + 2048, 1), (C_VS, n0 + 1792, 1),
                      (C_VW, n0 + 2304, 1), (C_POOL, 0, 2)):
        for j in range(n):
            chunk(c0 + j, w_in[:, at + 256 * j:at + 256 * (j + 1)])
    for c0, key in ((C_W1K, "cmp_w1_k"), (C_W1V, "cmp_w1_v")):
        for j in range(2):
            chunk(c0 + j, a[key][0][1024 * j:1024 * (j + 1)])
    for n in range(4):
        cs = slice(256 * n, 256 * (n + 1))
        for b in range(3):
            chunk(C_GATE + 3 * n + b, a["w_merge"][0][:, D * b:D * (b + 1)][:, cs])
        for j in range(2):
            chunk(C_BRANCH + 2 * n + j, a["w_branch"][0][1024 * j:1024 * (j + 1), cs])
        chunk(C_OUT + n, a["w_out"][0][:, cs])
    wr = np.concatenate([a["w_router_grp"][0], a["w_router_exp"][0]], 1)
    front[C_ROUTER][:, 0:KD * 36] = wr.reshape(KD, P, 36).transpose(1, 0, 2).reshape(P, -1)

    ex = np.empty((NGANG, GCH, P, SLOT), np.float32)
    gu = ex[:, 0:8].reshape(NGANG, 8, P, GANG, 2, DE)
    for j, key in enumerate(("w_exp_gate", "w_exp_up")):
        gu[:, :, :, :, j] = a[key][0].reshape(NGANG, GANG, KD, P, DE).transpose(0, 2, 3, 1, 4)
    ex[:, 8:12] = a["w_exp_down"][0].reshape(NGANG, GANG, 2, P, D).transpose(0, 1, 3, 2, 4).reshape(NGANG, GANG, P, -1)

    arrays = {
        "x": a["x"][0], "params": par, "consts": constants(), "front": front, "experts": ex,
        "g_final": np.ascontiguousarray(np.broadcast_to(a["norm_final"], (P, D))),
    }
    nc = _bacc.Bacc("TRN2", target_bir_lowering=False, num_devices=1)
    args = [nc.dram_tensor(n, v.shape, F32, kind="ExternalInput").ap() for n, v in arrays.items()]
    out = nc.dram_tensor("out", (S, D), F32, kind="ExternalOutput").ap()
    rows = nc.dram_tensor("bias_rows", (NH, 384), F32, kind="Internal").ap()
    build_layer(nc, *args, out, rows)
    r = _run(nc, [arrays], core_ids=[0])
    return r.results[0]["out"].reshape(1, S, D)
```

```python
import math
from contextlib import ExitStack

import numpy as np

import concourse.bass as bass
from concourse import mybir

F32 = mybir.dt.float32
ALU = mybir.AluOpType
ACT = mybir.ActivationFunctionType
AXX = mybir.AxisListType.X

P = 128
D = 1024
S = 256
NT = S // P
KD = D // P
PW = 512
RW = 512
RH = 8
NH, NG = 16, 4
DH = 64
NCMP, CSTRIDE, CBLOCK = 15, 16, 32
NB = 32
E, EPG, NGRP = 32, 8, 4
DE = 256
CH = 64
NCH = S // CH
NEG = -1.0e30
FAR = 3.0e38
DECAY = math.exp(-0.5)
GELU_C = math.sqrt(2.0 / math.pi)

SLOT = 2048
RING = 12
FRING = 4
C_LORA = 0
C_POOL = 1
C_K, C_R, C_V = 3, 5, 7
C_KC, C_VC = 9, 10
C_Q = (11, 12, 17, 18)
C_W1K, C_W1V = 13, 15
C_KS, C_KW, C_VS, C_VW = 19, 20, 21, 22
C_GATE = 23
C_BRANCH = 35
C_OUT = 43
C_ROUTER = 47
NFRONT = 48
GANG = 4
NGANG = E // GANG
CAP = 32
GCH = 12


RWKV_STEPS = []
for _i in range(NT):
    RWKV_STEPS += [("turn", _i, 0)] + ([("finish", _i - 1, 0)] if _i else [])
    RWKV_STEPS += [("products", _i, _half) for _half in range(2)]
    for _grp in range(2):
        RWKV_STEPS += [("seed", _i, (_grp, 0))] + [("level", _i, (_grp, _n)) for _n in range(5)]
    RWKV_STEPS += [("solve", _i, 0), ("local", _i, 0), ("scan", _i, 0), ("scan", _i, 1)]
RWKV_STEPS += [("finish", NT - 1, 0)]
BRANCHES = (2, 0, 1)
UNITS = [(_g, _u) for _g in range(NG) for _u in range(6)]
BEFORE = 4
DURING = BEFORE + NG + len(UNITS)
NGATE, NEARLY = 12, 4
LAST = len(RWKV_STEPS) - 1


def columns(parts):
    at, out = 0, {}
    for name, n in parts:
        out[name] = (at, at + n)
        at += n
    return out, at


PARAMS, NPARAMS = columns([
    ("g_mix", 8), ("g_ffn", 8), ("mu", 14), ("w0", 4), ("a0", 4), ("k_k", 4), ("k_a", 4), ("r_k", 4),
    ("gn_w", 4), ("gn_b", 4), ("pool_scale", 4), ("b_merge", 24),
    ("lora_up", RW), ("g_up", RW), ("pool_w", PW), ("w2_k", 2 * DH), ("w2_v", 2 * DH),
    ("pos_k", 16), ("pos_v", 16), ("rel", NH), ("b_router", NGRP + E)])
CONSTS, NCONSTS = columns([
    ("ident", P), ("neghalf", 8), ("flip", P), ("headsum", P), ("intra", 4 * P), ("level", 6 * P),
    ("onehot", 384), ("eye64", DH), ("count", 4 * 16), ("ones", P), ("earlier", P),
    ("falling", E)])
LEAD_PARAMS = PARAMS["lora_up"][0]
LEAD_CONSTS = CONSTS["flip"][0]


def t5_bucket(dist):
    n = np.maximum(dist, 0)
    nf = np.maximum(n, 1).astype(np.float32)
    large = 16 + (np.log(nf / np.float32(16)) / np.float32(math.log(8)) * np.float32(16)).astype(np.int32)
    return np.where(n < 16, n, np.minimum(large, NB - 1))


def constants():
    c = np.zeros((P, NCONSTS), np.float32)

    def put(name, a):
        lo, hi = CONSTS[name]
        c[:a.shape[0], lo:hi] = a.reshape(a.shape[0], hi - lo)

    r = np.arange(P)
    put("ident", np.eye(P))
    put("flip", np.eye(P)[::-1])
    put("headsum", (r[:, None] // DH == r[None, :] // DH) * 1.0)
    same = r[:, None] // CH == r[None, :] // CH
    before, upto = same & (r[:, None] < r[None, :]), same & (r[:, None] <= r[None, :])
    put("intra", np.concatenate([before, upto, before, upto], 1) * 1.0)
    level = []
    for n in (1, 2, 4, 8, 16, 32):
        level.append((r[:, None] // (2 * n) == r[None, :] // (2 * n))
                     & (r[:, None] % (2 * n) < n) & (r[None, :] % (2 * n) >= n))
    put("level", np.concatenate(level, 1) * 1.0)
    dist = 255 - np.arange(384)
    put("onehot", np.concatenate([(np.arange(NB)[:, None] == t5_bucket(dist)[None, :]) * 1.0,
                                  np.where(dist < 0, NEG, 0.0)[None]]))
    put("eye64", np.eye(P)[:, :DH] + np.eye(P)[:, DH:])
    w = np.array([2, 4, 8, 16])
    put("count", np.broadcast_to(1.0 / np.minimum(np.arange(16)[None] + 1, w[:, None]), (P, 4, 16)))
    put("ones", np.ones((P, P)))
    put("earlier", (r[:, None] < r[None, :]) * 1.0)
    put("neghalf", np.full((P, 8), -0.5))
    put("falling", np.broadcast_to(E - np.arange(E), (P, E)) * 1.0)
    return c


def build_layer(nc, x, params, consts, front, experts, g_final, out, bias_rows):
    ctx = ExitStack()
    with ctx:
        def sb(name, shape):
            return ctx.enter_context(nc.sbuf_tensor(name, shape, F32))

        def sem(name):
            return ctx.enter_context(nc.semaphore(name))

        def like(ap, shape):
            return ap.to_broadcast(shape)

        ring = sb("ring", [P, RING * SLOT])
        par = sb("par", [P, NPARAMS])
        con = sb("con", [P, NCONSTS])
        tok = sb("tok", [P, NT, D])
        hT = sb("hT", [P, KD, S])
        yT = sb("yT", [P, 16, S])
        rawf = sb("raw", [P, 4 * (S + 1)])
        raw = rawf[:, :].rearrange("p (b m t) -> p b m t", b=2, m=2)
        mix = sb("mix", [P, 14, S])
        t1 = sb("t1", [P, 4, S])
        t2 = sb("t2", [P, 4, S])
        t3 = sb("t3", [P, 4, S])
        arbk = sb("arbk", [P, 16, S])
        xcmp = sb("xcmp", [P, 2, 16, NG * NCMP])
        vtok = sb("vtok", [P, 2, NT, 256])
        small = sb("small", [P, 256])
        state = sb("state", [P, 2, 4, DH])
        gate_t = sb("gate_t", [P, NT, 3 * NH])
        gates_f = raw[64:112, 0, 0, 1:S + 1]

        def pr(name, rows=P):
            lo, hi = PARAMS[name]
            return par[0:rows, lo:hi]

        def cn(name, rows=P):
            lo, hi = CONSTS[name]
            return con[0:rows, lo:hi]

        ident = cn("ident")
        spare = ring[:, FRING * SLOT:RING * SLOT]
        bias = spare[:, 0:4096].rearrange("p (h m) -> p h m", h=NH)
        amat = spare[:, 4096:8192].rearrange("p (h j t) -> p h j t", h=RH, j=4)
        qT = spare[:, 8192:10240].rearrange("p (m t) -> p m t", m=8)
        kT = spare[:, 10240:14336].rearrange("p (q b g t) -> p q b g t", q=2, b=2, g=NG)
        window = arbk[:, :, :]
        ar = arbk[:, 0:8, :].rearrange("p c t -> p (c t)").rearrange("p (m i j t) -> p m i j t", m=4, i=2, j=2)
        bf = arbk[:, 8:12, :]
        kf = arbk[:, 12:16, :]
        kshift = yT[:, 8:16, :].rearrange("p (b g) t -> p b g t", b=2)
        btok = t1[:, 0:2, :].rearrange("p c t -> p (c t)")
        ktok = t1[:, 2:4, :].rearrange("p c t -> p (c t)")
        vrow = t2[:, 0:2, :].rearrange("p c t -> p (c t)")
        lmask = t2[:, 2:4, :].rearrange("p c t -> p (c t)").rearrange("p (h t) -> p h t", h=4)
        xinv = t3[:, 0:2, :].rearrange("p c t -> p (c t)").rearrange("p (h t) -> p h t", h=4)
        zinv = [rawf[:, g * 512:(g + 1) * 512].rearrange("p (h t) -> p h t", h=4) for g in range(2)]
        winv = t3[:, 2:4, :].rearrange("p c t -> p (c t)").rearrange("p (h t) -> p h t", h=4)
        rhs = mix[:, 0:4, :].rearrange("p c t -> p (c t)").rearrange("p (h j v) -> p h j v", h=RH, j=2)
        padded = t3[:, :, :].rearrange("p c t -> p (c t)").rearrange("p (m q n) -> p m q n", m=2, q=2)
        bonus = mix[:, 4:8, :]
        fc = t3[:, :, :].rearrange("p c t -> p (c t)").rearrange("p (c m j v) -> p c m j v", c=2, m=4, j=2)
        ynorm = t2[:, 2:4, :].rearrange("p c t -> p (c t)")
        ysq = t3[:, 0:2, :].rearrange("p c t -> p (c t)")
        pend = small[:, 0:16].rearrange("p (m c) -> p m c", m=4)
        stat = small[:, 16:64]
        tokf = tok[:, :, :].rearrange("p i d -> p (i d)")
        prob = tokf[:, 0:1024].rearrange("p (b n) -> p b n", b=2)
        probT = tokf[:, 1024:2048].rearrange("p (b n) -> p b n", b=2)
        xf = xcmp[:, :, :, :].rearrange("p b j n -> p (b j n)")
        gx = xf[0:60, 0:512]
        gy = xf[0:60, 512:1024]
        hidT = xf[:, 1024:1264].rearrange("p (f n) -> p f n", f=4)
        kcb = xf[:, 1700:1820].rearrange("p (q n) -> p q n", q=2)
        vcb = xf[0:NCMP, 1324:1580].rearrange("p (g v) -> p g v", g=NG)
        cprob = [xf[:, lo:lo + NH * n].rearrange("p (h n) -> p h n", h=NH)
                 for lo, n in ((1580, 7), (1024, NCMP))]
        cprobT = xf[0:NCMP, 0:1024].rearrange("p (i h t) -> p i h t", i=2, h=4)
        astat = small[:, 64:128]
        gsig = [spare[:, lo:lo + 512].rearrange("p (m t) -> p m t", m=2)
                for lo in list(range(14336, 14336 + 512 * NEARLY, 512)) + list(range(0, 4096, 512))]
        merged = arbk[:, 0:8, :]
        macc = t2[:, 0:2, :]
        mtmp = t2[:, 2:4, :]
        xn = mix[:, 0:8, :].rearrange("p c t -> p (c t)").rearrange("p (i d) -> p i d", i=2)
        arf = arbk[:, :, :].rearrange("p c t -> p (c t)")
        gath = arf[:, 0:1024].rearrange("p (k s) -> p k s", k=KD)
        ydown = arf[:, 1024:2048]
        gtanh = arf[:, 2048:2304]
        ghid = arf[:, 2304:2560]
        ghidT = arf[:, 2560:2816].rearrange("p (f s) -> p f s", f=2)
        sel = arf[:, 2816:3072].rearrange("p (i s) -> p i s", i=2)
        wsel = arf[:, 3072:3328].rearrange("p (i s) -> p i s", i=2)
        wselT = arf[:, 3328:3584].rearrange("p (i t) -> p i t", i=2)
        place = arf[:, 3584:3584 + 2 * (E + GANG)].rearrange("p (i e) -> p i e", i=2)
        gsi = arbk[:, 8:12, :].rearrange("p c t -> p (c t)").rearrange("p (e n) -> p e n", e=GANG)
        hid = arbk[:, 12:16, :].rearrange("p c t -> p (c t)").rearrange("p (e n) -> p e n", e=GANG)
        hidm = t1[:, :, :].rearrange("p c t -> p (c t)").rearrange("p (e f t) -> p e f t", e=GANG, f=2)
        combine = small[:, 112:112 + 2 * (E + GANG)].rearrange("p (i e) -> p i e", i=2)
        member = mix[:, 8, 0:2 * E].rearrange("p (i e) -> p i e", i=2)
        crowd = ctx.enter_context(nc.sbuf_tensor("crowd", [P, 1], mybir.dt.int32))
        halves = small[:, 192:224]
        rtf = t3[:, :, :].rearrange("p c t -> p (c t)")
        rt_at, _ = columns([("lg", 72), ("gh", 8), ("ge", 8), ("h1", 64), ("h2", 64), ("gm", 2), ("m1", 2), ("m2", 2),
                            ("tmp", 2), ("w1", 2), ("w2", 2)])

        def rt(name):
            lo, hi = rt_at[name]
            return rtf[:, lo:hi] if hi - lo == 2 else rtf[:, lo:hi].rearrange("p (i n) -> p i n", i=2)

        gfin = yT[:, 0:4, :].rearrange("p c t -> p (c t)")

        bank = [ctx.enter_context(nc.psum_tensor(f"bank{b}", [P, 512], F32)) for b in range(8)]

        loaded = [sem(f"slot_loaded{s}") for s in range(RING)]
        taken = sem("chunks_taken")
        bank_full = [sem(f"bank_full{b}") for b in range(8)]
        bank_free = [sem(f"bank_free{b}") for b in range(8)]
        names = [
            "lead_loaded", "small_loaded", "x_loaded0", "x_loaded1", "x_again", "stored", "gfin_loaded",
            "win_stored", "win_ready",
            "raw_zeroed", "keys_zeroed", "padded_zeroed", "padded_ready", "root_ready", "lmask_ready", "state_zeroed",
            "raw_ready", "gate_tanh", "lora_w_ready", "lora_g_tanh", "kshift_ready", "bias_ready", "q_ready",
            "k_ready", "v_ready", "u_ready", "gx_ready", "gelu_tanh", "decay_tanh", "rate_tanh", "kk_root",
            "hidT_ready", "cmp_kv_ready", "decay_exp", "cexp_ready", "cprobT_ready", "exp_ready", "probT_ready",
            "tok_ready", "w_ready", "rhs_ready", "xu_ready", "gn_ready", "gsig_ready", "router_exp",
            "silu_tanh", "hidT2_ready", "gtanh_ready", "wselT_ready", "ghidT_ready",
            "ydown_ready",
            "gathered", "wsel_turned", "gate_up", "hid_turned", "downed", "scattered",
            "halves_ready", "rms_in", "xn_ready", "hT_ready", "hT_odd_ready", "xn2_ready", "raw_used", "mix_ready", "win_row", "gates_ready",
            "xcmp_ready", "pool_ready", "kk_sq_ready", "kk_max", "gelu_in", "gelu_ready", "log_ready",
            "lora_g_ready", "pool_out", "bonus_ready", "rwkv_ready", "cexp_in", "cprob_ready", "exp_in",
            "prob_ready", "nsa_ready", "amat_ready", "z_ready", "x_ready", "rx_ready", "fc_ready",
            "state_ready", "ynorm_ready", "yrw_ready", "gated", "merged_ready", "sum_ready", "router_in",
            "combine_ready", "hid_ready", "moe_ready", "member_ready", "crowd_ready", "sel_ready", "gath_ready",
            "ghid_ready", "summed", "final_ready", "dve_chain"]
        q = {n: sem(n) for n in names}

        def ordinal():
            seen = {}

            def nth(b):
                seen[b] = seen.get(b, -1) + 1
                return seen[b]
            return nth

        plan = {}
        nth = ordinal()

        def hand(name, b):
            assert name not in plan
            plan[name] = (b, nth(b))

        for n in range(4):
            hand(f"xT{n}", n)
        hand("lora_in", 0), hand("pool0", 2)
        hand("gates", 1), hand("brow", 4)
        hand("pool1", 3)
        for c in range(1, 7):
            hand(f"rkv{c}", 4 + c % 2)
        hand("poolmix0", 2), hand("poolmix1", 3)
        for n in range(8):
            hand(f"bias{n}", 6 + n % 2)
        for n in range(2):
            hand(f"wup{n}", n)
        for n in range(2):
            hand(f"aup{n}", 2 + n)
        hand("kc", 0), hand("vc", 1)
        hand("kk0", 4), hand("kk1", 5)
        hand("q0", 2), hand("q1", 3)
        hand("mlp_k", 6), hand("mlp_v", 7)
        hand("q2", 2), hand("q3", 3)
        hand("hidT", 6)
        hand("ks", 0)
        hand("kcb", 7), hand("vcb", 6)
        hand("bonus0", 4), hand("bonus1", 5)

        def hand_early(step):
            kind, i, which = step
            if kind == "turn":
                hand(f"tok{i}0", 5), hand(f"tok{i}1", 6)
            elif kind == "finish":
                hand(f"gup{i}", 6)
            elif kind == "products":
                for h in range(4 * which, 4 * which + 2):
                    hand(f"A{i}{h}", 5 + h % 3)
            elif kind == "level":
                hand("W%d%d%d" % (i, *which), 5)
            elif kind == "solve":
                hand(f"w0{i}", 5)
            elif kind == "local":
                hand(f"rx{i}0", 5), hand(f"rx{i}1", 6)
            elif kind == "scan" and 2 * i + which < NCH - 1:
                hand(f"st{i}{which}", 5)

        def hand_late(step):
            kind, i, which = step
            if kind == "turn":
                hand(f"tok{i}2", 7), hand(f"atok{i}", 5)
            elif kind == "finish":
                hand(f"yT{i}", 5)
            elif kind == "products":
                for h in range(4 * which + 2, 4 * which + 4):
                    hand(f"A{i}{h}", 5 + h % 3)
            elif kind == "seed":
                hand("XZ%d%d" % (i, which[0]), 6)
            elif kind == "level":
                if which[1] < 4:
                    hand("X%d%d%d" % (i, *which), 6)
                hand("Z%d%d%d" % (i, *which), 7)
            elif kind == "solve":
                hand(f"xu{i}0", 6), hand(f"xu{i}1", 7)
            elif kind == "local":
                hand(f"fc{i}0", 5), hand(f"fc{i}1", 7)

        def hand_after(step):
            kind, i, which = step
            if kind == "local":
                hand(f"y{i}0", 6), hand(f"y{i}1", 7)

        hand("cs0", 2), hand("cs1", 3)
        for step, name, b in zip(RWKV_STEPS, ("kw", "vs", "vw"), (1, 2, 3)):
            hand_early(step), hand_late(step)
            if name == "vw":
                hand("s00", 0), hand("s01", 1)
            hand(name, b)
        hand_early(RWKV_STEPS[3]), hand_late(RWKV_STEPS[3])

        def gate_share(s):
            total, slots = NEARLY * 2 * KD, DURING - BEFORE
            return range(total * s // slots, total * (s + 1) // slots)

        def gates_done(s):
            return [x // (2 * KD) for x in gate_share(s) if x % (2 * KD) == 2 * KD - 1] if s >= 0 else []

        def hand_gates(s):
            for x in gate_share(s):
                if x % (2 * KD) == 0:
                    hand(f"mg{x // (2 * KD)}", 4)

        slot = iter(range(DURING - BEFORE))
        steps = iter(RWKV_STEPS[BEFORE:DURING])
        for n, (g, u) in enumerate(UNITS):
            if u == 0:
                step = next(steps)
                hand(f"cT{g}0", 2)
                hand_early(step)
                hand(f"cT{g}1", 2)
                hand_late(step)
                hand(f"o{g}", 3)
                hand_gates(next(slot))
            step = next(steps)
            hand_early(step)
            if n + 2 < len(UNITS):
                hand("s%d%d" % UNITS[n + 2], n % 2)
            hand(f"pT{g}{u}", 2)
            hand_late(step)
            hand_gates(next(slot))
            hand_after(step)
        beside = {NEARLY + j: step for j, step in enumerate(RWKV_STEPS[DURING:LAST])}
        beside[NGATE - 1] = RWKV_STEPS[LAST]
        for j in range(NEARLY, NGATE):
            if j in beside:
                hand_early(beside[j])
            hand(f"mg{j}", j % 4)
            if j in beside and j < NGATE - 1:
                hand_late(beside[j])
                hand_after(beside[j])
        for n in range(4):
            for at, b in enumerate(BRANCHES):
                hand(f"mb{n}{b}", (3 * n + at) % 4)
                if n == at == 0:
                    hand_late(beside[NGATE - 1])
        hand("out0", 6), hand("out1", 7), hand("hT20", 0)
        hand("out2", 6), hand("hT21", 1), hand("router", 4)
        hand("out3", 7), hand("hT22", 2), hand("hT23", 3)
        hand("places", 5)
        before_loop = [nth(b) for b in range(8)]


        def full(eng, name):
            b, n = plan[name]
            eng.wait_ge(bank_full[b], n + 1)
            return bank[b]

        def chainer(eng, own):
            count = {}

            def chain(ins, name=None, hold=True):
                name = name or own
                count[name] = count.get(name, 0) + 1
                ins.then_inc(q[name], 1)
                if hold:
                    eng.wait_ge(q[name], count[name])
            chain.count = count
            return chain

        block = ctx.enter_context(nc.Block())

        @block.sync
        def _(sp):
            xt = x.rearrange("(i p) d -> p i d", p=P)
            sp.dma_start(tok[:, 0, :], xt[:, 0, :]).then_inc(q["x_loaded0"], 16)
            sp.dma_start(con[:, 0:LEAD_CONSTS], consts[:, 0:LEAD_CONSTS]).then_inc(q["lead_loaded"], 16)
            sp.dma_start(par[:, 0:LEAD_PARAMS], params[:, 0:LEAD_PARAMS]).then_inc(q["lead_loaded"], 16)
            sp.dma_start(tok[:, 1, :], xt[:, 1, :]).then_inc(q["x_loaded1"], 16)
            for s in range(FRING):
                if s == FRING // 2:
                    sp.dma_start(con[:, LEAD_CONSTS:], consts[:, LEAD_CONSTS:]).then_inc(q["small_loaded"], 16)
                    sp.dma_start(par[:, LEAD_PARAMS:], params[:, LEAD_PARAMS:]).then_inc(q["small_loaded"], 16)
                sp.dma_start(ring[:, s * SLOT:(s + 1) * SLOT], front[s]).then_inc(loaded[s], 16)
            sp.wait_ge(q["win_row"], 1)
            sp.dma_start(bias_rows, arbk[0:NH, 0:2, :].rearrange("p a b -> p (a b)")[:, 0:384])\
                .then_inc(q["win_stored"], 16)
            sp.wait_ge(q["win_stored"], 16)
            sp.dma_start(window, bass.AP(bias_rows.tensor, 0, [[1, P], [384, NH], [1, 256]]))\
                .then_inc(q["win_ready"], 16)
            with sp.Fori(1, NFRONT // FRING) as rnd:
                for s in range(FRING):
                    sp.wait_ge(taken, rnd * FRING + (s + 1 - FRING))
                    sp.dma_start(ring[:, s * SLOT:(s + 1) * SLOT], front[rnd * FRING + s]).then_inc(loaded[s], 16)
            for s in range(FRING):
                sp.wait_ge(taken, NFRONT + s + 1 - FRING)
                sp.dma_start(ring[:, s * SLOT:(s + 1) * SLOT], experts[0, s]).then_inc(loaded[s], 16)
            with sp.Fori(1, NGANG) as gang:
                for s in range(GCH):
                    sp.wait_ge(taken, gang * GCH + (NFRONT - GCH + s + 1))
                    sp.dma_start(ring[:, s * SLOT:(s + 1) * SLOT], experts[gang, s]).then_inc(loaded[s], 16)
            res = hT[:, :, :].rearrange("p c t -> p (c t)").rearrange("p (i d) -> p i d", i=2)
            for i in range(NT):
                sp.wait_ge(q["final_ready"], i + 1)
                sp.dma_start(out[i * P:(i + 1) * P, :], res[:, i, :]).then_inc(q["stored"], 16)
            sp.wait_ge(q["stored"], 16 * NT)

        @block.tensor
        def _(pe):
            def begin(name):
                b, n = plan[name]
                if n:
                    pe.wait_ge(bank_free[b], n)
                return bank[b]

            def end(ins, name):
                ins.then_inc(bank_full[plan[name][0]], 1)

            def chunk(n):
                pe.wait_ge(loaded[n % FRING], 16 * (n // FRING + 1))
                return ring[:, (n % FRING) * SLOT:(n % FRING + 1) * SLOT]

            owed = [0]

            def pe_take():
                owed[0] += 1

            def first(ins):
                if owed[0]:
                    ins.then_inc(taken, owed[0])
                    owed[0] = 0
                return ins

            def mm(o, l, r, k, n):
                return first(pe.matmul(o, l, r, start=(k == 0), stop=(k == n - 1)))

            def project(name, n):
                w = chunk(n).rearrange("p (k c) -> p k c", k=KD)
                o = begin(name)
                for m in range(2):
                    for k in range(KD):
                        last = mm(o[:, m * S:(m + 1) * S], w[:, k, m * P:(m + 1) * P], hT[:, k, :], k, KD)
                end(last, name)
                pe_take()

            for n in range(4):
                i = n // 2
                pe.wait_ge(q["xn_ready"], i + 1)
                if n == 0:
                    pe.wait_ge(q["lead_loaded"], 32)
                o = begin(f"xT{n}")
                for k in range(4):
                    kk = (n % 2) * 4 + k
                    last = pe.transpose(o[:, k * P:(k + 1) * P], xn[:, i, kk * P:(kk + 1) * P], ident)
                end(last, f"xT{n}")
            pe.wait_ge(q["hT_ready"], 2)
            pe.wait_ge(q["hT_odd_ready"], 2)

            w = chunk(C_LORA).rearrange("p (k c) -> p k c", k=KD)
            o = begin("lora_in")
            for lo, n, col in ((0, 112, 0), (112, 96, S)):
                for k in range(KD):
                    last = mm(o[0:n, col:col + S], w[:, k, lo:lo + n], hT[:, k, :], k, KD)
            end(last, "lora_in")
            pe_take()
            project("pool0", C_POOL)
            pe.wait_ge(q["gate_tanh"], 1)
            o = begin("gates")
            for i in range(NT):
                last = first(pe.transpose(o[:, i * 48:(i + 1) * 48], gates_f[:, i * P:(i + 1) * P], ident[64:112, 64:112]))
            end(last, "gates")
            pe.wait_ge(q["small_loaded"], 32)
            o = begin("brow")
            end(pe.matmul(o[0:NH, 0:384], pr("rel", NB + 1), cn("onehot", NB + 1), start=True, stop=True), "brow")
            project("pool1", C_POOL + 1)
            for c in range(1, 7):
                project(f"rkv{c}", C_K + c - 1)

            pe.wait_ge(q["pool_ready"], 1)
            for n in range(2):
                o = begin(f"poolmix{n}")
                for m in range(2):
                    gi = 2 * n + m
                    last = first(pe.matmul(o[:, m * S:(m + 1) * S], pr("pool_w")[:, gi * P:(gi + 1) * P],
                                           yT[:, gi, :], start=True, stop=True))
                end(last, f"poolmix{n}")

            pe.wait_ge(q["win_ready"], 16)
            wf = window.rearrange("p a b -> p (a b)")
            for n in range(8):
                o = begin(f"bias{n}")
                end(pe.matmul(o[:, :], cn("flip"), wf[:, n * 512:(n + 1) * 512], start=True, stop=True), f"bias{n}")

            pe.wait_ge(q["lora_w_ready"], 1)
            for n in range(2):
                o = begin(f"wup{n}")
                for m in range(2):
                    c = (2 * n + m) * P
                    last = pe.matmul(o[:, m * S:(m + 1) * S], pr("lora_up")[0:32, c:c + P], mix[0:32, 12, :],
                                     start=True, stop=True)
                end(last, f"wup{n}")
            for n in range(2):
                o = begin(f"aup{n}")
                for m in range(2):
                    c = (2 * n + m) * P
                    last = pe.matmul(o[:, m * S:(m + 1) * S], pr("lora_up")[32:64, c:c + P], mix[32:64, 12, :],
                                     start=True, stop=True)
                end(last, f"aup{n}")

            project("kc", C_KC)
            project("vc", C_VC)
            pe.wait_ge(q["kk_sq_ready"], 1)
            for n in range(2):
                o = begin(f"kk{n}")
                end(pe.matmul(o[:, :], cn("headsum"), t3[:, 2 * n:2 * n + 2, :], start=True, stop=True), f"kk{n}")
            project("q0", C_Q[0])
            project("q1", C_Q[1])

            for b, (name, c0) in enumerate((("mlp_k", C_W1K), ("mlp_v", C_W1V))):
                pe.wait_ge(q["xcmp_ready"], b + 1)
                o = begin(name)
                for half in range(2):
                    w = chunk(c0 + half).rearrange("p (k c) -> p k c", k=KD)
                    for j in range(8):
                        last = mm(o[0:60, 0:256], xcmp[:, b, half * 8 + j, :], w[:, j, :], half * 8 + j, 16)
                    if half:
                        end(last, name)
                    pe_take()
            project("q2", C_Q[2])
            project("q3", C_Q[3])
            pe.wait_ge(q["gelu_ready"], 1)
            o = begin("hidT")
            for f in range(4):
                last = first(pe.transpose(o[:, f * 60:(f + 1) * 60], gx[:, f * P:(f + 1) * P], ident[0:60, 0:60]))
            end(last, "hidT")
            project("ks", C_KS)
            pe.wait_ge(q["hidT_ready"], 1)
            w2k = pr("w2_k").rearrange("p (f v) -> p f v", f=2)
            w2v = pr("w2_v").rearrange("p (f v) -> p f v", f=2)
            o = begin("kcb")
            for p in range(2):
                for f in range(2):
                    last = mm(o[64 * p:64 * p + 64, 0:60], w2k[:, f, :], hidT[:, f, :], f, 2)
            end(last, "kcb")
            o = begin("vcb")
            for g in range(NG):
                for f in range(2):
                    last = mm(o[0:NCMP, g * 64:g * 64 + 64], hidT[:, 2 + f, g * NCMP:(g + 1) * NCMP], w2v[:, f, :], f, 2)
            end(last, "vcb")
            pe.wait_ge(q["bonus_ready"], 1)
            for n in range(2):
                o = begin(f"bonus{n}")
                end(pe.matmul(o[:, :], cn("headsum"), mix[:, 4 + 2 * n:6 + 2 * n, :], start=True, stop=True), f"bonus{n}")

            def values(name, c):
                w = chunk(c).rearrange("p (k c) -> p k c", k=KD)
                o = begin(name)
                for i in range(NT):
                    for k in range(KD):
                        last = mm(o[:, i * 256:(i + 1) * 256], hT[:, k, i * P:(i + 1) * P], w[:, k, :], k, KD)
                end(last, name)
                pe_take()

            def early(step):
                kind, i, which = step
                ts = slice(i * P, (i + 1) * P)
                if kind == "turn":
                    if i == 0:
                        pe.wait_ge(q["rwkv_ready"], 1)
                    for w_, src in enumerate((bf, kf)):
                        turned(f"tok{i}{w_}", [src[:, m, ts] for m in range(4)])
                elif kind == "products":
                    products(i, range(4 * which, 4 * which + 2))
                elif kind == "level":
                    grp, n = which
                    turn_ = 2 * i + grp
                    pe.wait_ge(q["x_ready"], 5 * turn_ + n + 1)
                    pe.wait_ge(q["lmask_ready"], 6 * turn_ + n + 2)
                    o = begin(f"W{i}{grp}{n}")
                    for h in range(4):
                        last = pe.matmul(o[:, h * P:(h + 1) * P], lmask[:, h, :], xinv[:, h, :], start=True, stop=True)
                    end(last, f"W{i}{grp}{n}")
                elif kind == "solve":
                    pe.wait_ge(q["z_ready"], 12 * (i + 1))
                    pe.wait_ge(q["tok_ready"], 4 * (i + 1))
                    o = begin(f"w0{i}")
                    for h in range(RH):
                        last = pe.matmul(o[:, h * DH:(h + 1) * DH], amat[:, h, 2, :], vrow[:, h * DH:(h + 1) * DH],
                                         start=True, stop=True)
                    end(last, f"w0{i}")
                elif kind == "local":
                    pe.wait_ge(q["xu_ready"], 2 * (i + 1))
                    for n in range(2):
                        o = begin(f"rx{i}{n}")
                        for hh in range(4):
                            h = 4 * n + hh
                            last = pe.matmul(o[64 * (h % 2):64 * (h % 2) + 64, (hh // 2) * P:(hh // 2 + 1) * P],
                                             rhs[:, h, 0, :], amat[:, h, 1, :], start=True, stop=True)
                        end(last, f"rx{i}{n}")
                elif kind == "scan":
                    n = 2 * i + which
                    pe.wait_ge(q["rx_ready"], 2 * (i + 1))
                    pe.wait_ge(q["fc_ready"], n + 1)
                    pe.wait_ge(q["state_zeroed"], 1)
                    if n:
                        pe.wait_ge(q["state_ready"], n)
                    if n < NCH - 1:
                        o = begin(f"st{i}{which}")
                        for h in range(RH):
                            m, p = h // 2, h % 2
                            rows = slice(64 * p, 64 * p + 64)
                            last = pe.matmul(o[rows, m * DH:(m + 1) * DH], fc[rows, which, m, 0, :],
                                             state[rows, n % 2, m, :], start=True, stop=True)
                        end(last, f"st{i}{which}")
                elif kind == "finish":
                    pe.wait_ge(q["lora_g_ready"], 1)
                    o = begin(f"gup{i}")
                    for m in range(4):
                        last = pe.matmul(o[:, m * P:(m + 1) * P], pr("g_up", 96)[:, m * P:(m + 1) * P], mix[0:96, 13, ts],
                                         start=True, stop=True)
                    end(last, f"gup{i}")

            def late(step):
                kind, i, which = step
                ts = slice(i * P, (i + 1) * P)
                if kind == "turn":
                    turned(f"tok{i}2", [mix[:, 8 + m, ts] for m in range(4)])
                    turned(f"atok{i}", [ar[:, m, i, 0, :] for m in range(4)])
                elif kind == "products":
                    products(i, range(4 * which + 2, 4 * which + 4))
                elif kind == "seed":
                    grp = which[0]
                    pe.wait_ge(q["z_ready"], 6 * (2 * i + grp) + 1)
                    turned(f"XZ{i}{grp}", [zinv[grp][:, h, :] for h in range(4)])
                elif kind == "level":
                    grp, n = which
                    turn_ = 2 * i + grp
                    z = zinv[grp]
                    pe.wait_ge(q["w_ready"], 5 * turn_ + n + 1)
                    pe.wait_ge(q["z_ready"], 6 * turn_ + n + 1)
                    if n < 4:
                        o = begin(f"X{i}{grp}{n}")
                        for h in range(4):
                            last = pe.matmul(o[:, h * P:(h + 1) * P], z[:, h, :], winv[:, h, :], start=True, stop=True)
                        end(last, f"X{i}{grp}{n}")
                    o = begin(f"Z{i}{grp}{n}")
                    for h in range(4):
                        last = pe.matmul(o[:, h * P:(h + 1) * P], winv[:, h, :], z[:, h, :], start=True, stop=True)
                    end(last, f"Z{i}{grp}{n}")
                elif kind == "solve":
                    pe.wait_ge(q["rhs_ready"], i + 1)
                    for n in range(2):
                        o = begin(f"xu{i}{n}")
                        for h in range(4):
                            last = pe.matmul(o[:, h * P:(h + 1) * P], zinv[n][:, h, :], rhs[:, 4 * n + h, :, :],
                                             start=True, stop=True)
                        end(last, f"xu{i}{n}")
                elif kind == "local":
                    fbank = [begin(f"fc{i}{c}") for c in range(2)]
                    for m in range(4):
                        for flip in range(2):
                            for product in range(3):
                                for c in range(2):
                                    p = (c + flip) % 2
                                    h = 2 * m + p
                                    rows = slice(64 * c, 64 * c + 64)
                                    hs = slice(h * DH, (h + 1) * DH)
                                    oo = fbank[c][64 * p:64 * p + 64, m * P + (64 if product else 0):][:, 0:DH]
                                    left, right = ((rhs[rows, h, 0, :], btok[rows, hs]),
                                                   (btok[rows, hs], rhs[rows, h, 1, :]),
                                                   (ktok[rows, hs], vrow[rows, hs]))[product]
                                    last = pe.matmul(oo, left, right, start=(product < 2), stop=(product != 1))
                                    if m == 3 and flip == 1 and product == 2:
                                        end(last, f"fc{i}{c}")
                elif kind == "scan":
                    c = which
                    for p in range(2):
                        rows = slice(64 * p, 64 * p + 64)
                        yb = bank[plan[f"y{i}{p}"][0]]
                        for m in range(4):
                            last = pe.matmul(yb[64 * c:64 * c + 64, m * DH:(m + 1) * DH],
                                             ar[rows, m, i, 1, 64 * c:64 * c + 64], state[rows, (2 * i + c) % 2, m, :],
                                             start=False, stop=True, skip_group_check=True)
                        if c == 1:
                            end(last, f"y{i}{p}")
                elif kind == "finish":
                    pe.wait_ge(q["ynorm_ready"], i + 1)
                    turned(f"yT{i}", [ynorm[:, m * P:(m + 1) * P] for m in range(4)])

            def after(step):
                kind, i, _ = step
                if kind == "local":
                    ybank = [begin(f"y{i}{p}") for p in range(2)]
                    for h in range(RH):
                        m, p = h // 2, h % 2
                        oo = ybank[p][:, m * DH:(m + 1) * DH]
                        pe.matmul(oo, amat[:, h, 1, :], rhs[:, h, 1, :], start=(m == 0), stop=False, skip_group_check=True)
                        pe.matmul(oo, amat[:, h, 3, :], vrow[:, h * DH:(h + 1) * DH], start=False, stop=False,
                                  skip_group_check=True)

            def turned(name, parts):
                o = begin(name)
                for b, part in enumerate(parts):
                    last = pe.transpose(o[:, b * P:(b + 1) * P], part, ident)
                end(last, name)

            def products(i, heads):
                pe.wait_ge(q["padded_ready"], 2 * i + heads[0] // 4 + 1)
                for h in heads:
                    m, p = h // 2, h % 2
                    o = begin(f"A{i}{h}")
                    for j, left in enumerate((bf, kf)):
                        last = pe.matmul(o[:, j * S:(j + 1) * S], left[:, m, i * P:(i + 1) * P], padded[:, m % 2, p, :],
                                         start=True, stop=True)
                    end(last, f"A{i}{h}")

            def scores(g, u):
                p = u % 2
                o = begin(f"s{g}{u}")
                for hp in range(2):
                    i = 0 if u < 2 else 1
                    keys = kT[:, p, :, g, 0:P] if u < 2 else kT[:, p, (u - 2) // 2, g, :]
                    last = pe.matmul(o[:, hp * S:(hp + 1) * S], qT[:, 2 * g + hp, i * P:(i + 1) * P], keys,
                                     start=True, stop=True)
                end(last, f"s{g}{u}")

            def turn(g, u):
                n = g * 6 + u
                pe.wait_ge(q["prob_ready"], n + 1)
                turned(f"pT{g}{u}", [prob[:, n % 2, s * P:(s + 1) * P] for s in (0, 2, 1, 3)])

            def weigh(g, u, o):
                pe.wait_ge(q["probT_ready"], g * 6 + u + 1)
                i = 0 if u < 2 else 1
                for b in range(2):
                    br, kb = (b, 0) if u < 2 else ((u - 2) // 2, b)
                    for p in range(2):
                        last = pe.matmul(o[64 * p:64 * p + 64, :].rearrange("p (h t) -> p h t", h=2)[:, :, i * P:(i + 1) * P],
                                         vtok[:, br, kb, g * DH:(g + 1) * DH], probT[:, p, b * 2 * P:(b + 1) * 2 * P],
                                         start=False, stop=(b == 1 and (u < 2 or u >= 4)), skip_group_check=True)
                return last

            def turn_compressed(g, i):
                nc_ = 7 if i == 0 else NCMP
                o = begin(f"cT{g}{i}")
                for b in range(4):
                    p, hp = b // 2, b % 2
                    last = pe.transpose(o[0:nc_, b * P:(b + 1) * P], cprob[i][:, 4 * g + 2 * hp + p, :], ident)
                end(last, f"cT{g}{i}")

            pe.wait_ge(q["q_ready"], 4)
            pe.wait_ge(q["cmp_kv_ready"], 2)
            for i in range(NT):
                nc_ = 7 if i == 0 else NCMP
                o = begin(f"cs{i}")
                for m in range(8):
                    g = m // 2
                    last = pe.matmul(o[:, 2 * m * nc_:2 * (m + 1) * nc_], qT[:, m, i * P:(i + 1) * P],
                                     kcb[:, :, g * NCMP:g * NCMP + nc_], start=True, stop=True)
                end(last, f"cs{i}")
            for s in range(BEFORE):
                early(RWKV_STEPS[s])
                late(RWKV_STEPS[s])
                if s == 0:
                    project("kw", C_KW)
                elif s == 1:
                    values("vs", C_VS)
                elif s == 2:
                    pe.wait_ge(q["k_ready"], 2)
                    scores(0, 0)
                    scores(0, 1)
                    values("vw", C_VW)
            pe.wait_ge(q["v_ready"], 2)

            def gate_matmuls(share):
                for x in share:
                    j, m, k = x // (2 * KD), x // KD % 2, x % KD
                    w = chunk(C_GATE + j).rearrange("p (k c) -> p k c", k=KD)
                    o = begin(f"mg{j}") if m == k == 0 else bank[plan[f"mg{j}"][0]]
                    last = mm(o[:, m * S:(m + 1) * S], w[:, k, m * P:(m + 1) * P], hT[:, k, :], k, KD)
                    if m == 1 and k == KD - 1:
                        end(last, f"mg{j}")
                        pe_take()

            pe.wait_ge(q["cprob_ready"], 2)
            steps = iter(RWKV_STEPS[BEFORE:DURING])
            slot = iter(range(DURING - BEFORE))
            for n, (g, u) in enumerate(UNITS):
                if u == 0:
                    step = next(steps)
                    turn_compressed(g, 0)
                    early(step)
                    turn_compressed(g, 1)
                    late(step)
                    acc = begin(f"o{g}")
                    for i in range(NT):
                        nc_ = 7 if i == 0 else NCMP
                        pe.wait_ge(q["cprobT_ready"], 2 * g + i + 1)
                        for p in range(2):
                            last = pe.matmul(acc[64 * p:64 * p + 64, :].rearrange("p (h t) -> p h t", h=2)[:, :, i * P:(i + 1) * P],
                                             vcb[0:nc_, g, :], cprobT[0:nc_, i, 2 * p:2 * p + 2, :], start=(i == 0),
                                             stop=False, skip_group_check=True)
                    gate_matmuls(gate_share(next(slot)))
                step = next(steps)
                early(step)
                if n + 2 < len(UNITS):
                    scores(*UNITS[n + 2])
                turn(g, u)
                late(step)
                if u % 2:
                    last = weigh(g, u, acc)
                if u == 5:
                    end(last, f"o{g}")
                gate_matmuls(gate_share(next(slot)))
                after(step)

            for j in range(NEARLY, NGATE):
                x = 2 * KD * j
                if j in beside:
                    early(beside[j])
                gate_matmuls(range(x, x + KD))
                if j < NGATE - 1 and j in beside:
                    late(beside[j])
                gate_matmuls(range(x + KD, x + 2 * KD))
                if j in beside:
                    after(beside[j])

            pe.wait_ge(q["pool_out"], 2)
            pe.wait_ge(q["nsa_ready"], NG)
            for n in range(4):
                for b in BRANCHES:
                    if b != 1:
                        c = C_BRANCH + 2 * n + (0 if b == 2 else 1)
                        w = chunk(c).rearrange("p (k c) -> p k c", k=KD)
                    if n == 0 and b == 1:
                        pe.wait_ge(q["yrw_ready"], NT)
                    o = begin(f"mb{n}{b}")
                    k0, nk = ((0, 4), (4, 4), (0, 8))[b]
                    for m in range(2):
                        for k in range(nk):
                            last = mm(o[:, m * S:(m + 1) * S], w[:, k0 + k, m * P:(m + 1) * P],
                                      yT[:, (8 if b == 2 else 0) + k0 + k, :], k, nk)
                    end(last, f"mb{n}{b}")
                    if b:
                        pe_take()
                    if n == 0 and b == 2:
                        late(beside[NGATE - 1])
            def output(n, tiles):
                w = chunk(C_OUT + n).rearrange("p (k c) -> p k c", k=KD)
                o = begin(f"out{n}") if 0 in tiles else bank[plan[f"out{n}"][0]]
                for i in tiles:
                    for k in range(KD):
                        if n == 0 and i == 0 and k % 2 == 0:
                            pe.wait_ge(q["merged_ready"], k // 2 + 1)
                        last = mm(o[:, i * 256:(i + 1) * 256], merged[:, k, i * P:(i + 1) * P], w[:, k, :], k, KD)
                if 1 in tiles:
                    end(last, f"out{n}")
                    pe_take()

            def turn_sum(n):
                pe.wait_ge(q["sum_ready"], n + 1)
                o = begin(f"hT2{n}")
                for b in range(4):
                    i, k = b % 2, 2 * n + b // 2
                    last = first(pe.transpose(o[:, b * P:(b + 1) * P], tok[:, i, k * P:(k + 1) * P], ident))
                end(last, f"hT2{n}")

            def route(n):
                pe.wait_ge(q["hT_ready"], 2 + n + 1)
                w = chunk(C_ROUTER)[:, 0:8 * 36].rearrange("p (k c) -> p k c", k=KD)
                o = begin("router") if n == 0 else bank[plan["router"][0]]
                for k in range(2 * n, 2 * n + 2):
                    for i in range(NT):
                        last = pe.matmul(o[:, i * 36:(i + 1) * 36], hT[:, k, i * P:(i + 1) * P], w[:, k, :],
                                         start=(k == i == 0), stop=(k == KD - 1), skip_group_check=True)
                return last

            output(0, (0, 1))
            output(1, (0, 1))
            turn_sum(0)
            output(2, (0, 1))
            turn_sum(1)
            route(0)
            output(3, (0,))
            route(1)
            output(3, (1,))
            turn_sum(2)
            turn_sum(3)
            route(2)
            end(route(3), "router")
            full(pe, "router")
            pe.sem_inc(taken, owed[0] + 1)
            pe.wait_ge(q["member_ready"], 1)
            o = begin("places")
            pe.matmul(o[:, 0:E], cn("earlier"), member[:, 0, :], start=True, stop=True)
            pe.matmul(o[:, E:2 * E], cn("ones"), member[:, 0, :], start=True, stop=False)
            pe.matmul(o[:, E:2 * E], cn("earlier"), member[:, 1, :], start=False, stop=True)
            pe.matmul(o[:, 2 * E:3 * E], cn("ones"), member[:, 0, :], start=True, stop=False)
            end(pe.matmul(o[:, 2 * E:3 * E], cn("ones"), member[:, 1, :], start=False, stop=True), "places")

            pe.wait_ge(q["crowd_ready"], 1)
            most = pe.value_load(crowd[0:1, 0:1], min_val=0, max_val=S)

            def gathered_experts():
                with pe.Fori(0, NGANG) as gang:
                    pe.wait_ge(q["sel_ready"], gang + 1)
                    pe.wait_ge(q["xn2_ready"], NT)
                    for b in range(2):
                        if b == 0:
                            for j in range(8):
                                pe.wait_ge(bank_free[j], before_loop[j])
                        for kk in range(4):
                            k = 4 * b + kk
                            for i in range(NT):
                                last = pe.matmul(bank[b][:, kk * P:(kk + 1) * P], xn[:, i, k * P:(k + 1) * P],
                                                 sel[:, i, :], start=(i == 0), stop=(i == 1))
                        last.then_inc(q["gathered"], 1)
                    for i in range(NT):
                        last = pe.transpose(bank[3][:, (2 + i) * P:(3 + i) * P], wsel[:, i, :], ident)
                    last.then_inc(q["wsel_turned"], 1)
                    for k in range(KD):
                        pe.wait_ge(loaded[k], gang * 16 + 16 * ((NFRONT // FRING if k < FRING else 0) + 1))
                        if k % 4 == 0:
                            pe.wait_ge(q["gath_ready"], gang * 2 + (k // 4 + 1))
                        w = ring[:, k * SLOT:(k + 1) * SLOT].rearrange("p (e n) -> p e n", e=GANG)
                        for e in range(GANG):
                            last = pe.matmul(bank[2][CAP * e:CAP * (e + 1), :], gath[:, k, CAP * e:CAP * (e + 1)],
                                             w[:, e, :], start=(k == 0), stop=(k == KD - 1))
                            if k and e == 0:
                                last.then_inc(taken, 1)
                    last.then_inc(q["gate_up"], 1)
                    pe.wait_ge(q["ghid_ready"], gang + 1)
                    pe.wait_ge(q["wselT_ready"], gang + 1)
                    for f in range(2):
                        last = pe.transpose(bank[3][:, f * P:(f + 1) * P], ghid[:, f * P:(f + 1) * P], ident)
                        if f == 0:
                            last.then_inc(taken, 1)
                    last.then_inc(q["hid_turned"], 1)
                    for e in range(GANG):
                        pe.wait_ge(loaded[8 + e], gang * 16 + 16)
                    pe.wait_ge(q["ghidT_ready"], gang + 1)
                    for n in range(2):
                        for f in range(2):
                            for e in range(GANG):
                                w = ring[:, (8 + e) * SLOT:(9 + e) * SLOT].rearrange("p (f d) -> p f d", f=2)
                                last = pe.matmul(bank[4 + n][CAP * e:CAP * (e + 1), :], ghidT[:, f, CAP * e:CAP * (e + 1)],
                                                 w[:, f, n * 512:(n + 1) * 512], start=(f == 0), stop=(f == 1))
                        last.then_inc(q["downed"], 1)
                    for j in range(4):
                        n, i = j // 2, j % 2
                        if i == 0:
                            pe.wait_ge(q["ydown_ready"], gang * 2 + n + 1)
                        if j >= 2:
                            pe.wait_ge(q["summed"], gang * 4 + (j - 1))
                        last = pe.matmul(bank[6 + i][:, :], wselT[:, i, :], ydown[:, n * 512:(n + 1) * 512],
                                         start=True, stop=True)
                        last.then_inc(q["scattered"], 1)
                    pe.wait_ge(q["scattered"], gang * 4 + 4)
                    pe.sem_inc(taken, 4)
                    pe.wait_ge(q["summed"], gang * 4 + 4)

            def dense_experts():
                with pe.Fori(0, NGANG) as gang:
                    for c in range(GCH):
                        first = NFRONT // FRING if c < FRING else 0
                        pe.wait_ge(loaded[c], gang * 16 + 16 * (first + 1))
                    for i in range(NT):
                        slot = [ring[:, c * SLOT:(c + 1) * SLOT].rearrange("p (e n) -> p e n", e=GANG) for c in range(8)]
                        for e in range(GANG):
                            pe.wait_ge(bank_free[e], gang * 2 + (before_loop[e] + i))
                            for k in range(KD):
                                last = pe.matmul(bank[e][:, :], hT[:, k, i * P:(i + 1) * P], slot[k][:, e, :],
                                                 start=(k == 0), stop=(k == KD - 1))
                            last.then_inc(bank_full[e], 1)
                        for half in range(2):
                            pe.wait_ge(q["hid_ready"], gang * 8 + (4 * i + 2 * half + 2))
                            pe.wait_ge(bank_free[4 + half], gang * 2 + (before_loop[4 + half] + i))
                            for e in range(2):
                                for f in range(2):
                                    last = pe.transpose(bank[4 + half][:, (2 * e + f) * P:(2 * e + f + 1) * P],
                                                        hid[:, 2 * half + e, f * P:(f + 1) * P], ident)
                            last.then_inc(bank_full[4 + half], 1)
                        pe.wait_ge(q["hidT2_ready"], gang * 4 + (2 * i + 2))
                        for n in range(2):
                            pe.wait_ge(bank_free[6 + n], gang * 2 + (before_loop[6 + n] + i))
                            for e in range(GANG):
                                down = ring[:, (8 + e) * SLOT:(9 + e) * SLOT].rearrange("p (f d) -> p f d", f=2)
                                for f in range(2):
                                    last = pe.matmul(bank[6 + n][:, :], hidm[:, e, f, :], down[:, f, n * 512:(n + 1) * 512],
                                                     start=(e == 0 and f == 0), stop=(e == GANG - 1 and f == 1))
                            last.then_inc(bank_full[6 + n], 1)
                    pe.wait_ge(bank_full[7], gang * 2 + (before_loop[7] + 2))
                    pe.sem_inc(taken, GCH)

            with pe.If(most <= CAP):
                gathered_experts()
            with pe.Else():
                dense_experts()

        @block.gpsimd
        def _(pool):
            pool.memset(rawf[:, :], 0.0).then_inc(q["raw_zeroed"], 1)
            pool.memset(state[:, 0, :, :], 0.0).then_inc(q["state_zeroed"], 1)
            pool.wait_ge(q["lead_loaded"], 32)

            def inverse_root(n, lo, hi):
                pool.wait_ge(q["rms_in"], n + 1)
                pool.tensor_tensor(stat[:, 8 + lo:8 + hi], stat[:, lo:hi], cn("neghalf")[:, lo:hi], ALU.pow)\
                    .then_inc(q["root_ready"], 1)

            for i in range(NT):
                inverse_root(i, i, i + 1)
            pool.wait_ge(q["small_loaded"], 32)
            level = cn("level").rearrange("p (n t) -> p n t", n=6)
            for i in range(NT):
                pool.wait_ge(*((q["rwkv_ready"], 1) if i == 0 else (q["ynorm_ready"], i)))
                pool.memset(t3[:, :, :], 0.0).then_inc(q["padded_zeroed"], 1)
                for grp in range(2):
                    turn_ = 2 * i + grp
                    for n in range(6):
                        if n == 0:
                            pool.wait_ge(q["amat_ready"], 8 * i + 8)
                            if grp:
                                full(pool, f"W{i}{grp - 1}4")
                        elif n == 1:
                            pool.wait_ge(q["z_ready"], 6 * turn_ + 1)
                        else:
                            full(pool, f"W{i}{grp}{n - 2}")
                        pool.tensor_tensor(lmask, amat[:, 4 * grp:4 * grp + 4, 0, :],
                                           like(level[:, n:n + 1, :], [P, 4, P]), ALU.mult)\
                            .then_inc(q["lmask_ready"], 1)
                inverse_root(NT + i, 0, RH)
            for n in range(2):
                for i in range(NT):
                    inverse_root((2 + n) * NT + i, i, i + 1)

        @block.scalar
        def _(act):
            def copy(o, i_, scale=1.0):
                return act.activation(o, i_, ACT.Copy, scale=scale)

            def flat(o):
                return o[:, :].rearrange("p (a t) -> p a t", a=2)

            count = {}

            def give(ins, name, job):
                count[name] = count.get(name, 0) + 1
                ins.then_inc(q[name], 1)
                act.wait_ge(q[name], count[name])
                act.sem_inc(bank_free[plan[job][0]], 1)

            def to_hT(jobs, gain):
                for n in (1, 3):
                    i, k0 = n // 2, (n % 2) * 4
                    b0 = full(act, f"{jobs}{n}")
                    for k in range(4):
                        ins = copy(hT[:, k0 + k, i * P:(i + 1) * P], b0[:, k * P:(k + 1) * P],
                                   scale=pr(gain)[:, k0 + k:k0 + k + 1])
                    give(ins, "hT_odd_ready", f"{jobs}{n}")

            act.wait_ge(q["lead_loaded"], 32)
            copy(small[:, 255:256], ident[:, 0:1])
            to_hT("xT", "g_mix")
            act.wait_ge(q["raw_zeroed"], 1)
            b0 = full(act, "lora_in")
            copy(raw[0:64, 0, 0, 1:S + 1], b0[0:64, 0:S])
            ins = copy(raw[0:96, 0, 1, 1:S + 1], b0[0:96, S:2 * S])
            ins.then_inc(q["raw_ready"], 1)
            count["raw_ready"] = 1
            give(act.activation(gates_f, b0[64:112, 0:S], ACT.Tanh, scale=0.5), "gate_tanh", "lora_in")
            for n in range(2):
                b0 = full(act, f"pool{n}")
                give(copy(t1[:, 2 * n:2 * n + 2, :], flat(b0)), "u_ready", f"pool{n}")
            for c in range(1, 7):
                if c >= 2:
                    act.wait_ge(q["raw_used"], c - 1)
                b0 = full(act, f"rkv{c}")
                give(copy(raw[:, c % 2, :, 1:S + 1], flat(b0)), "raw_ready", f"rkv{c}")
                if c == 2:
                    act.wait_ge(q["mix_ready"], 1)
                    act.activation(mix[0:32, 12, :], mix[0:32, 12, :], ACT.Tanh).then_inc(q["lora_w_ready"], 1)
                    act.activation(mix[0:96, 13, :], mix[0:96, 13, :], ACT.Tanh, scale=0.5)\
                        .then_inc(q["lora_g_tanh"], 1)
            for n in range(8):
                b0 = full(act, f"bias{n}")
                give(copy(bias[:, 2 * n:2 * n + 2, :], flat(b0), scale=-1.0), "bias_ready", f"bias{n}")
            act.wait_ge(q["halves_ready"], 1)
            act.wait_ge(q["pool_ready"], 1)
            for n in range(2):
                b0 = full(act, f"wup{n}")
                for m in range(2):
                    c = 2 * n + m
                    ins = act.activation(t1[:, c, :], b0[:, m * S:(m + 1) * S], ACT.Tanh, bias=halves[:, c:c + 1], scale=0.5)
                give(ins, "decay_tanh", f"wup{n}")
            for n in range(2):
                b0 = full(act, f"aup{n}")
                for m in range(2):
                    c = 2 * n + m
                    ins = act.activation(kf[:, c, :], b0[:, m * S:(m + 1) * S], ACT.Tanh, bias=halves[:, 4 + c:5 + c],
                                         scale=0.5)
                give(ins, "rate_tanh", f"aup{n}")
            for b, name in enumerate(("kc", "vc")):
                b0 = full(act, name)
                for gp in range(2):
                    src = flat(b0[64 * gp:64 * gp + 64, :])
                    copy(kshift[0:64, b, gp::2, :], src)
                    ins = copy(kshift[64:128, b, gp::2, 0:S - 1], src[:, :, 1:S])
                give(ins, "kshift_ready", name)
            act.wait_ge(q["kk_max"], 2)
            act.activation(t3[:, :, :], t3[:, :, :], ACT.Sqrt).then_inc(q["kk_root"], 1)
            act.wait_ge(q["log_ready"], 1)
            act.activation(t3[:, :, :], t2[:, :, :], ACT.Exp).then_inc(q["decay_exp"], 1)
            act.wait_ge(q["log_ready"], 2)
            act.activation(t1[:, :, :], t1[:, :, :], ACT.Exp).then_inc(q["decay_exp"], 1)
            act.activation(t2[:, :, :], t2[:, :, :], ACT.Exp, scale=-1.0).then_inc(q["decay_exp"], 1)
            def queries(n):
                b0 = full(act, f"q{n}")
                give(copy(qT[:, 2 * n:2 * n + 2, :], flat(b0), scale=-DH ** -0.5), "q_ready", f"q{n}")

            def keys(b, name):
                act.wait_ge(q["keys_zeroed"], 2)
                b0 = full(act, name)
                for gp in range(2):
                    src = flat(b0[64 * gp:64 * gp + 64, :])
                    copy(kT[0:64, 0, b, gp::2, :], src)
                    ins = copy(kT[64:128, 1, b, gp::2, :], src)
                give(ins, "k_ready", name)

            def values(b, name):
                b0 = full(act, name)
                give(copy(vtok[:, b, :, :], flat(b0)), "v_ready", name)

            queries(0)
            queries(1)
            for b, name in enumerate(("mlp_k", "mlp_v")):
                b0 = full(act, name)
                give(copy(gx[:, b * 256:(b + 1) * 256], b0[0:60, 0:256]), "gx_ready", name)
            act.wait_ge(q["gelu_in"], 1)
            act.activation(gy, gy, ACT.Tanh, scale=GELU_C).then_inc(q["gelu_tanh"], 1)
            queries(2)
            queries(3)
            b0 = full(act, "hidT")
            give(copy(hidT, b0[:, 0:240].rearrange("p (f n) -> p f n", f=4)), "hidT_ready", "hidT")
            keys(0, "ks")
            b0 = full(act, "kcb")
            act.wait_ge(q["keys_zeroed"], 4)
            for p in range(2):
                ins = copy(kcb[64 * p:64 * p + 64, p, :], b0[64 * p:64 * p + 64, 0:60])
            give(ins, "cmp_kv_ready", "kcb")
            b0 = full(act, "vcb")
            give(copy(vcb, b0[0:NCMP, 0:256].rearrange("p (g v) -> p g v", g=NG)), "cmp_kv_ready", "vcb")

            def early(step):
                kind, i, which = step
                if kind == "turn":
                    for w_, dst in enumerate((btok, ktok)):
                        b0 = full(act, f"tok{i}{w_}")
                        give(copy(dst, b0[:, :]), "tok_ready", f"tok{i}{w_}")
                elif kind == "level":
                    name = "W%d%d%d" % (i, *which)
                    b0 = full(act, name)
                    give(copy(winv, b0[:, :].rearrange("p (h t) -> p h t", h=4)), "w_ready", name)
                elif kind == "solve":
                    b0 = full(act, f"w0{i}")
                    give(copy(rhs[:, :, 1, :], b0[:, :].rearrange("p (h v) -> p h v", h=RH)), "rhs_ready", f"w0{i}")

            def late(step):
                kind, i, which = step
                if kind == "turn":
                    b0 = full(act, f"tok{i}2")
                    give(copy(vrow, b0[:, :]), "tok_ready", f"tok{i}2")
                    b0 = full(act, f"atok{i}")
                    give(copy(rhs[:, :, 0, :], b0[:, :].rearrange("p (h v) -> p h v", h=RH)), "tok_ready", f"atok{i}")
                    if i == 0:
                        pad(0, 0)
                elif kind == "products" and which == 0:
                    full(act, f"A{i}3")
                    pad(i, 1)
                elif kind == "solve":
                    for n in range(2):
                        b0 = full(act, f"xu{i}{n}")
                        give(copy(rhs[:, 4 * n:4 * n + 4, :, :], b0[:, :].rearrange("p (h j v) -> p h j v", h=4, j=2)),
                             "xu_ready", f"xu{i}{n}")
                elif kind == "finish":
                    b0 = full(act, f"yT{i}")
                    for m in range(4):
                        ins = act.activation(yT[:, 4 + m, i * P:(i + 1) * P], b0[:, m * P:(m + 1) * P], ACT.Identity,
                                             bias=pr("gn_b")[:, m:m + 1], scale=pr("gn_w")[:, m:m + 1])
                    give(ins, "gn_ready", f"yT{i}")
                    if i + 1 < NT:
                        pad(i + 1, 0)

            def pad(i, which):
                act.wait_ge(q["padded_zeroed"], i + 1)
                for m in range(2):
                    for p in range(2):
                        rows = slice(64 * p, 64 * p + 64)
                        ins = copy(padded[rows, m, p, :], ar[rows, 2 * which + m, i, :, :].rearrange("p j t -> p (j t)"))
                ins.then_inc(q["padded_ready"], 1)

            def exps(g, u):
                n = 6 * g + u
                act.wait_ge(q["exp_in"], n + 1)
                nb, w = (4, P) if u < 2 else (2, S)
                for b in range(nb):
                    pb = prob[:, n % 2, b * w:(b + 1) * w]
                    ins = act.activation(pb, pb, ACT.Exp, scale=-1.0, bias=astat[:, 8 * (n % 2) + b:8 * (n % 2) + b + 1],
                                         accum_out=astat[:, 16 + 8 * (n % 2) + b:17 + 8 * (n % 2) + b])
                ins.then_inc(q["exp_ready"], 1)

            def turned_compressed(g, i):
                nc_ = 7 if i == 0 else NCMP
                b0 = full(act, f"cT{g}{i}")
                give(copy(cprobT[0:nc_, i, :, :], b0[0:nc_, :].rearrange("p (h t) -> p h t", h=4)), "cprobT_ready",
                     f"cT{g}{i}")

            def gate_tanh(gates):
                for j in gates:
                    b0 = full(act, f"mg{j}")
                    for m in range(2):
                        c = 8 + 8 * (j % 3) + 2 * (j // 3) + m
                        ins = act.activation(gsig[j][:, m, :], b0[:, m * S:(m + 1) * S], ACT.Tanh,
                                             bias=halves[:, c:c + 1], scale=0.5)
                    give(ins, "gsig_ready", f"mg{j}")

            for s in range(BEFORE):
                early(RWKV_STEPS[s])
                late(RWKV_STEPS[s])
                if s == 0:
                    for i in range(NT):
                        act.wait_ge(q["cexp_in"], i + 1)
                        act.activation(cprob[i], cprob[i], ACT.Exp, scale=-1.0).then_inc(q["cexp_ready"], 1)
                    keys(1, "kw")
                elif s == 1:
                    values(0, "vs")
            exps(0, 0)
            values(1, "vw")
            steps = iter(RWKV_STEPS[BEFORE:DURING])
            slot = iter(range(DURING - BEFORE))
            for n, (g, u) in enumerate(UNITS):
                if u == 0:
                    step = next(steps)
                    turned_compressed(g, 0)
                    early(step)
                    turned_compressed(g, 1)
                    late(step)
                    gate_tanh(gates_done(next(slot) - 1))
                step = next(steps)
                early(step)
                if n + 1 < len(UNITS):
                    exps(*UNITS[n + 1])
                b0 = full(act, f"pT{g}{u}")
                give(copy(probT[:, n % 2, :], b0[:, :]), "probT_ready", f"pT{g}{u}")
                late(step)
                gate_tanh(gates_done(next(slot) - 1))
            gate_tanh(gates_done(DURING - BEFORE - 1))

            act.wait_ge(q["nsa_ready"], NG)
            act.dma_start(tok[:, :, :], x.rearrange("(i p) d -> p i d", p=P)).then_inc(q["x_again"], 16)

            def first_gang(s):
                act.dma_start(ring[:, s * SLOT:(s + 1) * SLOT], experts[0, s]).then_inc(loaded[s], 16)

            for s in (8, 9, 10):
                first_gang(s)
            for j in range(NEARLY, NGATE):
                if j in beside:
                    early(beside[j])
                    if j < NGATE - 1:
                        late(beside[j])
                gate_tanh([j])
            late(beside[NGATE - 1])

            act.wait_ge(q["yrw_ready"], NT)
            first_gang(6)
            first_gang(7)
            act.wait_ge(q["gated"], NGATE)
            for s in (4, 5, 11):
                first_gang(s)
            act.wait_ge(q["merged_ready"], 4)
            act.dma_start(gfin, g_final).then_inc(q["gfin_loaded"], 16)
            for i in range(NT):
                act.wait_ge(q["root_ready"], 2 * NT + i + 1)
                copy(xn[:, i, :], tok[:, i, :], scale=stat[:, 8 + i:9 + i]).then_inc(q["xn2_ready"], 1)

            act.wait_ge(q["router_in"], 1)
            act.activation(rt("ge"), rt("ge"), ACT.Exp).then_inc(q["router_exp"], 1)
            act.wait_ge(q["router_in"], 2)
            act.activation(rt("w2"), rt("w2"), ACT.Exp).then_inc(q["router_exp"], 1)

            act.wait_ge(q["crowd_ready"], 1)
            most = act.value_load(crowd[0:1, 0:1], min_val=0, max_val=S)

            def gathered_experts():
                with act.Fori(0, NGANG) as gang:
                    act.wait_ge(q["wsel_turned"], gang + 1)
                    copy(wselT, bank[3][:, 2 * P:4 * P].rearrange("p (i t) -> p i t", i=2)).then_inc(q["wselT_ready"], 1)
                    act.wait_ge(q["gate_up"], gang + 1)
                    act.activation(gtanh, bank[2][:, 0:DE], ACT.Tanh, scale=0.5).then_inc(q["gtanh_ready"], 1)
                    act.wait_ge(q["hid_turned"], gang + 1)
                    copy(ghidT, bank[3][:, 0:2 * P].rearrange("p (f s) -> p f s", f=2)).then_inc(q["ghidT_ready"], 1)
                    for n in range(2):
                        act.wait_ge(q["downed"], gang * 2 + n + 1)
                        copy(ydown[:, n * 512:(n + 1) * 512], bank[4 + n][:, :]).then_inc(q["ydown_ready"], 1)

            def dense_experts():
                half_root = stat[:, 34:36]
                with act.Fori(0, NGANG) as gang:
                    for i in range(NT):
                        for e in range(GANG):
                            act.wait_ge(bank_full[e], gang * 2 + (before_loop[e] + i + 1))
                            act.activation(gsi[:, e, :], bank[e][:, 0:DE], ACT.Tanh, scale=half_root[:, i:i + 1]).then_inc(q["silu_tanh"], 1)
                        for half in range(2):
                            act.wait_ge(bank_full[4 + half], gang * 2 + (before_loop[4 + half] + i + 1))
                            copy(hidm[:, 2 * half:2 * half + 2, :, :],
                                 bank[4 + half][:, :].rearrange("p (e f t) -> p e f t", e=2, f=2))\
                                .then_inc(q["hidT2_ready"], 1)

            with act.If(most <= CAP):
                gathered_experts()
            with act.Else():
                dense_experts()

        @block.vector
        def _(dve):
            chain = chainer(dve, "dve_chain")

            def flat(o):
                return o[:, :].rearrange("p (a t) -> p a t", a=2)

            def tt(o, a, b, op):
                return dve.tensor_tensor(o, a, b, op)

            def ts(o, a, s1, s2, op0, op1=None):
                return dve.tensor_scalar(o, a, s1, s2, op0, op1) if op1 is not None else \
                    dve.tensor_scalar(o, a, s1, None, op0)

            def stt(o, a, s1, b, op0, op1):
                return dve.scalar_tensor_tensor(out=o, in0=a, scalar=s1, in1=b, op0=op0, op1=op1)

            roots = [0]

            def row_roots(src, summed=False, first=False):
                for i in range(NT):
                    total = stat[:, 16 + i:17 + i]
                    if summed:
                        chain(dve.tensor_reduce(total, stat[:, 24 + 4 * i:28 + 4 * i], AXX, ALU.add))
                    else:
                        if first:
                            dve.wait_ge(q[f"x_loaded{i}"], 16)
                        squares(src[:, i, :], total)
                    roots[0] += 1
                    chain(ts(stat[:, i:i + 1], total, 1.0 / D, 1e-6, ALU.mult, ALU.add), "rms_in")

            def squares(row, total, at=0, hold=True):
                o = t1[:, :, :].rearrange("p c t -> p (c t)")[:, at:at + row.shape[-1]]
                chain(dve.tensor_tensor_reduce(o, row, row, 1.0, 0.0, ALU.mult, ALU.add, total), hold=hold)

            def normalise(src, **how):
                row_roots(src, **how)
                for i in range(NT):
                    dve.wait_ge(q["root_ready"], roots[0] - NT + 1 + i)
                    chain(ts(xn[:, i, :], src[:, i, :], stat[:, 8 + i:9 + i], None, ALU.mult), "xn_ready")

            def to_hT(jobs, gain):
                for n in (0, 2):
                    i, k0 = n // 2, (n % 2) * 4
                    b0 = full(dve, f"{jobs}{n}")
                    chain(tt(hT[:, k0:k0 + 4, i * P:(i + 1) * P], b0[:, :].rearrange("p (k t) -> p k t", k=4),
                             like(pr(gain)[:, k0:k0 + 4, None], [P, 4, P]), ALU.mult), "hT_ready")
                    dve.sem_inc(bank_free[plan[f"{jobs}{n}"][0]], 1)

            normalise(tok, first=True)
            dve.wait_ge(q["lead_loaded"], 32)
            to_hT("xT", "g_mix")
            for lo, hi, name in ((0, 4, "w0"), (4, 8, "a0"), (8, 32, "b_merge")):
                ins = ts(halves[:, lo:hi], pr(name), 0.5, None, ALU.mult)
                chain(ins, "halves_ready" if name == "b_merge" else None)
            for p in range(2):
                chain(dve.memset(kT[64 * (1 - p):64 * (1 - p) + 64, p, :, :, :], 0.0), "keys_zeroed", hold=False)

            def shift(rows, c, j, tiles):
                r_ = raw[rows, c % 2, j, :]
                chain(tt(mix[rows, tiles, :], r_[:, :, 0:S], r_[:, :, 1:S + 1], ALU.subtract))
                for k in range(tiles.stop - tiles.start):
                    t = tiles.start + k
                    chain(stt(mix[rows, t, :], mix[rows, t, :], pr("mu")[rows, t:t + 1], r_[:, k, 1:S + 1],
                              ALU.mult, ALU.add))

            dve.wait_ge(q["raw_ready"], 1)
            shift(slice(0, 64), 0, slice(0, 1), slice(12, 13))
            shift(slice(0, 96), 0, slice(1, 2), slice(13, 14))
            dve.sem_inc(q["raw_used"], 1)
            dve.sem_inc(q["mix_ready"], 1)
            b0 = full(dve, "gates")
            chain(ts(gate_t[:, :, :].rearrange("p i n -> p (i n)"), b0[:, 0:2 * 3 * NH], 0.5, 0.5, ALU.mult, ALU.add),
                  "gates_ready")
            dve.sem_inc(bank_free[plan["gates"][0]], 1)
            b0 = full(dve, "brow")
            ins = dve.tensor_copy(arbk[0:NH, 0:2, :].rearrange("p a b -> p (a b)")[:, 0:384], b0[0:NH, 0:384])
            chain(ins, "win_row")
            dve.sem_inc(bank_free[plan["brow"][0]], 1)
            dve.wait_ge(q["small_loaded"], 32)

            dve.wait_ge(q["u_ready"], 2)
            sums = [None, t2, t3, t2, t3]
            for lv in range(1, 5):
                w = 2 ** (lv - 1)
                src, dst = (t1 if lv == 1 else sums[lv - 1]), sums[lv]
                gs = slice(lv - 1, 4)
                chain(dve.tensor_copy(dst[:, gs, 0:w], src[:, gs, 0:w]), hold=False)
                chain(tt(dst[:, gs, w:S], src[:, gs, w:S], src[:, gs, 0:S - w], ALU.add))
            cnt = cn("count").rearrange("p (g t) -> p g t", g=4)
            for gi in range(4):
                src = sums[gi + 1]
                chain(stt(yT[:, gi, :], src[:, gi, :], 0.5 ** (gi + 1), t1[:, gi, :], ALU.mult, ALU.subtract))
                chain(tt(src[:, gi, 0:16], src[:, gi, 0:16], cnt[:, gi, :], ALU.mult))
                ins = tt(yT[:, gi, 0:16], src[:, gi, 0:16], t1[:, gi, 0:16], ALU.subtract)
                chain(ins, "pool_ready" if gi == 3 else None)

            for c in range(1, 7):
                dve.wait_ge(q["raw_ready"], c + 1)
                shift(slice(0, P), c, slice(0, 2), slice(2 * c - 2, 2 * c))
                dve.sem_inc(q["raw_used"], 1)
            dve.wait_ge(q["lora_g_tanh"], 1)
            chain(ts(mix[0:96, 13, :], mix[0:96, 13, :], 0.5, 0.5, ALU.mult, ALU.add), "lora_g_ready")
            for n in range(2):
                b0 = full(dve, f"poolmix{n}")
                chain(tt(yT[:, 2 * n:2 * n + 2, :], flat(b0),
                         like(pr("pool_scale")[:, 2 * n:2 * n + 2, None], [P, 2, S]), ALU.mult), "pool_out")
                dve.sem_inc(bank_free[plan[f"poolmix{n}"][0]], 1)

            dve.wait_ge(q["bias_ready"], 8)
            for m in range(4):
                chain(ts(bf[:, m, :], mix[:, m, :], pr("k_k")[:, m:m + 1], None, ALU.mult), hold=(m == 3))
            chain(tt(t3[:, :, :], bf, bf, ALU.mult), "kk_sq_ready")

            dve.wait_ge(q["decay_tanh"], 2)
            chain(ts(t1[:, :, :], t1[:, :, :], 1.0, -0.5 * DECAY, ALU.add, ALU.mult))
            dve.wait_ge(q["rate_tanh"], 2)
            for m in range(4):
                for c in range(NCH):
                    cs = slice(c * CH, (c + 1) * CH)
                    chain(dve.tensor_tensor_scan(t2[:, m, cs], cn("ones")[:, 0:CH], t1[:, m, cs], 0.0, ALU.mult, ALU.add),
                          hold=(m == 3 and c == 3))
            for b, name in enumerate(("kc", "vc")):
                dve.wait_ge(q["kshift_ready"], b + 1)
                base = kshift[:, b, :, :]
                src = bass.AP(base.tensor, base.offset, [list(base.ap[0]), [2, 16], [S, NG], [CSTRIDE, NCMP]])
                pos = pr("pos_k" if b == 0 else "pos_v")
                chain(tt(xcmp[:, b, :, :].rearrange("p j (g n) -> p j g n", g=NG), src,
                         like(pos[:, :, None, None], [P, 16, NG, NCMP]), ALU.add), "xcmp_ready")
            for n in range(2):
                b0 = full(dve, f"kk{n}")
                ins = ts(t3[:, 2 * n:2 * n + 2, :], flat(b0), 1e-24, None, ALU.max)
                chain(ins, "kk_max")
                dve.sem_inc(bank_free[plan[f"kk{n}"][0]], 1)
            dve.wait_ge(q["kk_root"], 1)
            chain(dve.reciprocal(t3[:, :, :], t3[:, :, :]))
            chain(tt(bf, bf, t3[:, :, :], ALU.mult))
            dve.sem_inc(q["log_ready"], 1)
            ins = tt(t1[:, :, :], t2[:, :, :], t1[:, :, :], ALU.subtract)
            chain(ins)
            dve.sem_inc(q["log_ready"], 1)
            chain(ts(kf, kf, 0.5, 0.5, ALU.mult, ALU.add))
            dve.wait_ge(q["decay_exp"], 3)
            a_f = ar[:, :, :, 0, :]
            r_f = ar[:, :, :, 1, :]

            def tiles(t):
                return t.rearrange("p m (i t) -> p m i t", i=2)

            chain(stt(a_f.rearrange("p m i t -> p (m i) t"), bf.rearrange("p m (i t) -> p (m i) t", i=2), -1.0,
                      t1[:, :, :].rearrange("p m (i t) -> p (m i) t", i=2), ALU.mult, ALU.mult), hold=False)
            chain(tt(r_f.rearrange("p m i t -> p (m i) t"), mix[:, 4:8, :].rearrange("p m (i t) -> p (m i) t", i=2),
                     t3[:, :, :].rearrange("p m (i t) -> p (m i) t", i=2), ALU.mult))
            chain(dve.tensor_copy(pend, t3[:, :, :].rearrange("p m (c t) -> p m c t", c=NCH)[:, :, :, CH - 1]))
            chain(tt(bf, bf, kf, ALU.mult))
            chain(tt(bf, bf, t2[:, :, :], ALU.mult))
            for m in range(4):
                chain(ts(kf[:, m, :], kf[:, m, :], -1.0, pr("k_a")[:, m:m + 1], ALU.add, ALU.mult), hold=(m == 3))
            chain(stt(kf, kf, 1.0, mix[:, 0:4, :], ALU.add, ALU.mult))
            for m in range(4):
                ins = stt(mix[:, 4 + m, :], mix[:, 4 + m, :], pr("r_k")[:, m:m + 1], kf[:, m, :], ALU.mult, ALU.mult)
                chain(ins, "bonus_ready" if m == 3 else None)
            chain(tt(kf, kf, t2[:, :, :], ALU.mult), "rwkv_ready")
            dve.wait_ge(q["gx_ready"], 2)
            for p in range(2):
                chain(dve.memset(kcb[64 * (1 - p):64 * (1 - p) + 64, p, :], 0.0), "keys_zeroed", hold=False)
            chain(tt(gy, gx, gx, ALU.mult))
            chain(ts(gy, gy, 0.044715, 1.0, ALU.mult, ALU.add))
            chain(tt(gy, gy, gx, ALU.mult), "gelu_in")
            dve.wait_ge(q["gelu_tanh"], 1)
            chain(stt(gy, gy, 1.0, gx, ALU.add, ALU.mult))
            chain(ts(gx, gy, 0.5, None, ALU.mult), "gelu_ready")

            for n in range(2):
                b0 = full(dve, f"bonus{n}")
                chain(tt(mix[:, 4 + 2 * n:6 + 2 * n, :], flat(b0), mix[:, 8 + 2 * n:10 + 2 * n, :], ALU.mult))
                dve.sem_inc(bank_free[plan[f"bonus{n}"][0]], 1)

            def attended(g):
                b0 = full(dve, f"o{g}")
                chain(dve.tensor_copy(yT[:, 8 + 2 * g:10 + 2 * g, :], flat(b0)), "nsa_ready")
                dve.sem_inc(bank_free[plan[f"o{g}"][0]], 1)

            for i in range(NT):
                nc_ = 7 if i == 0 else NCMP
                b0 = full(dve, f"cs{i}")
                cp = cprob[i]
                first = CBLOCK - 1 + (P if i == 0 else 0)
                chain(tt(cp, b0[:, 0:NH * nc_].rearrange("p (h n) -> p h n", h=NH),
                         bias[:, :, first:first + CSTRIDE * (nc_ - 1) + 1:CSTRIDE], ALU.add))
                dve.sem_inc(bank_free[plan[f"cs{i}"][0]], 1)
                mx = astat[:, 32:48]
                chain(dve.tensor_reduce(mx, cp, AXX, ALU.min))
                chain(ts(mx, mx, 1.0e20, None, ALU.min))
                chain(tt(cp, cp, like(mx[:, :, None], [P, NH, nc_]), ALU.subtract), "cexp_in")
            for i in range(NT):
                nc_ = 7 if i == 0 else NCMP
                cp = cprob[i]
                dve.wait_ge(q["cexp_ready"], i + 1)
                sm = astat[:, 32:48]
                chain(dve.tensor_reduce(sm, cp, AXX, ALU.add))
                chain(ts(sm, sm, 1e-30, None, ALU.max))
                chain(dve.reciprocal(sm, sm))
                chain(tt(sm, sm, gate_t[:, i, 0::3], ALU.mult))
                chain(tt(cp, cp, like(sm[:, :, None], [P, NH, nc_]), ALU.mult), "cprob_ready")

            def logits(g, u):
                n = 6 * g + u
                p = u % 2
                b0 = full(dve, f"s{g}{u}")
                if n >= 2:
                    b, cnt_ = plan[f"pT{(n - 2) // 6}{(n - 2) % 6}"]
                    dve.wait_ge(bank_full[b], cnt_ + 1)
                nb, w = (4, P) if u < 2 else (2, S)
                for b in range(nb):
                    bs = slice(b * w, (b + 1) * w)
                    ins = dve.tensor_tensor_reduce(prob[:, n % 2, bs], b0[:, bs],
                                                   bias[:, 4 * g + p + 2 * (b * w // S), 2 * P - w:2 * P], 1.0, FAR,
                                                   ALU.add, ALU.min, astat[:, 8 * (n % 2) + b:8 * (n % 2) + b + 1])
                chain(ins, "exp_in")
                dve.sem_inc(bank_free[plan[f"s{g}{u}"][0]], 1)

            def gated(g, u):
                n = 6 * g + u
                p = u % 2
                dve.wait_ge(q["exp_ready"], n + 1)
                nb, w = (4, P) if u < 2 else (2, S)
                sm = astat[:, 16 + 8 * (n % 2):16 + 8 * (n % 2) + nb]
                chain(dve.reciprocal(sm, sm))
                c0 = 12 * g + 3 * p + 1
                if u < 2:
                    gates = gate_t[:, 0, 12 * g:12 * g + 12].rearrange("p (h x) -> p h x", h=2)[:, :, 3 * p + 1:3 * p + 3]
                    sm2 = sm.rearrange("p (h b) -> p h b", h=2)
                    chain(tt(sm2, sm2, gates, ALU.mult))
                else:
                    br = (u - 2) // 2
                    chain(tt(sm, sm, gate_t[:, 1, c0 + br:c0 + br + 7:6], ALU.mult))
                pv = prob[:, n % 2, :].rearrange("p (b k) -> p b k", b=nb)
                chain(tt(pv, pv, like(sm[:, :, None], [P, nb, w]), ALU.mult), "prob_ready", hold=False)

            def rwkv(step):
                kind, i, which = step
                if kind == "products":
                    for h in range(4 * which, 4 * which + 4):
                        b0 = full(dve, f"A{i}{h}")
                        chain(tt(amat[:, h, :, :].rearrange("p j t -> p (j t)"), b0[:, :], cn("intra"), ALU.mult),
                              "amat_ready")
                        dve.sem_inc(bank_free[plan[f"A{i}{h}"][0]], 1)
                elif kind == "seed":
                    grp = which[0]
                    dve.wait_ge(q["lmask_ready"], 6 * (2 * i + grp) + 1)
                    chain(tt(zinv[grp], lmask, like(ident[:, None, :], [P, 4, P]), ALU.add), "z_ready")
                    b0 = full(dve, f"XZ{i}{grp}")
                    chain(dve.tensor_copy(xinv, b0[:, :].rearrange("p (h t) -> p h t", h=4)), "x_ready")
                    dve.sem_inc(bank_free[plan[f"XZ{i}{grp}"][0]], 1)
                elif kind == "level":
                    grp, n = which
                    z = zinv[grp]
                    if n < 4:
                        b0 = full(dve, f"X{i}{grp}{n}")
                        chain(tt(xinv, xinv, b0[:, :].rearrange("p (h t) -> p h t", h=4), ALU.add), "x_ready", hold=False)
                    b0 = full(dve, f"Z{i}{grp}{n}")
                    chain(tt(z, z, b0[:, :].rearrange("p (h t) -> p h t", h=4), ALU.add), "z_ready")
                    if n < 4:
                        dve.wait_ge(q["x_ready"], chain.count["x_ready"])
                        dve.sem_inc(bank_free[plan[f"X{i}{grp}{n}"][0]], 1)
                    dve.sem_inc(bank_free[plan[f"Z{i}{grp}{n}"][0]], 1)
                elif kind == "local":
                    for n in range(2):
                        b0 = full(dve, f"rx{i}{n}")
                        rv = ar[:, 2 * n:2 * n + 2, i, 1, :]
                        chain(tt(rv, rv, b0[:, 0:2 * P].rearrange("p (m t) -> p m t", m=2), ALU.add), "rx_ready")
                        dve.sem_inc(bank_free[plan[f"rx{i}{n}"][0]], 1)
                    for c in range(2):
                        b0 = full(dve, f"fc{i}{c}")
                        bv = b0[:, :].rearrange("p (m j v) -> p m j v", m=4, j=2)
                        chain(tt(fc[:, c, :, 0, :], bv[:, :, 0, :], like(cn("eye64")[:, None, :], [P, 4, DH]), ALU.add),
                              hold=False)
                        chain(dve.tensor_copy(fc[:, c, :, 1, :], bv[:, :, 1, :]), "fc_ready")
                        dve.sem_inc(bank_free[plan[f"fc{i}{c}"][0]], 1)
                elif kind == "scan":
                    n = 2 * i + which
                    if n < NCH - 1:
                        b0 = full(dve, f"st{i}{which}")
                        sv = state[:, (n + 1) % 2, :, :]
                        du = fc[:, which, :, 1, :]
                        chain(tt(du, b0[:, 0:4 * DH].rearrange("p (m v) -> p m v", m=4), du, ALU.add))
                        dve.sem_inc(bank_free[plan[f"st{i}{which}"][0]], 1)
                        chain(tt(sv, du, like(pend[:, :, n:n + 1], [P, 4, DH]), ALU.mult), "state_ready")
                    if which == 1:
                        group_norm(i)
                elif kind == "finish":
                    dve.wait_ge(q["gn_ready"], i + 1)
                    yr = yT[:, 4:8, i * P:(i + 1) * P]
                    chain(tt(yr, yr, bonus[:, :, i * P:(i + 1) * P], ALU.add))
                    b0 = full(dve, f"gup{i}")
                    chain(tt(yr, yr, b0[:, :].rearrange("p (m t) -> p m t", m=4), ALU.mult), "yrw_ready")
                    dve.sem_inc(bank_free[plan[f"gup{i}"][0]], 1)

            def group_norm(i):
                yv = ynorm.rearrange("p (m j v) -> p m j v", m=4, j=2)
                for p in range(2):
                    b0 = full(dve, f"y{i}{p}")
                    chain(dve.tensor_copy(yv[:, :, p, :], b0[:, 0:4 * DH].rearrange("p (m v) -> p m v", m=4)))
                    dve.sem_inc(bank_free[plan[f"y{i}{p}"][0]], 1)
                yh = ynorm.rearrange("p (h v) -> p h v", h=RH)
                ys = ysq.rearrange("p (h v) -> p h v", h=RH)
                mean = stat[:, 16:24]
                chain(dve.tensor_reduce(mean, yh, AXX, ALU.add))
                chain(ts(mean, mean, 1.0 / DH, None, ALU.mult))
                chain(tt(yh, yh, like(mean[:, :, None], [P, RH, DH]), ALU.subtract))
                chain(tt(ys, yh, yh, ALU.mult))
                chain(dve.tensor_reduce(mean, ys, AXX, ALU.add))
                roots[0] += 1
                chain(ts(stat[:, 0:8], mean, 1.0 / DH, 64e-5, ALU.mult, ALU.add), "rms_in")
                dve.wait_ge(q["root_ready"], roots[0])
                chain(tt(yh, yh, like(stat[:, 8:16][:, :, None], [P, RH, DH]), ALU.mult), "ynorm_ready")

            for s in range(BEFORE):
                if s == 3:
                    logits(0, 0)
                    logits(0, 1)
                    gated(0, 0)
                rwkv(RWKV_STEPS[s])
            steps = iter(RWKV_STEPS[BEFORE:DURING])
            for n, (g, u) in enumerate(UNITS):
                if u == 0:
                    if g:
                        attended(g - 1)
                    rwkv(next(steps))
                rwkv(next(steps))
                if n + 1 < len(UNITS):
                    gated(*UNITS[n + 1])
                if n + 2 < len(UNITS):
                    logits(*UNITS[n + 2])
            attended(NG - 1)
            for j in sorted(beside):
                rwkv(beside[j])

            for n in range(4):
                dve.wait_ge(q["gsig_ready"], 3 * n + 3)
                for at, b in enumerate(BRANCHES):
                    b0 = full(dve, f"mb{n}{b}")
                    o = macc if at == 0 else mtmp
                    chain(stt(o, gsig[3 * n + b], 1.0, flat(b0), ALU.add, ALU.mult), "gated")
                    dve.sem_inc(bank_free[plan[f"mb{n}{b}"][0]], 1)
                    if at == 1:
                        chain(tt(macc, macc, mtmp, ALU.add))
                    if at == 2:
                        chain(tt(merged[:, 2 * n:2 * n + 2, :], macc, mtmp, ALU.add), "merged_ready")
            dve.wait_ge(q["x_again"], 16)
            def sum_turned(n):
                b0 = full(dve, f"hT2{n}")
                chain(tt(hT[:, 2 * n:2 * n + 2, :], flat(b0), like(pr("g_ffn")[:, 2 * n:2 * n + 2, None], [P, 2, S]),
                         ALU.mult), "hT_ready")
                dve.sem_inc(bank_free[plan[f"hT2{n}"][0]], 1)

            for n in range(4):
                b0 = full(dve, f"out{n}")
                o = tok[:, :, n * 256:(n + 1) * 256]
                chain(stt(o, flat(b0), 0.5, o, ALU.mult, ALU.add), "sum_ready")
                dve.sem_inc(bank_free[plan[f"out{n}"][0]], 1)
                if n == 3:
                    sum_turned(2)
                    sum_turned(3)
                for i in range(NT):
                    squares(o[:, i, :], stat[:, 24 + 4 * i + n:25 + 4 * i + n], at=256 * i, hold=(i == 1))
                if n in (1, 2):
                    sum_turned(n - 1)
            row_roots(tok, summed=True)

            lg = rt("lg")
            for i in range(NT):
                dve.wait_ge(q["root_ready"], roots[0] - NT + 1 + i)
            chain(ts(stat[:, 34:36], stat[:, 8:10], 0.5, None, ALU.mult))
            b0 = full(dve, "router")
            for i in range(NT):
                chain(stt(lg[:, i, :], b0[:, 36 * i:36 * (i + 1)], stat[:, 8 + i:9 + i], pr("b_router"),
                          ALU.mult, ALU.add), hold=(i == 1))
            dve.sem_inc(bank_free[plan["router"][0]], 1)
            fall = cn("falling")

            def first_best(values, width, best, hot, tmp):
                shape = [P, 2, width]
                f = like(fall[:, None, 0:width], shape)
                chain(dve.tensor_reduce(best, values, AXX, ALU.max))
                chain(tt(hot, values, like(best[:, :, None], shape), ALU.is_equal))
                chain(tt(hot, hot, f, ALU.mult))
                chain(dve.tensor_reduce(tmp, hot, AXX, ALU.max))
                chain(tt(hot, f, like(tmp[:, :, None], shape), ALU.is_equal))

            gl, el = lg[:, :, 0:NGRP], lg[:, :, NGRP:NGRP + E]
            first_best(gl, NGRP, rt("gm"), rt("gh"), rt("tmp"))
            chain(tt(rt("ge"), gl, like(rt("gm")[:, :, None], [P, 2, NGRP]), ALU.subtract), "router_in")
            chain(ts(rt("gh"), rt("gh"), 1.0, 1.0e30, ALU.subtract, ALU.mult))
            el4 = el.rearrange("p i (g e) -> p i g e", g=NGRP)
            chain(tt(el4, el4, like(rt("gh")[:, :, :, None], [P, 2, NGRP, EPG]), ALU.add))
            first_best(el, E, rt("m1"), rt("h1"), rt("tmp"))
            chain(stt(el, rt("h1"), -2.0e30, el, ALU.mult, ALU.add))
            first_best(el, E, rt("m2"), rt("h2"), rt("tmp"))
            chain(tt(rt("w2"), rt("m2"), rt("m1"), ALU.subtract), "router_in")
            dve.wait_ge(q["router_exp"], 2)
            chain(dve.tensor_reduce(rt("tmp"), rt("ge"), AXX, ALU.add))
            chain(ts(rt("w1"), rt("w2"), 1.0, None, ALU.add))
            chain(tt(rt("w1"), rt("w1"), rt("tmp"), ALU.mult))
            chain(dve.reciprocal(rt("w1"), rt("w1")))
            chain(tt(member, rt("h1"), rt("h2"), ALU.add), "member_ready")
            chain(ts(rt("w1"), rt("w1"), 0.5, None, ALU.mult))
            chain(tt(rt("w2"), rt("w2"), rt("w1"), ALU.mult))
            chain(tt(rt("h1"), rt("h1"), like(rt("w1")[:, :, None], [P, 2, E]), ALU.mult))
            chain(tt(rt("h2"), rt("h2"), like(rt("w2")[:, :, None], [P, 2, E]), ALU.mult))
            chain(dve.memset(small[:, 112:112 + 2 * (E + GANG)], 0.0))
            chain(tt(combine[:, :, 0:E], rt("h1"), rt("h2"), ALU.add), "combine_ready")
            b0 = full(dve, "places")
            chain(dve.memset(place[:, :, :], 99.0))
            at = place[:, :, 0:E]
            chain(stt(at, b0[:, 0:2 * E].rearrange("p (i e) -> p i e", i=2), 99.0 - CAP, member, ALU.add, ALU.mult))
            chain(ts(at, at, -1.0, 99.0, ALU.mult, ALU.add))
            chain(dve.tensor_reduce(crowd[:, :], b0[:, 2 * E:3 * E], AXX, ALU.max), "crowd_ready")
            dve.sem_inc(bank_free[plan["places"][0]], 1)
            most = dve.value_load(crowd[0:1, 0:1], min_val=0, max_val=S)

            def seat(gang):
                slots = like(cn("falling")[:, None, 0:CAP], [P, GANG, CAP])
                for i in range(NT):
                    o = sel[:, i, :].rearrange("p (e s) -> p e s", e=GANG)
                    tt(o, slots, like(place[:, i, bass.ds(gang * GANG, GANG)][:, :, None], [P, GANG, CAP]),
                       ALU.is_equal).then_inc(q["moe_ready"], 1)

            def weigh_seats(gang):
                for i in range(NT):
                    o = sel[:, i, :].rearrange("p (e s) -> p e s", e=GANG)
                    w = wsel[:, i, :].rearrange("p (e s) -> p e s", e=GANG)
                    ins = tt(w, o, like(combine[:, i, bass.ds(gang * GANG, GANG)][:, :, None], [P, GANG, CAP]), ALU.mult)
                    if i == 1:
                        ins.then_inc(q["sel_ready"], 1)

            def gathered_experts():
                seat(0)
                dve.wait_ge(q["moe_ready"], 2)
                weigh_seats(0)
                with dve.Fori(0, NGANG) as gang:
                    for b in range(2):
                        dve.wait_ge(q["gathered"], gang * 2 + b + 1)
                        tt(gath[:, 4 * b:4 * b + 4, :], bank[b][:, :].rearrange("p (k s) -> p k s", k=4),
                           like(pr("g_ffn")[:, 4 * b:4 * b + 4, None], [P, 4, P]), ALU.mult).then_inc(q["gath_ready"], 1)
                    dve.wait_ge(q["gtanh_ready"], gang + 1)
                    stt(ghid, gtanh, 1.0, bank[2][:, 0:DE], ALU.add, ALU.mult).then_inc(q["moe_ready"], 1)
                    dve.wait_ge(q["moe_ready"], gang * 3 + 3)
                    tt(ghid, ghid, bank[2][:, DE:2 * DE], ALU.mult).then_inc(q["ghid_ready"], 1)
                    dve.wait_ge(q["wsel_turned"], gang + 1)
                    seat(gang + 1)
                    dve.wait_ge(q["moe_ready"], gang * 3 + 5)
                    weigh_seats(gang + 1)
                    for j in range(4):
                        n, i = j // 2, j % 2
                        dve.wait_ge(q["scattered"], gang * 4 + j + 1)
                        o = tok[:, i, n * 512:(n + 1) * 512]
                        tt(o, o, bank[6 + i][:, :], ALU.add).then_inc(q["summed"], 1)

            def dense_experts():
                loop_chain = q["moe_ready"]
                for i in range(NT):
                    ts(combine[:, i, :], combine[:, i, :], stat[:, 8 + i:9 + i], stat[:, 8 + i:9 + i], ALU.mult, ALU.mult)\
                        .then_inc(loop_chain, 1)
                dve.wait_ge(loop_chain, NT)
                with dve.Fori(0, NGANG) as gang:
                    step = 0
                    for i in range(NT):
                        for e in range(GANG):
                            dve.wait_ge(q["silu_tanh"], gang * 8 + (4 * i + e + 1))
                            h_ = hid[:, e, :]
                            for k in range(2):
                                if k == 0:
                                    ins = stt(h_, gsi[:, e, :], 1.0, bank[e][:, 0:DE], ALU.add, ALU.mult)
                                else:
                                    ins = tt(h_, h_, bank[e][:, DE:2 * DE], ALU.mult)
                                ins.then_inc(loop_chain, 1)
                                step += 1
                                dve.wait_ge(loop_chain, gang * 20 + (NT + step))
                            dve.sem_inc(bank_free[e], 1)
                            ts(h_, h_, combine[:, i, bass.ds(gang * GANG + e, 1)], None, ALU.mult).then_inc(q["hid_ready"], 1)
                        for half in range(2):
                            dve.wait_ge(q["hidT2_ready"], gang * 4 + (2 * i + half + 1))
                            dve.sem_inc(bank_free[4 + half], 1)
                        for n in range(2):
                            dve.wait_ge(bank_full[6 + n], gang * 2 + (before_loop[6 + n] + i + 1))
                            o = tok[:, i, n * 512:(n + 1) * 512]
                            tt(o, o, bank[6 + n][:, :], ALU.add).then_inc(loop_chain, 1)
                            step += 1
                            dve.wait_ge(loop_chain, gang * 20 + (NT + step))
                            dve.sem_inc(bank_free[6 + n], 1)
                    assert step == 20

            with dve.If(most <= CAP):
                gathered_experts()
            with dve.Else():
                dense_experts()
            chain(dve.memset(stat[:, 24:25], 0.0))

            dve.wait_ge(q["gfin_loaded"], 16)
            row_roots(tok)
            res = hT[:, :, :].rearrange("p c t -> p (c t)").rearrange("p (i d) -> p i d", i=2)
            for i in range(NT):
                dve.wait_ge(q["root_ready"], roots[0] - NT + 1 + i)
                chain(stt(res[:, i, :], tok[:, i, :], stat[:, 8 + i:9 + i], gfin, ALU.mult, ALU.mult), "final_ready")


def kernel(**inputs):
    import concourse.bacc as _bacc
    from concourse.bass_utils import run_bass_kernel_spmd as _run

    a = {k: np.asarray(v) for k, v in inputs.items()}

    def channels(v):
        return v.reshape(-1, P).T

    par = np.zeros((P, NPARAMS), np.float32)

    def put(name, v):
        lo, hi = PARAMS[name]
        par[:v.shape[0], lo:hi] = v

    rk, kk, vv = (slice(n * RW, (n + 1) * RW) for n in range(3))
    lo_ = 3 * RW
    mu = a["rw_mu"][0]
    put("g_mix", channels(a["norm_mix"][0]))
    put("g_ffn", channels(a["norm_ffn"][0]))
    put("mu", np.concatenate([channels(mu[kk]), channels(mu[rk]), channels(mu[vv]),
                              np.pad(mu[lo_:lo_ + 64], (0, 64))[:, None], np.pad(mu[lo_ + 64:], (0, 32))[:, None]], 1))
    for name, key in (("w0", "rw_w0"), ("a0", "rw_a0"), ("k_k", "rw_k_k"), ("k_a", "rw_k_a"), ("r_k", "rw_r_k"),
                      ("gn_w", "rw_gn_w"), ("gn_b", "rw_gn_b"), ("pool_scale", "pool_scale"), ("b_merge", "b_merge")):
        put(name, channels(a[key][0].reshape(-1)))
    put("lora_up", np.concatenate([a["rw_w_up"][0], a["rw_a_up"][0]]))
    put("g_up", a["rw_g_up"][0])
    put("pool_w", a["pool_w"][0].transpose(1, 0, 2).reshape(P, -1))
    for b in "kv":
        put(f"w2_{b}", a[f"cmp_w2_{b}"][0].reshape(2, P, DH).transpose(1, 0, 2).reshape(P, -1))
        put(f"pos_{b}", a[f"cmp_pos_{b}"][0].reshape(16, P).T)
    put("rel", np.concatenate([a["rel_bias"], np.ones((1, NH), np.float32)]))
    put("b_router", np.broadcast_to(np.concatenate([a["b_router_grp"][0], a["b_router_exp"][0]]), (P, NGRP + E)))

    front = np.zeros((NFRONT, P, SLOT), np.float32)

    def chunk(n, w):
        c = w.shape[1]
        front[n].reshape(P, KD, -1)[:, :, :c] = w.reshape(KD, P, c).transpose(1, 0, 2)

    w_in = a["w_in"][0]
    r0 = PW
    n0 = PW + 3 * RW + 160
    chunk(C_LORA, np.concatenate([w_in[:, r0 + 3 * RW:r0 + 3 * RW + 64], w_in[:, n0 + 1024 + 6 * 256:],
                                   w_in[:, r0 + 3 * RW + 64:r0 + 3 * RW + 160]], 1))
    for c0, at, n in ((C_K, r0 + RW, 2), (C_R, r0, 2), (C_V, r0 + 2 * RW, 2), (C_KC, n0 + 1024, 1), (C_VC, n0 + 1280, 1),
                      (C_Q[0], n0, 2), (C_Q[2], n0 + 512, 2), (C_KS, n0 + 1536, 1), (C_KW, n0 + 2048, 1), (C_VS, n0 + 1792, 1),
                      (C_VW, n0 + 2304, 1), (C_POOL, 0, 2)):
        for j in range(n):
            chunk(c0 + j, w_in[:, at + 256 * j:at + 256 * (j + 1)])
    for c0, key in ((C_W1K, "cmp_w1_k"), (C_W1V, "cmp_w1_v")):
        for j in range(2):
            chunk(c0 + j, a[key][0][1024 * j:1024 * (j + 1)])
    for n in range(4):
        cs = slice(256 * n, 256 * (n + 1))
        for b in range(3):
            chunk(C_GATE + 3 * n + b, a["w_merge"][0][:, D * b:D * (b + 1)][:, cs])
        for j in range(2):
            chunk(C_BRANCH + 2 * n + 1 - j, a["w_branch"][0][1024 * j:1024 * (j + 1), cs])
        chunk(C_OUT + n, a["w_out"][0][:, cs])
    wr = np.concatenate([a["w_router_grp"][0], a["w_router_exp"][0]], 1)
    front[C_ROUTER][:, 0:KD * 36] = wr.reshape(KD, P, 36).transpose(1, 0, 2).reshape(P, -1)

    ex = np.empty((NGANG, GCH, P, SLOT), np.float32)
    gu = ex[:, 0:8].reshape(NGANG, 8, P, GANG, 2, DE)
    for j, key in enumerate(("w_exp_gate", "w_exp_up")):
        gu[:, :, :, :, j] = a[key][0].reshape(NGANG, GANG, KD, P, DE).transpose(0, 2, 3, 1, 4)
    ex[:, 8:12] = a["w_exp_down"][0].reshape(NGANG, GANG, 2, P, D).transpose(0, 1, 3, 2, 4).reshape(NGANG, GANG, P, -1)

    arrays = {
        "x": a["x"][0], "params": par, "consts": constants(), "front": front, "experts": ex,
        "g_final": np.ascontiguousarray(np.broadcast_to(a["norm_final"], (P, D))),
    }
    nc = _bacc.Bacc("TRN2", target_bir_lowering=False, num_devices=1)
    args = [nc.dram_tensor(n, v.shape, F32, kind="ExternalInput").ap() for n, v in arrays.items()]
    out = nc.dram_tensor("out", (S, D), F32, kind="ExternalOutput").ap()
    rows = nc.dram_tensor("bias_rows", (NH, 384), F32, kind="Internal").ap()
    build_layer(nc, *args, out, rows)
    r = _run(nc, [arrays], core_ids=[0])
    return r.results[0]["out"].reshape(1, S, D)
```
